# Optimizing a Trainium2 kernel written in Bass

```python
import math
import jax, jax.numpy as jnp
from jax import lax
import numpy as np

D_MODEL = 1024
BATCH = 1
SEQ = 256
DEPTH = 2

N_EVEN = (DEPTH + 1) // 2
N_ODD = DEPTH // 2
DN_ALPHA = (2.0 * DEPTH) ** 0.25
DN_BETA = (8.0 * DEPTH) ** -0.25
LN_EPS = 1e-5
NEG = -1e30
Q_BLOCK = 128

GM_WIDTH = D_MODEL // 2
GM_GROUPS = 4
GM_GROUP_DIM = GM_WIDTH // GM_GROUPS
GM_CHUNK = 128

MLA_HEADS = 8
MLA_NOPE = 64
MLA_ROPE = 32
MLA_V = 64
MLA_Q_RANK = D_MODEL // 4
MLA_KV_RANK = D_MODEL // 8
ROPE_BASE = 10000.0
AB_IN = 2 * GM_WIDTH + MLA_Q_RANK + MLA_KV_RANK + MLA_ROPE
AB_MIX = GM_WIDTH + MLA_HEADS * MLA_V
AB_SPLITS = (GM_WIDTH, 2 * GM_WIDTH, 2 * GM_WIDTH + MLA_Q_RANK,
             2 * GM_WIDTH + MLA_Q_RANK + MLA_KV_RANK)

NSA_HEADS = 16
NSA_GROUPS = 2
NSA_HPG = NSA_HEADS // NSA_GROUPS
NSA_DH = 64
NSA_CMP_LEN = 32
NSA_CMP_STRIDE = 16
NSA_CMP_HIDDEN = 256
NSA_SEL_LEN = 64
NSA_TOPK = 8
NSA_SEL_QBLOCK = 64
NSA_WINDOW = 512
NSA_BRANCHES = 3
NSA_KV = NSA_GROUPS * NSA_DH
C_MIX = NSA_HEADS * NSA_DH
C_IN = C_MIX + 6 * NSA_KV + NSA_BRANCHES * NSA_HEADS
NSA_SPLITS = tuple(C_MIX + i * NSA_KV for i in range(7))
NSA_FORCE = 1e4

MOE_GROUPS = 4
MOE_EPG = 8
MOE_EXPERTS = MOE_GROUPS * MOE_EPG
MOE_TOPK = 2
MOE_HIDDEN = D_MODEL // 4


def layer_norm(x, g, b):
    xf = x.astype(jnp.float32)
    mu = xf.mean(-1, keepdims=True)
    var = jnp.square(xf - mu).mean(-1, keepdims=True)
    return ((xf - mu) * lax.rsqrt(var + LN_EPS) * g + b).astype(x.dtype)

def rms_norm(x, g):
    xf = x.astype(jnp.float32)
    return (xf * lax.rsqrt(jnp.mean(xf * xf, -1, keepdims=True) + LN_EPS) * g).astype(x.dtype)

def rope(x, pos):
    half = x.shape[-1] // 2
    freq = jnp.exp(-math.log(ROPE_BASE) * jnp.arange(half, dtype=jnp.float32) / half)
    ang = pos.astype(jnp.float32)[:, :, None, None] * freq
    cos, sin = jnp.cos(ang), jnp.sin(ang)
    x1 = x[..., :half].astype(jnp.float32)
    x2 = x[..., half:].astype(jnp.float32)
    return jnp.concatenate([x1 * cos - x2 * sin, x1 * sin + x2 * cos], -1).astype(x.dtype)

def gmlp_mix(u, v, ln_g, ln_b, w_s, b_s):
    B, S, _ = u.shape
    nc = S // GM_CHUNK
    vn = layer_norm(v, ln_g, ln_b).reshape(B, nc, GM_CHUNK, GM_GROUPS, GM_GROUP_DIM)
    causal = jnp.tril(jnp.ones((GM_CHUNK, GM_CHUNK), dtype=bool))
    ws = jnp.where(causal, w_s, 0.0).astype(vn.dtype)
    s = jnp.einsum('gts,bnsgc->bntgc', ws, vn) + jnp.transpose(b_s)[:, :, None]
    return u * s.reshape(B, S, GM_WIDTH)

def mla_mix(c_q, c_kv, k_r, pos, q_norm_g, kv_norm_g, w_uq, w_uk, w_uv):
    B, S, _ = c_q.shape
    q = (rms_norm(c_q, q_norm_g) @ w_uq).reshape(B, S, MLA_HEADS, MLA_NOPE + MLA_ROPE)
    q_nope = q[..., :MLA_NOPE]
    q_rope = rope(q[..., MLA_NOPE:], pos)
    ckv = rms_norm(c_kv, kv_norm_g)
    k_nope = (ckv @ w_uk).reshape(B, S, MLA_HEADS, MLA_NOPE)
    v = (ckv @ w_uv).reshape(B, S, MLA_HEADS, MLA_V)
    k_rope = rope(k_r[:, :, None, :], pos)[:, :, 0]
    scale = (MLA_NOPE + MLA_ROPE) ** -0.5
    outs = []
    for i in range(S // Q_BLOCK):
        q0, q1 = i * Q_BLOCK, (i + 1) * Q_BLOCK
        s = (jnp.einsum('bqhd,bkhd->bhqk', q_nope[:, q0:q1], k_nope[:, :q1])
             + jnp.einsum('bqhr,bkr->bhqk', q_rope[:, q0:q1], k_rope[:, :q1]))
        mask = (q0 + jnp.arange(Q_BLOCK))[:, None] >= jnp.arange(q1)[None, :]
        s = jnp.where(mask, s.astype(jnp.float32) * scale, NEG)
        p = jax.nn.softmax(s, axis=-1).astype(v.dtype)
        outs.append(jnp.einsum('bhqk,bkhd->bqhd', p, v[:, :q1]))
    return jnp.concatenate(outs, axis=1).reshape(B, S, MLA_HEADS * MLA_V)

def ab_mixer(x, pos, w_in, gm_ln_g, gm_ln_b, gm_ws, gm_bs, q_norm_g, kv_norm_g,
             w_uq, w_uk, w_uv, w_o):
    h = x @ w_in
    u, v, c_q, c_kv, k_r = jnp.split(h, AB_SPLITS, axis=-1)
    y_a = gmlp_mix(jax.nn.gelu(u), jax.nn.gelu(v), gm_ln_g, gm_ln_b, gm_ws, gm_bs)
    y_b = mla_mix(c_q, c_kv, k_r, pos, q_norm_g, kv_norm_g, w_uq, w_uk, w_uv)
    return jnp.concatenate([y_a, y_b], axis=-1) @ w_o

def compress_kv(k, pos_emb, w1, w2):
    B, S, G, D = k.shape
    r = NSA_CMP_LEN // NSA_CMP_STRIDE
    sub = k.reshape(B, S // NSA_CMP_STRIDE, NSA_CMP_STRIDE, G, D)
    nc = S // NSA_CMP_STRIDE - r + 1
    blocks = jnp.concatenate([sub[:, j:j + nc] for j in range(r)], axis=2) + pos_emb[:, None, :]
    flat = blocks.transpose(0, 1, 3, 2, 4).reshape(B, nc, G, NSA_CMP_LEN * D)
    return jax.nn.gelu(flat @ w1) @ w2

def nsa_compressed(q, k_cmp, v_cmp):
    S, nc = q.shape[1], k_cmp.shape[1]
    s = jnp.einsum('btgid,bngd->bgitn', q, k_cmp).astype(jnp.float32) * NSA_DH ** -0.5
    end = jnp.arange(nc) * NSA_CMP_STRIDE + NSA_CMP_LEN - 1
    mask = jnp.arange(S)[:, None] >= end[None, :]
    p = jnp.where(mask, jax.nn.softmax(jnp.where(mask, s, NEG), axis=-1), 0.0)
    o = jnp.einsum('bgitn,bngd->btgid', p.astype(v_cmp.dtype), v_cmp)
    return o, p

def nsa_select_blocks(p_cmp):
    S, nc = p_cmp.shape[3], p_cmp.shape[4]
    nsel = S // NSA_SEL_LEN
    c0 = jnp.arange(nc) * NSA_CMP_STRIDE
    s0 = jnp.arange(nsel) * NSA_SEL_LEN
    cover = ((c0[:, None] < s0[None, :] + NSA_SEL_LEN)
             & (c0[:, None] + NSA_CMP_LEN > s0[None, :])).astype(jnp.float32)
    imp = jnp.einsum('bgitn,nj->bgtj', p_cmp, cover)
    jj = jnp.arange(nsel)[None, :]
    tb = (jnp.arange(S) // NSA_SEL_LEN)[:, None]
    forced = (jj == 0) | (jj == tb) | (jj == tb - 1)
    score = jnp.where(forced, NSA_FORCE, jnp.where(jj <= tb, imp, -NSA_FORCE))
    _, idx = lax.top_k(score, min(NSA_TOPK, nsel))
    return idx

def nsa_selected(q, k_s, v_s, sel_idx):
    B, S, G, HPG, D = q.shape
    K = sel_idx.shape[-1]
    nsel = S // NSA_SEL_LEN
    kb = k_s.reshape(B, nsel, NSA_SEL_LEN, G, D).transpose(0, 3, 1, 2, 4)
    vb = v_s.reshape(B, nsel, NSA_SEL_LEN, G, D).transpose(0, 3, 1, 2, 4)
    nqb = S // NSA_SEL_QBLOCK
    q_b = q.reshape(B, nqb, NSA_SEL_QBLOCK, G, HPG, D).transpose(1, 0, 2, 3, 4, 5)
    idx_b = sel_idx.reshape(B, G, nqb, NSA_SEL_QBLOCK, K).transpose(2, 0, 1, 3, 4)
    bi = jnp.arange(B)[:, None, None, None]
    gi = jnp.arange(G)[None, :, None, None]

    def one_block(args):
        i, qi, idx = args
        tq = i * NSA_SEL_QBLOCK + jnp.arange(NSA_SEL_QBLOCK)
        kg = kb[bi, gi, idx]
        vg = vb[bi, gi, idx]
        kpos = idx[..., None] * NSA_SEL_LEN + jnp.arange(NSA_SEL_LEN)
        mask = kpos <= tq[None, None, :, None, None]
        s = jnp.einsum('bqgid,bgqkld->bgiqkl', qi, kg).astype(jnp.float32) * NSA_DH ** -0.5
        s = jnp.where(mask[:, :, None], s, NEG)
        p = jax.nn.softmax(s.reshape(B, G, HPG, NSA_SEL_QBLOCK, K * NSA_SEL_LEN), axis=-1)
        p = p.reshape(s.shape).astype(vg.dtype)
        return jnp.einsum('bgiqkl,bgqkld->bqgid', p, vg)

    o = lax.map(one_block, (jnp.arange(nqb), q_b, idx_b))
    return o.transpose(1, 0, 2, 3, 4, 5).reshape(B, S, G, HPG, D)

def nsa_window(q, k_w, v_w):
    B, S, G, HPG, D = q.shape
    nb = S // Q_BLOCK
    span = NSA_WINDOW + Q_BLOCK
    kp = jnp.pad(k_w, ((0, 0), (NSA_WINDOW, 0), (0, 0), (0, 0)))
    vp = jnp.pad(v_w, ((0, 0), (NSA_WINDOW, 0), (0, 0), (0, 0)))
    q_b = q.reshape(B, nb, Q_BLOCK, G, HPG, D).transpose(1, 0, 2, 3, 4, 5)

    def one_block(args):
        i, qi = args
        start = i * Q_BLOCK
        kb = lax.dynamic_slice_in_dim(kp, start, span, axis=1)
        vb = lax.dynamic_slice_in_dim(vp, start, span, axis=1)
        tq = (start + jnp.arange(Q_BLOCK))[:, None]
        kpos = (start - NSA_WINDOW + jnp.arange(span))[None, :]
        mask = (kpos <= tq) & (kpos > tq - NSA_WINDOW) & (kpos >= 0)
        s = jnp.einsum('bqgid,bkgd->bgiqk', qi, kb).astype(jnp.float32) * NSA_DH ** -0.5
        p = jax.nn.softmax(jnp.where(mask, s, NEG), axis=-1).astype(vb.dtype)
        return jnp.einsum('bgiqk,bkgd->bqgid', p, vb)

    o = lax.map(one_block, (jnp.arange(nb), q_b))
    return o.transpose(1, 0, 2, 3, 4, 5).reshape(B, S, G, HPG, D)

def nsa_mixer(x, w_in, cmp_pos, w_ck1, w_ck2, w_cv1, w_cv2, gate_b, w_o):
    B, S, _ = x.shape
    h = x @ w_in
    q, kc, vc, ks, vs, kw, vw, g = jnp.split(h, NSA_SPLITS, axis=-1)
    q = q.reshape(B, S, NSA_GROUPS, NSA_HPG, NSA_DH)

    def kv(t):
        return t.reshape(B, S, NSA_GROUPS, NSA_DH)

    k_cmp = compress_kv(kv(kc), cmp_pos[0], w_ck1, w_ck2)
    v_cmp = compress_kv(kv(vc), cmp_pos[1], w_cv1, w_cv2)
    o_cmp, p_cmp = nsa_compressed(q, k_cmp, v_cmp)
    sel_idx = nsa_select_blocks(p_cmp)
    o_slc = nsa_selected(q, kv(ks), kv(vs), sel_idx)
    o_win = nsa_window(q, kv(kw), kv(vw))
    gates = jax.nn.sigmoid(g + gate_b).reshape(B, S, NSA_BRANCHES, NSA_GROUPS, NSA_HPG, 1)
    o = gates[:, :, 0] * o_cmp + gates[:, :, 1] * o_slc + gates[:, :, 2] * o_win
    return o.reshape(B, S, C_MIX) @ w_o

def hier_moe(x, w_rg, b_rg, w_re, b_re, w_gate, w_up, w_down):
    B, S, D = x.shape
    T = B * S
    xt = x.reshape(T, D)
    g_logits = (xt @ w_rg + b_rg).astype(jnp.float32)
    g_prob = jax.nn.softmax(g_logits, axis=-1)
    g_sel = jnp.argmax(g_logits, axis=-1)
    g_w = jnp.take_along_axis(g_prob, g_sel[:, None], axis=-1)
    e_logits = (xt @ w_re + b_re).astype(jnp.float32).reshape(T, MOE_GROUPS, MOE_EPG)
    e_sel = jnp.take_along_axis(e_logits, g_sel[:, None, None], axis=1)[:, 0]
    top_p, top_i = lax.top_k(jax.nn.softmax(e_sel, axis=-1), MOE_TOPK)
    top_p = top_p / top_p.sum(-1, keepdims=True)
    w_grp = (jax.nn.one_hot(top_i, MOE_EPG, dtype=jnp.float32) * top_p[..., None]).sum(1) * g_w
    y = jnp.zeros_like(xt)
    for gi in range(MOE_GROUPS):
        e0 = gi * MOE_EPG
        wg = jnp.where(g_sel[:, None] == gi, w_grp, 0.0).astype(x.dtype)
        hg = (jax.nn.silu(jnp.einsum('td,edf->tef', xt, w_gate[e0:e0 + MOE_EPG]))
              * jnp.einsum('td,edf->tef', xt, w_up[e0:e0 + MOE_EPG]))
        y = y + jnp.einsum('tef,efd->td', hg * wg[..., None], w_down[e0:e0 + MOE_EPG])
    return y.reshape(B, S, D)

def first_inputs(seed: int = 0) -> dict:
    key = jax.random.key(seed)
    keys = iter(jax.random.split(key, 48))

    def nrm(shape, scale):
        return jax.random.normal(next(keys), shape, jnp.float32) * scale

    def gain(shape):
        return 1.0 + nrm(shape, 0.1)

    x = nrm((BATCH, SEQ, D_MODEL), 1.0)
    offset = jax.random.randint(next(keys), (BATCH, 1), 0, 4096, dtype=jnp.int32)
    positions = (offset + jnp.arange(SEQ, dtype=jnp.int32)[None, :]).astype(jnp.int32)
    return {
        'x': x,
        'positions': positions,
        'ab_w_in': nrm((N_EVEN, D_MODEL, AB_IN), D_MODEL ** -0.5),
        'ab_gm_ln_g': gain((N_EVEN, GM_WIDTH)),
        'ab_gm_ln_b': nrm((N_EVEN, GM_WIDTH), 0.02),
        'ab_gm_ws': nrm((N_EVEN, GM_GROUPS, GM_CHUNK, GM_CHUNK), GM_CHUNK ** -0.5),
        'ab_gm_bs': gain((N_EVEN, GM_GROUPS, GM_CHUNK)),
        'ab_mla_q_norm': gain((N_EVEN, MLA_Q_RANK)),
        'ab_mla_kv_norm': gain((N_EVEN, MLA_KV_RANK)),
        'ab_mla_w_uq': nrm((N_EVEN, MLA_Q_RANK, MLA_HEADS * (MLA_NOPE + MLA_ROPE)), MLA_Q_RANK ** -0.5),
        'ab_mla_w_uk': nrm((N_EVEN, MLA_KV_RANK, MLA_HEADS * MLA_NOPE), MLA_KV_RANK ** -0.5),
        'ab_mla_w_uv': nrm((N_EVEN, MLA_KV_RANK, MLA_HEADS * MLA_V), MLA_KV_RANK ** -0.5),
        'ab_w_o': nrm((N_EVEN, AB_MIX, D_MODEL), AB_MIX ** -0.5 * DN_BETA),
        'c_w_in': nrm((N_ODD, D_MODEL, C_IN), D_MODEL ** -0.5),
        'c_cmp_pos': nrm((N_ODD, 2, NSA_CMP_LEN, NSA_DH), 0.1),
        'c_w_ck1': nrm((N_ODD, NSA_CMP_LEN * NSA_DH, NSA_CMP_HIDDEN), (NSA_CMP_LEN * NSA_DH) ** -0.5),
        'c_w_ck2': nrm((N_ODD, NSA_CMP_HIDDEN, NSA_DH), NSA_CMP_HIDDEN ** -0.5),
        'c_w_cv1': nrm((N_ODD, NSA_CMP_LEN * NSA_DH, NSA_CMP_HIDDEN), (NSA_CMP_LEN * NSA_DH) ** -0.5),
        'c_w_cv2': nrm((N_ODD, NSA_CMP_HIDDEN, NSA_DH), NSA_CMP_HIDDEN ** -0.5),
        'c_gate_b': nrm((N_ODD, NSA_BRANCHES * NSA_HEADS), 0.1),
        'c_w_o': nrm((N_ODD, C_MIX, D_MODEL), C_MIX ** -0.5 * DN_BETA),
        'moe_w_rg': nrm((DEPTH, D_MODEL, MOE_GROUPS), D_MODEL ** -0.5),
        'moe_b_rg': nrm((DEPTH, MOE_GROUPS), 0.01),
        'moe_w_re': nrm((DEPTH, D_MODEL, MOE_EXPERTS), D_MODEL ** -0.5),
        'moe_b_re': nrm((DEPTH, MOE_EXPERTS), 0.01),
        'moe_w_gate': nrm((DEPTH, MOE_EXPERTS, D_MODEL, MOE_HIDDEN), D_MODEL ** -0.5),
        'moe_w_up': nrm((DEPTH, MOE_EXPERTS, D_MODEL, MOE_HIDDEN), D_MODEL ** -0.5),
        'moe_w_down': nrm((DEPTH, MOE_EXPERTS, MOE_HIDDEN, D_MODEL), MOE_HIDDEN ** -0.5 * DN_BETA),
        'ln1_g': gain((DEPTH, D_MODEL)),
        'ln1_b': nrm((DEPTH, D_MODEL), 0.02),
        'ln2_g': gain((DEPTH, D_MODEL)),
        'ln2_b': nrm((DEPTH, D_MODEL), 0.02),
    }

def first_block(x, positions, ab_w_in, ab_gm_ln_g, ab_gm_ln_b, ab_gm_ws, ab_gm_bs,
              ab_mla_q_norm, ab_mla_kv_norm, ab_mla_w_uq, ab_mla_w_uk, ab_mla_w_uv, ab_w_o,
              c_w_in, c_cmp_pos, c_w_ck1, c_w_ck2, c_w_cv1, c_w_cv2, c_gate_b, c_w_o,
              moe_w_rg, moe_b_rg, moe_w_re, moe_b_re, moe_w_gate, moe_w_up, moe_w_down,
              ln1_g, ln1_b, ln2_g, ln2_b):
    for layer in range(DEPTH):
        j = layer // 2
        if layer % 2 == 0:
            mix = ab_mixer(x, positions, ab_w_in[j], ab_gm_ln_g[j], ab_gm_ln_b[j], ab_gm_ws[j],
                           ab_gm_bs[j], ab_mla_q_norm[j], ab_mla_kv_norm[j], ab_mla_w_uq[j],
                           ab_mla_w_uk[j], ab_mla_w_uv[j], ab_w_o[j])
        else:
            mix = nsa_mixer(x, c_w_in[j], c_cmp_pos[j], c_w_ck1[j], c_w_ck2[j], c_w_cv1[j],
                            c_w_cv2[j], c_gate_b[j], c_w_o[j])
        x = layer_norm(DN_ALPHA * x + mix, ln1_g[layer], ln1_b[layer])
        ffn = hier_moe(x, moe_w_rg[layer], moe_b_rg[layer], moe_w_re[layer], moe_b_re[layer],
                       moe_w_gate[layer], moe_w_up[layer], moe_w_down[layer])
        x = layer_norm(DN_ALPHA * x + ffn, ln2_g[layer], ln2_b[layer])
    return x


GRID_W = 64
CTX_LEN = 256
N_MIXERS = 2
N_HEADS = 16
N_KV_HEADS = 4
HEAD_DIM = D_MODEL // N_HEADS
GQA_GROUP = N_HEADS // N_KV_HEADS
Q_DIM = N_HEADS * HEAD_DIM
KV_DIM = N_KV_HEADS * HEAD_DIM
ROPE_AXIS_DIM = HEAD_DIM // 2
ROPE_THETA = 10000.0
ATTN_SCALE = HEAD_DIM ** -0.5
FOURIER_GROUPS = 4
N_GROUPS = 4
EXPERTS_PER_GROUP = 8
N_EXPERTS = N_GROUPS * EXPERTS_PER_GROUP
TOP_K_IN_GROUP = 2
D_EXPERT = D_MODEL // 2
MOE_BLOCK = 128
N_ATTN_LAYERS = (DEPTH + N_MIXERS - 1) // N_MIXERS
N_FOURIER_LAYERS = DEPTH // N_MIXERS
EPS = 1e-6


def _rms_norm(x, gain):
    xf = x.astype(jnp.float32)
    y = xf * lax.rsqrt(jnp.mean(xf * xf, axis=-1, keepdims=True) + EPS)
    return y.astype(x.dtype) * gain

def _ada_params(silu_cond, w_mod, b_mod):
    return jnp.split(silu_cond @ w_mod + b_mod, 6, axis=-1)

def _modulate(x, gain, shift, scale):
    return _rms_norm(x, gain) * (1 + scale) + shift

def _axial_rope_tables(rows, dtype):
    half = ROPE_AXIS_DIM // 2
    inv = ROPE_THETA ** (-jnp.arange(half, dtype=jnp.float32) / half)
    ang_r = jnp.arange(rows, dtype=jnp.float32)[:, None] * inv
    ang_c = jnp.arange(GRID_W, dtype=jnp.float32)[:, None] * inv
    ang_r = jnp.broadcast_to(ang_r[:, None, :], (rows, GRID_W, half)).reshape(-1, half)
    ang_c = jnp.broadcast_to(ang_c[None, :, :], (rows, GRID_W, half)).reshape(-1, half)
    return (jnp.cos(ang_r).astype(dtype), jnp.sin(ang_r).astype(dtype),
            jnp.cos(ang_c).astype(dtype), jnp.sin(ang_c).astype(dtype))

def _rotate_half(x, cos, sin):
    shp = (cos.shape[0],) + (1,) * (x.ndim - 3) + (cos.shape[-1],)
    cos, sin = cos.reshape(shp), sin.reshape(shp)
    x1, x2 = jnp.split(x, 2, axis=-1)
    return jnp.concatenate([x1 * cos - x2 * sin, x2 * cos + x1 * sin], axis=-1)

def _apply_axial_rope(x, tables):
    cos_r, sin_r, cos_c, sin_c = tables
    return jnp.concatenate([_rotate_half(x[..., :ROPE_AXIS_DIM], cos_r, sin_r),
                            _rotate_half(x[..., ROPE_AXIS_DIM:], cos_c, sin_c)], axis=-1)

def _project_qkv(h, w_qkv, q_gain, k_gain, with_q):
    b, l, _ = h.shape
    if with_q:
        qkv = h @ w_qkv
        q = _rms_norm(qkv[..., :Q_DIM].reshape(b, l, N_KV_HEADS, GQA_GROUP, HEAD_DIM), q_gain)
        kv = qkv[..., Q_DIM:]
    else:
        q = None
        kv = h @ w_qkv[:, Q_DIM:]
    k = _rms_norm(kv[..., :KV_DIM].reshape(b, l, N_KV_HEADS, HEAD_DIM), k_gain)
    v = kv[..., KV_DIM:].reshape(b, l, N_KV_HEADS, HEAD_DIM)
    return q, k, v

def _attend(q, k, v):
    s = jnp.einsum('bqkgd,bskd->bkgqs', q, k).astype(jnp.float32) * ATTN_SCALE
    p = jax.nn.softmax(s, axis=-1).astype(v.dtype)
    return jnp.einsum('bkgqs,bskd->bqkgd', p, v)

def _gqa_attention(h_lat, h_ctx, w_qkv, q_gain, k_gain, w_o, rope, need_ctx_out):
    b, n, _ = h_lat.shape
    q_l, k_l, v_l = _project_qkv(h_lat, w_qkv, q_gain, k_gain, True)
    q_c, k_c, v_c = _project_qkv(h_ctx, w_qkv, q_gain, k_gain, need_ctx_out)
    q_l = _apply_axial_rope(q_l, rope)
    k_l = _apply_axial_rope(k_l, rope)
    k_all = jnp.concatenate([k_l, k_c], axis=1)
    v_all = jnp.concatenate([v_l, v_c], axis=1)
    n_blk = n // Q_BLOCK
    q_blocks = jnp.moveaxis(q_l.reshape(b, n_blk, Q_BLOCK, N_KV_HEADS, GQA_GROUP, HEAD_DIM), 1, 0)
    o = lax.map(lambda qb: _attend(qb, k_all, v_all), q_blocks)
    y_lat = jnp.moveaxis(o, 0, 1).reshape(b, n, Q_DIM) @ w_o
    y_ctx = None
    if need_ctx_out:
        y_ctx = _attend(q_c, k_c, v_c).reshape(b, h_ctx.shape[1], Q_DIM) @ w_o
    return y_lat, y_ctx

def _fourier_mix(h, w_o):
    b, n, d = h.shape
    hg = h.astype(jnp.float32).reshape(b, n, FOURIER_GROUPS, d // FOURIER_GROUPS)
    f = jnp.fft.fft2(hg, axes=(1, 3), norm='ortho').real
    return f.reshape(b, n, d).astype(h.dtype) @ w_o

def _hier_moe(h, w_rg, b_rg, w_re, b_re, w1, w3, w2):
    b, n, d = h.shape
    xt = h.reshape(-1, d)
    t = xt.shape[0]
    lg = (xt @ w_rg + b_rg).astype(jnp.float32)
    g_sel = jnp.argmax(lg, axis=-1)
    p_grp = jnp.max(jax.nn.softmax(lg, axis=-1), axis=-1)
    le = (xt @ w_re + b_re).astype(jnp.float32).reshape(t, N_GROUPS, EXPERTS_PER_GROUP)
    le_sel = jnp.take_along_axis(le, g_sel[:, None, None], axis=1)[:, 0]
    top_l, top_i = lax.top_k(le_sel, TOP_K_IN_GROUP)
    gate = p_grp[:, None] * jax.nn.softmax(top_l, axis=-1)
    eid = (g_sel[:, None] * EXPERTS_PER_GROUP + top_i).astype(jnp.int32)
    a = t * TOP_K_IN_GROUP
    flat_e = eid.reshape(-1)
    flat_t = jnp.arange(a, dtype=jnp.int32) // TOP_K_IN_GROUP
    flat_w = gate.reshape(-1).astype(h.dtype)
    order = jnp.argsort(flat_e)
    se = flat_e[order]
    counts = jnp.bincount(flat_e, length=N_EXPERTS)
    pcounts = (counts + MOE_BLOCK - 1) // MOE_BLOCK * MOE_BLOCK
    pend = jnp.cumsum(pcounts)
    pstart = pend - pcounts
    start = jnp.cumsum(counts) - counts
    dest = pstart[se] + jnp.arange(a, dtype=jnp.int32) - start[se]
    n_blk = (a + N_EXPERTS * (MOE_BLOCK - 1) + MOE_BLOCK - 1) // MOE_BLOCK
    p_rows = n_blk * MOE_BLOCK
    row_t = jnp.full((p_rows,), t, jnp.int32).at[dest].set(flat_t[order])
    row_w = jnp.zeros((p_rows,), h.dtype).at[dest].set(flat_w[order])
    blk_e = jnp.minimum(jnp.searchsorted(pend, jnp.arange(n_blk) * MOE_BLOCK, side='right'),
                        N_EXPERTS - 1).astype(jnp.int32)
    x_pad = jnp.concatenate([xt, jnp.zeros((1, d), xt.dtype)], axis=0)
    xb = x_pad[row_t].reshape(n_blk, MOE_BLOCK, d)

    def expert_block(args):
        xblk, e = args
        return (jax.nn.silu(xblk @ w1[e]) * (xblk @ w3[e])) @ w2[e]

    yb = lax.map(expert_block, (xb, blk_e)).reshape(p_rows, d)
    y = jax.ops.segment_sum(yb * row_w[:, None], row_t, num_segments=t + 1)[:t]
    return y.reshape(b, n, d)

def _context_needed_after(i):
    return any(j % N_MIXERS == 0 for j in range(i + 1, DEPTH))

def second_inputs(seed: int = 0) -> dict:
    key = jax.random.key(seed)
    ks = jax.random.split(key, 21)
    nrm = lambda k, shape, s: jax.random.normal(k, shape, jnp.float32) * s
    return {
        'x': nrm(ks[0], (BATCH, SEQ, D_MODEL), 1.0),
        'c': nrm(ks[1], (BATCH, D_MODEL), 1.0),
        'ctx': nrm(ks[2], (BATCH, CTX_LEN, D_MODEL), 1.0),
        'c_ctx': nrm(ks[3], (D_MODEL,), 1.0),
        'w_mod': nrm(ks[4], (DEPTH, D_MODEL, 6 * D_MODEL), 0.5 * D_MODEL ** -0.5),
        'b_mod': nrm(ks[5], (DEPTH, 6 * D_MODEL), 0.02),
        'norm_mix': 1.0 + nrm(ks[6], (DEPTH, D_MODEL), 0.02),
        'norm_ffn': 1.0 + nrm(ks[7], (DEPTH, D_MODEL), 0.02),
        'attn_w_qkv': nrm(ks[8], (N_ATTN_LAYERS, D_MODEL, Q_DIM + 2 * KV_DIM), D_MODEL ** -0.5),
        'attn_q_norm': 1.0 + nrm(ks[9], (N_ATTN_LAYERS, HEAD_DIM), 0.02),
        'attn_k_norm': 1.0 + nrm(ks[10], (N_ATTN_LAYERS, HEAD_DIM), 0.02),
        'attn_w_o': nrm(ks[11], (N_ATTN_LAYERS, Q_DIM, D_MODEL), Q_DIM ** -0.5),
        'fourier_w_o': nrm(ks[12], (N_FOURIER_LAYERS, D_MODEL, D_MODEL), D_MODEL ** -0.5),
        'moe_w_rg': nrm(ks[13], (DEPTH, D_MODEL, N_GROUPS), D_MODEL ** -0.5),
        'moe_b_rg': nrm(ks[14], (DEPTH, N_GROUPS), 0.01),
        'moe_w_re': nrm(ks[15], (DEPTH, D_MODEL, N_EXPERTS), D_MODEL ** -0.5),
        'moe_b_re': nrm(ks[16], (DEPTH, N_EXPERTS), 0.01),
        'moe_w1': nrm(ks[17], (DEPTH, N_EXPERTS, D_MODEL, D_EXPERT), D_MODEL ** -0.5),
        'moe_w3': nrm(ks[18], (DEPTH, N_EXPERTS, D_MODEL, D_EXPERT), D_MODEL ** -0.5),
        'moe_w2': nrm(ks[19], (DEPTH, N_EXPERTS, D_EXPERT, D_MODEL), D_EXPERT ** -0.5),
        'final_norm': 1.0 + nrm(ks[20], (D_MODEL,), 0.02),
    }

def second_block(x, c, ctx, c_ctx, w_mod, b_mod, norm_mix, norm_ffn, attn_w_qkv, attn_q_norm, attn_k_norm,
              attn_w_o, fourier_w_o, moe_w_rg, moe_b_rg, moe_w_re, moe_b_re, moe_w1, moe_w3, moe_w2,
              final_norm):
    n_tok = x.shape[1]
    rows = n_tok // GRID_W
    rope = _axial_rope_tables(rows, x.dtype)
    silu_c = jax.nn.silu(c)[:, None, :]
    silu_cc = jax.nn.silu(c_ctx)[None, None, :]
    s_ctx = ctx
    for i in range(DEPTH):
        kind = i % N_MIXERS
        j = i // N_MIXERS
        ctx_next = _context_needed_after(i)
        moe_p = (moe_w_rg[i], moe_b_rg[i], moe_w_re[i], moe_b_re[i], moe_w1[i], moe_w3[i], moe_w2[i])
        sh1, sc1, g1, sh2, sc2, g2 = _ada_params(silu_c, w_mod[i], b_mod[i])
        h = _modulate(x, norm_mix[i], sh1, sc1)
        if kind == 0 or ctx_next:
            csh1, csc1, cg1, csh2, csc2, cg2 = _ada_params(silu_cc, w_mod[i], b_mod[i])
            h_c = _modulate(s_ctx, norm_mix[i], csh1, csc1)
        if kind == 0:
            y, y_c = _gqa_attention(h, h_c, attn_w_qkv[j], attn_q_norm[j], attn_k_norm[j], attn_w_o[j],
                                    rope, ctx_next)
        else:
            y = _fourier_mix(h, fourier_w_o[j])
            y_c = _fourier_mix(h_c, fourier_w_o[j]) if ctx_next else None
        x = x + g1 * y
        x = x + g2 * _hier_moe(_modulate(x, norm_ffn[i], sh2, sc2), *moe_p)
        if ctx_next:
            s_ctx = s_ctx + cg1 * y_c
            s_ctx = s_ctx + cg2 * _hier_moe(_modulate(s_ctx, norm_ffn[i], csh2, csc2), *moe_p)
    return _rms_norm(x, final_norm)


def setup_inputs(seed=0):
    out = dict(first_inputs(seed))
    for name, value in second_inputs(seed + 1).items():
        if name != "x":
            out[name + "_2"] = value
    return out


def reference(
    x, positions, ab_w_in, ab_gm_ln_g, ab_gm_ln_b, ab_gm_ws, ab_gm_bs, ab_mla_q_norm,
    ab_mla_kv_norm, ab_mla_w_uq, ab_mla_w_uk, ab_mla_w_uv, ab_w_o, c_w_in, c_cmp_pos, c_w_ck1,
    c_w_ck2, c_w_cv1, c_w_cv2, c_gate_b, c_w_o, moe_w_rg, moe_b_rg, moe_w_re, moe_b_re,
    moe_w_gate, moe_w_up, moe_w_down, ln1_g, ln1_b, ln2_g, ln2_b, c_2, ctx_2, c_ctx_2, w_mod_2,
    b_mod_2, norm_mix_2, norm_ffn_2, attn_w_qkv_2, attn_q_norm_2, attn_k_norm_2, attn_w_o_2,
    fourier_w_o_2, moe_w_rg_2, moe_b_rg_2, moe_w_re_2, moe_b_re_2, moe_w1_2, moe_w3_2, moe_w2_2,
    final_norm_2,
):
    x = first_block(
        x, positions, ab_w_in, ab_gm_ln_g, ab_gm_ln_b, ab_gm_ws, ab_gm_bs, ab_mla_q_norm,
        ab_mla_kv_norm, ab_mla_w_uq, ab_mla_w_uk, ab_mla_w_uv, ab_w_o, c_w_in, c_cmp_pos,
        c_w_ck1, c_w_ck2, c_w_cv1, c_w_cv2, c_gate_b, c_w_o, moe_w_rg, moe_b_rg, moe_w_re,
        moe_b_re, moe_w_gate, moe_w_up, moe_w_down, ln1_g, ln1_b, ln2_g, ln2_b,
    )
    return second_block(
        x, c_2, ctx_2, c_ctx_2, w_mod_2, b_mod_2, norm_mix_2, norm_ffn_2, attn_w_qkv_2,
        attn_q_norm_2, attn_k_norm_2, attn_w_o_2, fourier_w_o_2, moe_w_rg_2, moe_b_rg_2,
        moe_w_re_2, moe_b_re_2, moe_w1_2, moe_w3_2, moe_w2_2, final_norm_2,
    )


_drawn_inputs = setup_inputs


def setup_inputs(seed=0):
    import zlib

    import numpy as np

    out = dict(_drawn_inputs(seed))
    spreads = {}
    factors = {'ab_gm_ln_b': 7.038,
     'ab_mla_q_norm': 5.566,
     'ab_mla_kv_norm': 3.625,
     'c_cmp_pos': 3.972,
     'c_gate_b': 5.108,
     'moe_b_rg': 5.027,
     'moe_b_re': 5.488,
     'norm_mix_2': 7.652,
     'norm_ffn_2': 3.483,
     'attn_q_norm_2': 8.0,
     'attn_k_norm_2': 8.0,
     'moe_b_rg_2': 7.678,
     'moe_b_re_2': 6.547,
     'final_norm_2': 2.834}
    for name, (base, spread) in spreads.items():
        noise = np.random.default_rng([zlib.crc32(name.encode()), seed]).standard_normal(out[name].shape)
        drawn = base * np.exp(spread * noise) if base else spread * noise
        out[name] = __import__('jax').numpy.asarray(drawn.astype(out[name].dtype))
    for name, factor in factors.items():
        out[name] = (out[name] * factor).astype(out[name].dtype)
    return out
```

```python
from contextlib import ExitStack

import numpy as np

import concourse.bass as bass
from concourse import mybir

F32 = mybir.dt.float32
I32 = mybir.dt.int32
ALU = mybir.AluOpType
ACT = mybir.ActivationFunctionType
AX = mybir.AxisListType

P = 128
D = 1024
TOK = 256
TT = TOK // P
KC = D // P
NEG = -1e30

RING = 6
SLOT = 4096
FILL = 32

NG, EPG = 4, 8
NE = NG * EPG
CAP = 32
SIDE = P // CAP
ROUNDS = NE // SIDE
MAXPASS = TOK // CAP
START = 1
UNITS = 12
CREDIT = 4
XSLOTS = 2


FN1, FN2 = D // 4, D // 2
ALPHA = (2.0 * 2) ** 0.25
LN_EPS, RMS_EPS = 1e-5, 1e-6
CONSTS = 9


class Phase:

    def __init__(self, kind, layer, fn=0):
        self.kind, self.layer, self.fn = kind, layer, fn
        self.slot0 = 0
        self.moe = 0
        self.xt = 0
        self.h = 0
        self.ln = 0
        self.rms = 0

    def slots(self):
        if self.kind == "moe":
            return ROUNDS * moe_slots(self.fn)
        return {"ab": 6, "nsa": 8, "mod": 12, "gqa": 6, "fourier": 2}[self.kind]


def moe_slots(fn):
    return (2 * D * fn * SIDE + fn * D * SIDE) // (P * SLOT)




def build_model(nc, a, out, plan):
    with ExitStack() as ctx:
        def sb(name, shape, dt=F32):
            return ctx.enter_context(nc.sbuf_tensor(name, shape, dt))

        def sem(name):
            return ctx.enter_context(nc.semaphore(name))

        ring = sb("ring", [P, RING, SLOT])
        X = sb("X", [P, TT, D])
        XT = sb("XT", [P, KC, TOK])
        HM = sb("HM", [P, TT, D])
        gain = sb("gain", [P, D])
        shift = sb("shift", [P, D])
        mod = sb("mod", [P, 6 * D])
        work = sb("work", [P, 11300])
        wr = sb("wr", [P, KC, 4 + NE])
        br = sb("br", [P, 4 + NE])
        ident = sb("ident", [P, P])
        ones = sb("ones", [P, P])
        zeros = sb("zeros", [P, P])
        before = sb("before", [P, P])
        causal = sb("causal", [P, 3 * P])
        iota = sb("iota", [P, CAP])
        iota_i = sb("iota_i", [P, CAP], I32)
        thresh = sb("thresh", [P, MAXPASS - 1])
        stat = sb("stat", [P, 64])
        half = sb("half", [P, 64])
        extra_f = sb("extra_f", [P, 4])
        extra_i = sb("extra_i", [1, 4, 2], I32)

        acc = ctx.enter_context(nc.psum_tensor("acc", [P, TT, D], F32))
        pa = ctx.enter_context(nc.psum_tensor("pa", [P, 2, 512], F32))
        pb = ctx.enter_context(nc.psum_tensor("pb", [P, 2, 512], F32))

        x_loaded = sem("x_loaded")
        consts = sem("consts")
        full = [sem(f"slot{i}_full") for i in range(RING)]
        freed = sem("slot_freed")
        h_ready = sem("h_ready")
        xt_ps = sem("xt_ps")
        xt_ready = sem("xt_ready")
        vec = sem("vec_step")
        sca = sem("sca_step")
        poo = sem("pool_step")
        ln_loaded = sem("ln_loaded")
        ln_used = sem("ln_used")
        var_ready = sem("var_ready")
        rstd_ready = sem("rstd_ready")
        mix_done = sem("mix_done")
        small = sem("small_loaded")
        out_done = sem("out_done")
        phase_done = sem("phase_done")
        S = {}

        def sg(name):
            if name not in S:
                S[name] = sem(name)
            return S[name]

        class Link:

            def __init__(self, eng, s):
                self.eng, self.s, self.n = eng, s, 0

            def __call__(self, ins):
                self.n += 1
                ins.then_inc(self.s, 1)
                self.eng.wait_ge(self.s, self.n)

        def slot_wait(eng, q):
            eng.wait_ge(full[q % RING], FILL * (q // RING + 1))

        def slot_fill(sp, q, parts):
            if q >= RING:
                sp.wait_ge(freed, q - RING + 1)
            for dst, src in parts:
                sp.dma_start(dst, src).then_inc(full[q % RING], 16)

        def bc(v, shape):
            return v.to_broadcast(shape)

        class Area:

            def __init__(self, t):
                self.t, self.at = t, 0

            def take(self, *shape, rows=P):
                n = 1
                for s in shape:
                    n *= s
                v = self.t[0:rows, self.at:self.at + n]
                self.at += n
                assert self.at <= self.t.shape[1], (self.at, self.t.shape)
                if len(shape) == 1:
                    return v
                names = " ".join(f"d{i}" for i in range(len(shape)))
                return v.rearrange(f"p ({names}) -> p {names}", **{f"d{i}": s for i, s in enumerate(shape) if i})

        def source(ph):
            return X if ph.kind in ("ab", "nsa") or (ph.kind == "moe" and ph.fn == FN1) else HM

        def by_chunk(v):
            return v[:, :, :].rearrange("p a (k c) -> p (a k) c", c=P)

        def input_wait(eng, ph):
            if ph.h == 0:
                eng.wait_ge(x_loaded, 16)
                eng.wait_ge(consts, CONSTS)
            else:
                eng.wait_ge(h_ready, ph.h)

        def transpose_tensor(pe, src):
            for t in range(TT):
                dst = by_chunk((pa, pb)[t])
                for k in range(KC):
                    last = nc.tensor.transpose(dst[:, k, :], src[:, t, k * P:(k + 1) * P], ident[:, :])
                last.then_inc(xt_ps, 1)

        def transpose_scalar(act, n, dst):
            act.wait_ge(xt_ps, 2 * n + 1)
            nc.scalar.copy(dst[:, :, 0:P], by_chunk(pa)).then_inc(xt_ready, 1)

        def transpose_vector(dve, n, dst):
            dve.wait_ge(xt_ps, 2 * n + 2)
            nc.vector.tensor_copy(dst[:, :, P:TOK], by_chunk(pb)).then_inc(xt_ready, 1)

        def gain_pool(pool, n, g, b=None):
            if n:
                pool.wait_ge(ln_used, n)
            if b is None:
                pool.dma_start(gain[:, :], g.partition_broadcast(P)).then_inc(ln_loaded, 32)
                return
            pool.dma_start(gain[:, :], g.partition_broadcast(P)).then_inc(ln_loaded, 16)
            pool.dma_start(shift[:, :], b.partition_broadcast(P)).then_inc(ln_loaded, 16)

        def pow_pool(pool, n, cols):
            pool.wait_ge(var_ready, n + 1)
            nc.gpsimd.tensor_tensor(stat[:, cols], stat[:, cols], half[:, 0:cols.stop - cols.start],
                                    ALU.pow).then_inc(rstd_ready, 1)

        def ln_vector(dve, ph, link):
            for t in range(TT):
                link(nc.vector.scalar_tensor_tensor(X[:, t, :], X[:, t, :], ALPHA, acc[:, t, :], ALU.mult, ALU.add))
            st = stat[:, 0:24].rearrange("p (t h s) -> p t h s", t=TT, h=2)
            for t in range(TT):
                for h in range(2):
                    last = nc.vector.bn_stats(st[:, t, h, :], X[:, t, h * 512:(h + 1) * 512])
            link(last)
            mv = stat[:, 24:28].rearrange("p (t s) -> p t s", s=2)
            for t in range(TT):
                last = nc.vector.bn_aggr(mv[:, t, :], st[:, t, :, :].rearrange("p h s -> p (h s)"))
            link(last)
            nc.vector.tensor_scalar(stat[:, 32:34], mv[:, :, 1], LN_EPS, None, ALU.add).then_inc(var_ready, 1)
            dve.wait_ge(rstd_ready, ph.pow0 + ph.npow)
            for t in range(TT):
                last = nc.vector.tensor_scalar(X[:, t, :], X[:, t, :], mv[:, t, 0:1], stat[:, 32 + t:33 + t],
                                               ALU.subtract, ALU.mult)
            link(last)
            dve.wait_ge(ln_loaded, 32 * (ph.res + 1))
            link(nc.vector.tensor_tensor(X[:, :, :], X[:, :, :], bc(gain[:, :].unsqueeze(1), [P, TT, D]), ALU.mult))
            link(nc.vector.tensor_tensor(X[:, :, :], X[:, :, :], bc(shift[:, :].unsqueeze(1), [P, TT, D]), ALU.add))
            dve.sem_inc(ln_used, 1)
            dve.sem_inc(h_ready, 1)

        def squares(link, x, junk, col, n):
            for t in range(TT):
                link(nc.vector.tensor_tensor_reduce(out=junk[:, t, :], in0=x[:, t, :], in1=x[:, t, :], scale=1.0 / n, scalar=0.0,
                                                    op0=ALU.mult, op1=ALU.add, accum_out=stat[:, col + t:col + t + 1]))
            link(nc.vector.tensor_scalar(stat[:, col:col + TT], stat[:, col:col + TT], RMS_EPS, None, ALU.add))

        def modulate(link, x, dst, col, scale1, sh):
            for t in range(TT):
                link(nc.vector.scalar_tensor_tensor(dst[:, t, :], x[:, t, :], stat[:, col + t:col + t + 1], scale1, ALU.mult, ALU.mult))
            link(nc.vector.tensor_tensor(dst[:, :, :], dst[:, :, :], bc(sh.unsqueeze(1), [P, TT, D]), ALU.add))

        def mod_of(i):
            return mod[:, i * D:(i + 1) * D]

        def norm_vector(dve, ph, link, which):
            squares(link, X, HM, 32, D)
            dve.sem_inc(var_ready, 1)
            dve.wait_ge(ln_loaded, 32 * (ph.ln + 1))
            link(nc.vector.scalar_tensor_tensor(shift[:, :], mod_of(which + 1), 1.0, gain[:, :], ALU.add, ALU.mult))
            dve.wait_ge(rstd_ready, ph.pow0 + 1)
            modulate(link, X, HM, 32, shift[:, :], mod_of(which))
            dve.sem_inc(h_ready, 1)
            dve.sem_inc(ln_used, 1)

        def gated_vector(dve, link, which):
            link(nc.vector.tensor_tensor(HM[:, :, :], acc[:, :, :], bc(mod_of(which).unsqueeze(1), [P, TT, D]), ALU.mult))
            link(nc.vector.tensor_tensor(X[:, :, :], X[:, :, :], HM[:, :, :], ALU.add))

        area = Area(work)
        m_xg = XT[:, :, 0:P]
        m_p = area.take(TT, P)
        m_pw = area.take(TT, P)
        m_pwt = area.take(TOK)
        m_silu = area.take(512)
        m_hh = area.take(512)
        m_ht = area.take(4, P)
        m_yg = XT[:, :, P:TOK]
        m_log = area.take(TT, 4 + NE)
        m_rank = area.take(TT, NE)
        m_w = area.take(TT, NE)
        m_a = area.take(TT, NE)
        m_t = [area.take(TT, NE) for _ in range(4)]
        m_g = [area.take(TT, NG) for _ in range(3)]
        m_s = area.take(16, TT)
        xring = area.take(XSLOTS, SLOT)

        R = [{n: sem(f"{n}{k}") for n in (
            "p_ready", "pw_ready", "rank_next", "gathered", "xg_copied", "pwt_ps", "pwt_copied", "silu_done", "hh_ready", "ht_ps", "ht_copied", "y_copied", "added")} for k in ("", "_x")]
        xfull = [sem(f"xslot{i}_full") for i in range(XSLOTS)]
        xfreed = sem("xslot_freed")
        logits_done, ranks_done = sem("logits_done"), sem("ranks_done")
        assign_ready, extra_ready = sem("assign_ready"), sem("extra_ready")
        rexp_in, rexp_out = sem("router_exp_in"), sem("router_exp_out")
        wr_loaded = sem("router_loaded")

        def moe_names(ph):
            if ph.fn == FN1:
                return a["moe_w_gate"][ph.layer], a["moe_w_up"][ph.layer], a["moe_w_down"][ph.layer]
            return a["moe_w1_2"][ph.layer], a["moe_w3_2"][ph.layer], a["moe_w2_2"][ph.layer]

        def router_pool(pool, ph):
            s = "" if ph.fn == FN1 else "_2"
            if ph.moe:
                pool.wait_ge(assign_ready, ph.moe)
            for lo, hi, n in ((0, NG, "g"), (NG, NG + NE, "e")):
                pool.dma_start(wr[:, :, lo:hi], a[f"moe_w_r{n}{s}"][ph.layer].rearrange("(k p) n -> p k n", p=P)).then_inc(wr_loaded, 16)
                pool.dma_start(br[:, lo:hi], a[f"moe_b_r{n}{s}"][ph.layer].partition_broadcast(P)).then_inc(wr_loaded, 16)

        def router_tensor(pe, ph):
            pe.wait_ge(xt_ready, 2 * (ph.xt + 1))
            pe.wait_ge(wr_loaded, 64 * (ph.moe + 1))
            for t in range(TT):
                for k in range(KC):
                    last = nc.tensor.matmul(pa[:, t, 0:NG + NE], XT[:, k, t * P:(t + 1) * P], wr[:, k, :],
                                            start=(k == 0), stop=(k == KC - 1))
            last.then_inc(logits_done, 1)
            for t in range(TT):
                for h in range(2):
                    nc.tensor.matmul(acc[:, t, h * 512:(h + 1) * 512], zeros[:, :], source(ph)[:, t, h * 512:(h + 1) * 512],
                                     start=True, stop=True)
            pe.wait_ge(assign_ready, ph.moe + 1)
            nc.tensor.matmul(pb[:, 0, 0:NE], before[:, :], m_a[:, 0, :], start=True, stop=True)
            nc.tensor.matmul(pb[:, 0, NE:2 * NE], before[:, :], m_a[:, 1, :], start=True, stop=False)
            nc.tensor.matmul(pb[:, 0, NE:2 * NE], ones[:, :], m_a[:, 0, :], start=False, stop=True)
            nc.tensor.matmul(pb[:, 1, 0:NE], ones[:, :], m_a[:, 0, :], start=True, stop=False)
            nc.tensor.matmul(pb[:, 1, 0:NE], ones[:, :], m_a[:, 1, :], start=False, stop=True).then_inc(ranks_done, 1)

        def router_scalar(act, ph):
            n = 2 * ph.moe
            act.wait_ge(rexp_in, n + 1)
            nc.scalar.activation(m_g[1], m_g[1], ACT.Exp).then_inc(rexp_out, 1)
            act.wait_ge(rexp_in, n + 2)
            nc.scalar.activation(m_s[:, 4, :], m_s[:, 4, :], ACT.Exp).then_inc(rexp_out, 1)

        def router_vector(dve, ph, link):
            v = nc.vector

            def first_of(out_, x, m, iv, tmp, n):
                link(v.tensor_tensor(tmp, x, bc(m.unsqueeze(2), [P, TT, n]), ALU.is_equal))
                link(v.scalar_tensor_tensor(tmp, tmp, -64.0, bc(iv.unsqueeze(1), [P, TT, n]), ALU.mult, ALU.add))
                link(v.tensor_reduce(m_s[:, 15, :], tmp, AX.X, ALU.min))
                link(v.tensor_tensor(out_, tmp, bc(m_s[:, 15, :].unsqueeze(2), [P, TT, n]), ALU.is_equal))

            dve.wait_ge(logits_done, ph.moe + 1)
            link(v.tensor_tensor(m_log, pa[:, :, 0:NG + NE], bc(br[:, :].unsqueeze(1), [P, TT, NG + NE]), ALU.add))
            lg, le = m_log[:, :, 0:NG], m_log[:, :, NG:]
            gmax, l1, l2, gw, w1, w2 = (m_s[:, i, :] for i in range(6))
            l1, l2, gw, w1, w2 = (m_s[:, i, :] for i in (1, 2, 3, 5, 6))
            dif = m_s[:, 4, :]
            link(v.tensor_reduce(gmax, lg, AX.X, ALU.max))
            first_of(m_g[0], lg, gmax, iota[:, 0:NG], m_g[2], NG)
            v.tensor_tensor(m_g[1], lg, bc(gmax.unsqueeze(2), [P, TT, NG]), ALU.subtract).then_inc(rexp_in, 1)
            link(v.tensor_scalar(m_g[2], m_g[0], 1.0, -NEG, ALU.subtract, ALU.mult))
            lm, o1, o2, tmp = m_t
            link(v.tensor_tensor(lm.rearrange("p t (g e) -> p t g e", g=NG), le.rearrange("p t (g e) -> p t g e", g=NG),
                                 bc(m_g[2].unsqueeze(3), [P, TT, NG, EPG]), ALU.add))
            link(v.tensor_reduce(l1, lm, AX.X, ALU.max))
            first_of(o1, lm, l1, iota[:, 0:NE], tmp, NE)
            link(v.scalar_tensor_tensor(lm, o1, 3 * NEG, lm, ALU.mult, ALU.add))
            link(v.tensor_reduce(l2, lm, AX.X, ALU.max))
            first_of(o2, lm, l2, iota[:, 0:NE], tmp, NE)
            v.tensor_tensor(dif, l2, l1, ALU.subtract).then_inc(rexp_in, 1)
            v.tensor_tensor(m_a, o1, o2, ALU.add).then_inc(assign_ready, 1)
            dve.wait_ge(rexp_out, 2 * ph.moe + 2)
            link(v.tensor_reduce(gw, m_g[1], AX.X, ALU.add))
            link(v.tensor_scalar(w1, dif, 1.0, None, ALU.add))
            link(v.tensor_tensor(w1, w1, gw, ALU.mult))
            link(v.reciprocal(w1, w1))
            link(v.tensor_tensor(w2, w1, dif, ALU.mult))
            link(v.tensor_tensor(o1, o1, bc(w1.unsqueeze(2), [P, TT, NE]), ALU.mult))
            link(v.tensor_tensor(o2, o2, bc(w2.unsqueeze(2), [P, TT, NE]), ALU.mult))
            link(v.tensor_tensor(m_w, o1, o2, ALU.add))
            dve.wait_ge(ranks_done, ph.moe + 1)
            link(v.scalar_tensor_tensor(m_rank, pb[:, 0, 0:2 * NE].rearrange("p (t e) -> p t e", t=TT), 1.0, m_a,
                                        ALU.add, ALU.mult))
            link(v.tensor_scalar(m_rank, m_rank, 1.0, None, ALU.subtract))
            link(v.tensor_reduce(extra_f[:, 2:3], pb[:, 1, 0:NE], AX.X, ALU.max))
            link(v.tensor_scalar(m_s[:, 8:12, :].rearrange("p a b -> p (a b)")[:, 0:MAXPASS - 1], thresh[:, :], extra_f[:, 2:3], None, ALU.is_lt))
            link(v.tensor_reduce(extra_f[:, 0:1], m_s[:, 8:12, :].rearrange("p a b -> p (a b)")[:, 0:MAXPASS - 1], AX.X, ALU.add))
            link(v.tensor_copy(extra_i[0:1, ph.moe, :], extra_f[0:1, 0:2]))
            link(v.tensor_tensor(extra_f[:, 1:2], extra_f[:, 1:2], extra_f[:, 0:1], ALU.add))
            dve.sem_inc(extra_ready, 1)

        def round_sync(sp, ph, g, wait_free, fills, slot_of, inc):
            gate, up, down = moe_names(ph)
            ex = bass.ds(g * SIDE, SIDE)
            n = moe_slots(ph.fn)
            n_down = ph.fn // P
            rows = SLOT // (2 * SIDE * ph.fn)
            for i in range(n):
                dst = slot_of(i)
                wait_free(i)
                if i < n - n_down:
                    for m, w in enumerate((gate, up)):
                        src = w[ex].rearrange("j (c p r) f -> c p j (r f)", p=P, r=rows)[i]
                        sp.dma_start(dst[:, m * SLOT // 2:(m + 1) * SLOT // 2].rearrange("p (j f) -> p j f", j=SIDE), src).then_inc(fills(i), inc)
                else:
                    for m in range(2):
                        c = i - (n - n_down)
                        src = down[bass.ds(g * SIDE + m * 2, 2), c * P:(c + 1) * P, :].rearrange("j p f -> p j f")
                        sp.dma_start(dst[:, m * SLOT // 2:(m + 1) * SLOT // 2].rearrange("p (j f) -> p j f", j=2), src).then_inc(fills(i), inc)

        def round_tensor(pe, ph, r, t, wait_full, free, slot_of):
            fn = ph.fn
            src = source(ph)
            rows = SLOT // (2 * SIDE * fn)
            n_down = fn // P
            n_up = moe_slots(fn) - n_down
            xg_ps = pa[:, :, :].rearrange("p a (k c) -> p (a k) c", c=P)
            hbank = (pb[:, 0, 0:fn], pb[:, 1, 0:fn])
            pe.wait_ge(r["p_ready"], t + 1 + START)
            pe.wait_ge(r["y_copied"], 2 * t + START)
            for c in range(n_up):
                for q in range(rows):
                    for tt in range(TT):
                        lhs = src[:, tt, c * P * rows:(c + 1) * P * rows].rearrange("p (f r) -> p f r", r=rows)[:, :, q]
                        last = nc.tensor.matmul(xg_ps[:, c * rows + q, :], lhs, m_p[:, tt, :], start=(tt == 0), stop=(tt == TT - 1))
            last.then_inc(r["gathered"], 1)
            pe.wait_ge(r["pw_ready"], t + 1 + START)
            pe.wait_ge(r["hh_ready"], t + START)
            for tt in range(TT):
                last = nc.tensor.transpose(pb[:, 1, tt * P:(tt + 1) * P], m_pw[:, tt, :], ident[:, :])
            last.then_inc(r["pwt_ps"], 1)
            pe.wait_ge(r["pwt_copied"], t + 1 + START)
            pe.wait_ge(r["ht_copied"], t + START)
            pe.wait_ge(r["xg_copied"], 2 * (t + 1) + START)
            for c in range(n_up):
                wait_full(c)
                slot = slot_of(c).rearrange("p (m j r f) -> p m j r f", m=2, j=SIDE, r=rows)
                for q in range(rows):
                    k = c * rows + q
                    for m in range(2):
                        for j in range(SIDE):
                            last = nc.tensor.matmul(hbank[m][j * CAP:(j + 1) * CAP, :], m_xg[:, k, j * CAP:(j + 1) * CAP],
                                                    slot[:, m, j, q, :], start=(k == 0), stop=(k == KC - 1))
                last.then_inc(*free)
            pe.wait_ge(r["hh_ready"], t + 1 + START)
            for c in range(n_down):
                last = nc.tensor.transpose(pb[:, 0, c * P:(c + 1) * P], m_hh[:, c * P:(c + 1) * P], ident[:, :])
            last.then_inc(r["ht_ps"], 1)
            pe.wait_ge(r["ht_copied"], t + 1 + START)
            for c in range(n_down):
                wait_full(n_up + c)
                slot = slot_of(n_up + c).rearrange("p (j f) -> p j f", j=SIDE)
                for h in range(2):
                    for j in range(SIDE):
                        last = nc.tensor.matmul(pa[j * CAP:(j + 1) * CAP, h, :], m_ht[:, c, j * CAP:(j + 1) * CAP],
                                                slot[:, j, h * 512:(h + 1) * 512], start=(c == 0), stop=(c == n_down - 1))
                last.then_inc(*free)
            pe.wait_ge(r["y_copied"], 2 * (t + 1) + START)
            for tt in range(TT):
                for h in range(2):
                    last = nc.tensor.matmul(acc[:, tt, h * 512:(h + 1) * 512], m_pwt[:, tt * P:(tt + 1) * P],
                                            m_yg[:, 4 * h:4 * h + 4, :], start=False, stop=True, skip_group_check=True)
            last.then_inc(r["added"], 1)

        def round_scalar(act, ph, r, t, freed_up, freed_all):
            fn = ph.fn
            act.wait_ge(r["gathered"], t + 1 + START)
            nc.scalar.copy(m_xg[:, 0:4, :], pa[:, 0, :].rearrange("p (k c) -> p k c", c=P)).then_inc(r["xg_copied"], 1)
            freed_up(act)
            nc.scalar.activation(m_silu[:, 0:fn], pb[:, 0, 0:fn], ACT.Silu).then_inc(r["silu_done"], 1)
            freed_all(act)
            nc.scalar.copy(m_yg[:, 0:4, :], pa[:, 0, :].rearrange("p (k c) -> p k c", c=P)).then_inc(r["y_copied"], 1)

        def round_vector(dve, ph, r, t, g, freed_all):
            fn = ph.fn
            v = nc.vector
            ex = bass.ds(g * SIDE, SIDE)
            shape = [P, TT, SIDE, CAP]
            dve.wait_ge(r["rank_next"], t + START)
            dve.wait_ge(r["gathered"], t + START)
            one = m_p.rearrange("p t (j s) -> p t j s", j=SIDE)
            gated = m_pw.rearrange("p t (j s) -> p t j s", j=SIDE)
            v.tensor_tensor(one, bc(iota[:, :].unsqueeze(1).unsqueeze(1), shape),
                            bc(m_rank[:, :, ex].unsqueeze(3), shape), ALU.is_equal).then_inc(r["p_ready"], 1)
            dve.wait_ge(r["p_ready"], t + 1 + START)
            dve.wait_ge(r["pwt_ps"], t + START)
            v.tensor_tensor(gated, one, bc(m_w[:, :, ex].unsqueeze(3), shape), ALU.mult).then_inc(r["pw_ready"], 1)
            v.tensor_scalar(m_rank[:, :, ex], m_rank[:, :, ex], float(CAP), None, ALU.subtract).then_inc(r["rank_next"], 1)
            dve.wait_ge(r["gathered"], t + 1 + START)
            v.tensor_copy(m_xg[:, 4:8, :], pa[:, 1, :].rearrange("p (k c) -> p k c", c=P)).then_inc(r["xg_copied"], 1)
            dve.wait_ge(r["pwt_ps"], t + 1 + START)
            v.tensor_copy(m_pwt, pb[:, 1, 0:TOK]).then_inc(r["pwt_copied"], 1)
            dve.wait_ge(r["silu_done"], t + 1 + START)
            v.tensor_tensor(m_hh[:, 0:fn], m_silu[:, 0:fn], pb[:, 1, 0:fn], ALU.mult).then_inc(r["hh_ready"], 1)
            dve.wait_ge(r["ht_ps"], t + 1 + START)
            v.tensor_copy(m_ht[:, 0:fn // P, :], pb[:, 0, 0:fn].rearrange("p (c s) -> p c s", s=P)).then_inc(r["ht_copied"], 1)
            freed_all(dve)
            v.tensor_copy(m_yg[:, 4:8, :], pa[:, 1, :].rearrange("p (k c) -> p k c", c=P)).then_inc(r["y_copied"], 1)

        def moe_sync(sp, ph):
            n = moe_slots(ph.fn)
            with sp.Fori(0, ROUNDS) as g:
                def wait_free(i):
                    sp.wait_ge(freed, ph.slot0 + g * n + i - RING + 1)
                round_sync(sp, ph, g, wait_free, lambda i: full[(ph.slot0 + i) % RING],
                           lambda i: ring[:, (ph.slot0 + i) % RING, :], 16)
            sp.wait_ge(extra_ready, ph.moe + 1)
            more = sp.value_load(extra_i[0:1, ph.moe, 0:1], min_val=0, max_val=MAXPASS - 1)
            base = sp.value_load(extra_i[0:1, ph.moe, 1:2], min_val=0, max_val=4 * (MAXPASS - 1))
            unit = UNITS // n
            with sp.If(more > 0):
                with sp.Fori(0, more) as ps:
                    with sp.Fori(0, ROUNDS) as g:
                        t = (base + ps) * ROUNDS + g

                        def wait_free(i):
                            sp.wait_ge(xfreed, t * UNITS + (CREDIT + unit * (i + 1 - XSLOTS)))
                        round_sync(sp, ph, g, wait_free, lambda i: xfull[i % XSLOTS],
                                   lambda i: xring[:, i % XSLOTS, :], 16 * unit)

        def moe_tensor(pe, ph):
            n = moe_slots(ph.fn)
            router_tensor(pe, ph)
            with pe.Fori(0, ROUNDS) as g:
                def wait_full(i):
                    q = ph.slot0 + i
                    pe.wait_ge(full[q % RING], g * (FILL * (n // RING)) + FILL * (q // RING + 1))
                round_tensor(pe, ph, R[0], g + ROUNDS * ph.moe, wait_full, (freed, 1),
                             lambda i: ring[:, (ph.slot0 + i) % RING, :])
            pe.wait_ge(extra_ready, ph.moe + 1)
            more = pe.value_load(extra_i[0:1, ph.moe, 0:1], min_val=0, max_val=MAXPASS - 1)
            base = pe.value_load(extra_i[0:1, ph.moe, 1:2], min_val=0, max_val=4 * (MAXPASS - 1))
            unit = UNITS // n
            with pe.If(more > 0):
                pe.wait_ge(R[0]["y_copied"], 2 * ROUNDS * (ph.moe + 1) + START)
                with pe.Fori(0, more) as ps:
                    with pe.Fori(0, ROUNDS) as g:
                        t = (base + ps) * ROUNDS + g

                        def wait_full(i):
                            pe.wait_ge(xfull[i % XSLOTS], t * (FILL * UNITS // XSLOTS) + 32 * unit * (i // XSLOTS + 1))
                        round_tensor(pe, ph, R[1], t, wait_full, (xfreed, unit), lambda i: xring[:, i % XSLOTS, :])

        def moe_other(eng, ph, body, last=False):
            n = moe_slots(ph.fn)
            up = n - ph.fn // P
            with eng.Fori(0, ROUNDS) as g:
                body(R[0], g + ROUNDS * ph.moe, g,
                     lambda e: e.wait_ge(freed, ph.slot0 + g * n + up),
                     lambda e: e.wait_ge(freed, ph.slot0 + g * n + n))
            if last:
                eng.wait_ge(R[0]["added"], ROUNDS * (ph.moe + 1) + START)
            eng.wait_ge(extra_ready, ph.moe + 1)
            more = eng.value_load(extra_i[0:1, ph.moe, 0:1], min_val=0, max_val=MAXPASS - 1)
            base = eng.value_load(extra_i[0:1, ph.moe, 1:2], min_val=0, max_val=4 * (MAXPASS - 1))
            unit = UNITS // n
            with eng.If(more > 0):
                eng.wait_ge(R[0]["added"], ROUNDS * (ph.moe + 1) + START)
                eng.wait_ge(R[0]["rank_next"], ROUNDS * (ph.moe + 1) + START)
                with eng.Fori(0, more) as ps:
                    with eng.Fori(0, ROUNDS) as g:
                        t = (base + ps) * ROUNDS + g
                        body(R[1], t, g,
                             lambda e: e.wait_ge(xfreed, t * UNITS + (CREDIT + unit * up)),
                             lambda e: e.wait_ge(xfreed, t * UNITS + (CREDIT + UNITS)))
            if last:
                eng.wait_ge(R[1]["added"], (base + more) * ROUNDS + START)

        def tables_pool(pool, link):
            g = nc.gpsimd
            g.memset(ones[:, :], 1.0).then_inc(consts, 1)
            g.memset(zeros[:, :], 0.0).then_inc(consts, 1)
            g.memset(half[:, :], -0.5).then_inc(consts, 1)
            link(g.memset(ident[:, :], 0.0))
            g.affine_select(out=ident[:, :], in_=ident[:, :], compare_op=ALU.not_equal, fill=1.0, base=0,
                            pattern=[[-1, P]], channel_multiplier=1).then_inc(consts, 1)
            link(g.memset(before[:, :], 1.0))
            g.affine_select(out=before[:, :], in_=before[:, :], compare_op=ALU.is_gt, fill=0.0, base=0,
                            pattern=[[1, P]], channel_multiplier=-1).then_inc(consts, 1)
            link(g.memset(causal[:, :], 0.0))
            for lo, wide, base in ((0, P, 0), (P, 2 * P, P)):
                g.affine_select(out=causal[:, lo:lo + wide], in_=causal[:, lo:lo + wide], compare_op=ALU.is_ge, fill=NEG,
                                base=base, pattern=[[-1, wide]], channel_multiplier=1).then_inc(consts, 1)
            link(g.iota(iota_i[:, :], pattern=[[1, CAP]], base=0, channel_multiplier=0))
            g.tensor_copy(iota[:, :], iota_i[:, :]).then_inc(consts, 1)
            link(g.tensor_copy(thresh[:, :], iota_i[:, 0:MAXPASS - 1]))
            link(g.tensor_scalar(thresh[:, :], thresh[:, :], 1.0, float(CAP), ALU.add, ALU.mult))
            g.memset(extra_f[:, :], 0.0).then_inc(consts, 1)

        area = Area(work)
        d_part = area.take(2, 512)
        d_cond = area.take(KC, CAP)
        d_raw = area.take(2 * KC)
        d_sel = area.take(P)
        d_selx = area.take(P)
        d_bias = area.take(6 * D, rows=1)
        c_mod = work[:, 9200:9200 + 2 * D]
        MODC = 6 * D // 512
        cond_ready, cond_silu = sem("cond_ready"), sem("cond_silu")
        part_copied, row_ps, row_copied = sem("part_copied"), sem("row_ps"), sem("row_copied")

        def weights_of(w, cols, kk, i):
            return w[i * kk * P:(i + 1) * kk * P, cols].rearrange("(k p) c -> p k c", p=P)

        def stream_sync(sp, w, q0, n, kk, width):
            for i in range(n):
                dst = ring[:, (q0 + i) % RING, 0:kk * width].rearrange("p (k c) -> p k c", k=kk)
                src = weights_of(w, slice(0, width), kk, i)
                h = kk // 2
                slot_fill(sp, q0 + i, [(dst[:, 0:h, :], src[:, 0:h, :]), (dst[:, h:kk, :], src[:, h:kk, :])])

        def mod_sync(sp, ph):
            w = a["w_mod_2"][ph.layer]
            for n in range(MODC):
                dst = ring[:, (ph.slot0 + n) % RING, :].rearrange("p (k c) -> p k c", k=KC)
                src = w[:, n * 512:(n + 1) * 512].rearrange("(k p) c -> p k c", p=P)
                slot_fill(sp, ph.slot0 + n, [(dst[:, 0:4, :], src[:, 0:4, :]), (dst[:, 4:8, :], src[:, 4:8, :])])

        def mod_pool(pool, ph):
            pool.wait_ge(phase_done, ph.i)
            pool.dma_start(d_raw, a["cond"]).then_inc(small, 16)
            pool.dma_start(d_bias, a["b_mod_2"][ph.layer:ph.layer + 1, :]).then_inc(small, 16)

        def mod_tensor(pe, ph):
            n0 = MODC * ph.layer

            def row(n):
                pe.wait_ge(part_copied, n0 + n + 1)
                if n0 + n >= 2:
                    pe.wait_ge(row_copied, n0 + n - 1)
                lhs = [(d_sel, pb[:, n % 2, :])] + ([(d_selx, acc[:, n % 2, 0:512])] if ph.layer == 0 and n < 4 else [])
                for s, dst in lhs:
                    nc.tensor.matmul(dst, s, d_part[:, n % 2, :], start=True, stop=False)
                    last = nc.tensor.matmul(dst, ones[0:1, :], d_bias[0:1, n * 512:(n + 1) * 512], start=False, stop=True)
                last.then_inc(row_ps, 1)

            pe.wait_ge(phase_done, ph.i)
            pe.wait_ge(cond_silu, ph.layer + 1)
            pe.wait_ge(cond_ready, ph.layer + 1)
            pe.wait_ge(small, ph.small)
            for n in range(MODC):
                slot_wait(pe, ph.slot0 + n)
                if n >= 2:
                    pe.wait_ge(part_copied, n0 + n - 1)
                w = ring[:, (ph.slot0 + n) % RING, :].rearrange("p (k c) -> p k c", k=KC)
                for r in range(2):
                    for j in range(SIDE):
                        k = SIDE * r + j
                        last = nc.tensor.matmul(pa[j * CAP:(j + 1) * CAP, n % 2, :], d_cond[:, k, :], w[:, k, :],
                                                start=(r == 0), stop=(r == 1))
                last.then_inc(freed, 1)
                if n:
                    row(n - 1)
            row(MODC - 1)

        def mod_scalar(act, ph):
            n0 = MODC * ph.layer
            act.wait_ge(small, ph.small)
            act.wait_ge(cond_ready, ph.layer + 1)
            nc.scalar.activation(d_cond[:, :, 0:2], d_raw.rearrange("p (c k) -> p k c", c=2), ACT.Silu).then_inc(cond_silu, 1)
            for n in range(MODC):
                act.wait_ge(freed, ph.slot0 + n + 1)
                if n >= 2:
                    act.wait_ge(row_ps, n0 + n - 1)
                nc.scalar.copy(d_part[:, n % 2, :], pa[:, n % 2, :]).then_inc(part_copied, 1)

        def mod_vector(dve, ph, link):
            n0 = MODC * ph.layer
            v = nc.vector
            link(v.memset(d_cond, 0.0))
            link(v.memset(d_sel, 0.0))
            link(v.memset(d_selx, 0.0))
            for j in range(SIDE):
                v.memset(d_sel[j * CAP:j * CAP + 1, :], 1.0)
                last = v.memset(d_selx[j * CAP:j * CAP + 2, :], 1.0)
            link(last)
            link(v.tensor_tensor(d_selx, d_selx, d_sel, ALU.subtract))
            dve.sem_inc(cond_ready, 1)
            for n in range(MODC):
                dve.wait_ge(row_ps, n0 + n + 1)
                last = v.tensor_copy(mod[:, n * 512:(n + 1) * 512], pb[:, n % 2, :])
                if ph.layer == 0 and n < 4:
                    last = v.tensor_copy(c_mod[:, n * 512:(n + 1) * 512], acc[:, n % 2, 0:512])
                last.then_inc(row_copied, 1)
            dve.wait_ge(row_copied, n0 + MODC)

        area = Area(work)
        area.at = 6144
        t_e = area.take(2, 512)
        t_d = area.take(2, 2, P)
        t_pt = area.take(2, 512)
        t_m = area.take(2, 2)
        t_s = area.take(2, 2)
        s_done, s_masked, s_max, s_exp = sem("scores_done"), sem("scores_masked"), sem("scores_max"), sem("scores_exp")
        s_sumr, s_diag, s_pt, s_ptc, s_pv = sem("sum_inverse"), sem("diag_ready"), sem("weights_ps"), sem("weights_copied"), sem("values_done")
        heads_copied, mix_ready = sem("heads_copied"), sem("heads_ready")

        def att_tensor(pe, n0, sp):
            for i in range(sp["n"] + 2):
                if i < sp["n"]:
                    if i >= 2:
                        pe.wait_ge(s_masked, n0 + i - 1)
                    for cols, lhs, rhs in sp["scores"](i):
                        last = nc.tensor.matmul(pa[:, i % 2, cols], lhs, rhs, start=True, stop=True)
                    last.then_inc(s_done, 1)
                j = i - 1
                if 0 <= j < sp["n"]:
                    pe.wait_ge(s_diag, n0 + j + 1)
                    if j >= 2:
                        pe.wait_ge(s_ptc, n0 + j - 1)
                    for b, seg in enumerate(sp["blocks"]):
                        last = nc.tensor.matmul(pb[:, j % 2, b * P:(b + 1) * P], t_e[:, j % 2, b * P:(b + 1) * P],
                                                t_d[:, j % 2, seg, :], start=True, stop=True)
                    last.then_inc(s_pt, 1)
                j = i - 2
                if j >= 0:
                    pe.wait_ge(s_ptc, n0 + j + 1)
                    for dst, lhs, rhs, first, end in sp["values"](j, t_pt[:, j % 2, :]):
                        last = nc.tensor.matmul(dst, lhs, rhs, start=first, stop=end, skip_group_check=True)
                    last.then_inc(s_pv, 1)

        def att_scalar(act, n0, sp):
            w = len(sp["blocks"]) * P
            for i in range(sp["n"] + 1):
                if i < sp["n"]:
                    act.wait_ge(s_max, n0 + i + 1)
                    for k, (lo, hi) in enumerate(sp["segs"]):
                        last = nc.scalar.activation(t_e[:, i % 2, lo:hi], t_e[:, i % 2, lo:hi], ACT.Exp, bias=t_m[:, i % 2, k:k + 1],
                                                    accum_out=t_s[:, i % 2, k:k + 1])
                    last.then_inc(s_exp, 1)
                j = i - 1
                if j >= 0:
                    act.wait_ge(s_pt, n0 + j + 1)
                    if j >= 2:
                        act.wait_ge(s_pv, n0 + j - 1)
                    nc.scalar.copy(t_pt[:, j % 2, 0:w], pb[:, j % 2, 0:w]).then_inc(s_ptc, 1)

        def att_vector(dve, n0, sp):
            w = len(sp["blocks"]) * P
            ns = len(sp["segs"])
            v = nc.vector
            for i in range(sp["n"] + 1):
                if i < sp["n"]:
                    dve.wait_ge(s_done, n0 + i + 1)
                    if i >= 2:
                        dve.wait_ge(s_pt, n0 + i - 1)
                    if sp["mask"] is None:
                        v.tensor_scalar(t_e[:, i % 2, 0:w], pa[:, i % 2, 0:w], sp["scale"], None, ALU.mult).then_inc(s_masked, 1)
                    else:
                        v.scalar_tensor_tensor(t_e[:, i % 2, 0:w], pa[:, i % 2, 0:w], sp["scale"], sp["mask"], ALU.mult, ALU.add).then_inc(s_masked, 1)
                    dve.wait_ge(s_masked, n0 + i + 1)
                    for k, (lo, hi) in enumerate(sp["segs"]):
                        last = v.tensor_reduce(t_m[:, i % 2, k:k + 1], t_e[:, i % 2, lo:hi], AX.X, ALU.max, negate=True)
                    last.then_inc(s_max, 1)
                j = i - 1
                if j >= 0:
                    dve.wait_ge(s_exp, n0 + j + 1)
                    v.reciprocal(t_s[:, j % 2, 0:ns], t_s[:, j % 2, 0:ns]).then_inc(s_sumr, 1)
                    dve.wait_ge(s_sumr, n0 + j + 1)
                    for k in range(ns):
                        if sp["gate"]:
                            last = v.tensor_scalar(t_d[:, j % 2, k, :], ident[:, :], t_s[:, j % 2, k:k + 1], sp["gate"](j)[:, k:k + 1],
                                                   ALU.mult, ALU.mult)
                        else:
                            last = v.tensor_scalar(t_d[:, j % 2, k, :], ident[:, :], t_s[:, j % 2, k:k + 1], None, ALU.mult)
                    last.then_inc(s_diag, 1)

        def heads_scalar(act, ph):
            act.wait_ge(s_pv, ph.att0 + ph.natt)
            nc.scalar.copy(XT[:, KC - 4:KC - 2, :] if ph.kind == "ab" else XT[:, 0:4, :],
                           acc[:, 0, 0:512].rearrange("p (k c) -> p k c", c=TOK) if ph.kind == "ab"
                           else acc[:, 0, :].rearrange("p (k c) -> p k c", c=TOK)).then_inc(heads_copied, 1)

        def heads_vector(dve, ph):
            dve.wait_ge(s_pv, ph.att0 + ph.natt)
            nc.vector.tensor_copy(XT[:, KC - 2:KC, :] if ph.kind == "ab" else XT[:, 4:8, :],
                                  acc[:, 0, 512:D].rearrange("p (k c) -> p k c", c=TOK) if ph.kind == "ab"
                                  else acc[:, 1, :].rearrange("p (k c) -> p k c", c=TOK)).then_inc(heads_copied, 1)

        def out_tensor(pe, ph, q0):
            pe.wait_ge(heads_copied, 2 * (ph.mix + 1))
            for c in range(KC):
                if c % 4 == 0:
                    slot_wait(pe, q0 + c // 4)
                w = ring[:, (q0 + c // 4) % RING, :].rearrange("p (k c) -> p k c", k=4)[:, c % 4, :]
                for t in range(TT):
                    for h in range(2):
                        last = nc.tensor.matmul(acc[:, t, h * 512:(h + 1) * 512], XT[:, c, t * P:(t + 1) * P], w[:, h * 512:(h + 1) * 512],
                                                start=(c == 0), stop=(c == KC - 1))
                if c == 3:
                    last.then_inc(freed, 1)
            last.then_inc(freed, 1)

        NH, HD, NKV = 16, 64, 4
        NKEY = 2 * TOK
        area = Area(work)
        g_cx = area.take(TT, D)
        g_k = work[:, 0:2048].rearrange("p (t j u e) -> p t j u e", t=4, j=NKV, u=2)
        g_hct = area.take(KC, TOK)
        g_q = g_hct
        g_v = area.take(4, NKV * HD)
        g_tmp = area.take(D)
        area.at = 8800
        g_rope_flat = area.take(TT, 64)
        g_rope = g_rope_flat.rearrange("p t (s a e) -> p t s a e", s=2, a=2)
        g_gain = area.take(2, HD)
        g_kt = work[:, 9200:11248].rearrange("p (j t) -> p j t", j=NKV)
        cx_ready, kv_copied, q_copied = sem("context_ready"), sem("kv_copied"), sem("q_copied")
        qk_ready, qkt_ps, qkt_copied = sem("qk_ready"), sem("qkt_ps"), sem("qkt_copied")

        def gqa_spec():
            def scores(i):
                h, t = i // TT, i % TT
                r = slice(64 * (h % 2), 64 * (h % 2) + 64)
                yield slice(0, NKEY), g_q[r, h // 2, t * P:(t + 1) * P], g_kt[r, h // (NH // NKV), :]

            def values(i, weights):
                h, t = i // TT, i % TT
                dst = acc[64 * (h % 2):64 * (h % 2) + 64, h // 8, (h // 2 % 4) * TOK + t * P:(h // 2 % 4) * TOK + (t + 1) * P]
                j = h // (NH // NKV)
                for b in range(4):
                    yield dst, g_v[:, b, j * HD:(j + 1) * HD], weights[:, b * P:(b + 1) * P], b == 0, b == 3
            return dict(n=NH * TT, scores=scores, values=values, blocks=[0, 0, 0, 0], segs=[(0, NKEY)], mask=None,
                        scale=HD ** -0.5, gate=None)

        def gqa_sync(sp, ph):
            stream_sync(sp, a["attn_w_qkv_2"][0], ph.slot0, 4, 2, D + 2 * NKV * HD)
            stream_sync(sp, a["attn_w_o_2"][0], ph.slot0 + 4, 2, 4, D)

        def gqa_pool(pool, ph):
            pool.wait_ge(phase_done, ph.i)
            pool.dma_start(g_cx, a["ctx_2"][0].rearrange("(t p) d -> p t d", p=P)).then_inc(small, 16)
            pool.dma_start(g_rope_flat, a["rope_axes"].rearrange("(t p) e -> p t e", p=P)).then_inc(small, 16)
            pool.dma_start(g_gain[:, 0, :], a["attn_q_norm_2"][0].partition_broadcast(P)).then_inc(small, 16)
            pool.dma_start(g_gain[:, 1, :], a["attn_k_norm_2"][0].partition_broadcast(P)).then_inc(small, 16)
            gain_pool(pool, ph.ln, a["norm_mix_2"][ph.layer])
            pow_pool(pool, ph.pow0, slice(32, 36))
            pow_pool(pool, ph.pow0 + 1, slice(0, 48))

        def gqa_tensor(pe, ph):
            input_wait(pe, ph)
            transpose_tensor(pe, HM)
            pe.wait_ge(cx_ready, 1)
            pe.wait_ge(xt_ready, 2 * (ph.xt + 1))
            transpose_tensor(pe, g_cx)
            pe.wait_ge(xt_ready, 2 * (ph.xt + 2))
            for k in range(KC):
                q = ph.slot0 + k // 2
                if k % 2 == 0:
                    slot_wait(pe, q)
                w = ring[:, q % RING, 0:3072].rearrange("p (k c) -> p k c", k=2)[:, k % 2, :]
                for t in range(TT):
                    fl = dict(start=(k == 0), stop=(k == KC - 1))
                    lat = XT[:, k, t * P:(t + 1) * P]
                    for h in range(2):
                        nc.tensor.matmul(acc[:, t, h * 512:(h + 1) * 512], lat, w[:, h * 512:(h + 1) * 512], **fl)
                    nc.tensor.matmul(pa[:, t, :], lat, w[:, D:D + 512], **fl)
                    last = nc.tensor.matmul(pb[:, t, :], g_hct[:, k, t * P:(t + 1) * P], w[:, D:D + 512], **fl)
                if k % 2:
                    last.then_inc(freed, 1)
            pe.wait_ge(qk_ready, 1)
            for c in range(KC):
                for t in range(TT):
                    last = nc.tensor.transpose(acc[:, c // 4, (c % 4) * TOK + t * P:(c % 4) * TOK + (t + 1) * P],
                                               HM[:, t, c * P:(c + 1) * P], ident[:, :])
            for j in range(NKV):
                for t in range(4):
                    last = nc.tensor.transpose((pa, pb)[j // 2][:, j % 2, t * P:(t + 1) * P],
                                               work[:, (t * NKV + j) * P:(t * NKV + j + 1) * P], ident[:, :])
            last.then_inc(qkt_ps, 1)
            pe.wait_ge(qkt_copied, 2)
            att_tensor(pe, ph.att0, gqa_spec())
            out_tensor(pe, ph, ph.slot0 + 4)

        def gqa_scalar(act, ph):
            transpose_scalar(act, ph.xt, XT)
            transpose_scalar(act, ph.xt + 1, g_hct)
            act.wait_ge(freed, ph.slot0 + 4)
            for t in range(TT):
                last = nc.scalar.copy(HM[:, t, :], acc[:, t, :])
            last.then_inc(q_copied, 1)
            act.wait_ge(qkt_ps, 1)
            nc.scalar.copy(g_q[:, 0:4, :], acc[:, 0, :].rearrange("p (k c) -> p k c", c=TOK))
            nc.scalar.copy(g_kt[:, 0:2, :], pa[:, :, :]).then_inc(qkt_copied, 1)
            att_scalar(act, ph.att0, gqa_spec())
            heads_scalar(act, ph)

        def gqa_vector(dve, ph, link):
            v = nc.vector
            dve.wait_ge(small, ph.small)
            squares(link, X, HM, 32, D)
            for t in range(TT):
                link(v.tensor_tensor_reduce(out=HM[:, t, :], in0=g_cx[:, t, :], in1=g_cx[:, t, :], scale=1.0 / D, scalar=0.0,
                                            op0=ALU.mult, op1=ALU.add, accum_out=stat[:, 34 + t:35 + t]))
            link(v.tensor_scalar(stat[:, 34:36], stat[:, 34:36], RMS_EPS, None, ALU.add))
            dve.sem_inc(var_ready, 1)
            dve.wait_ge(ln_loaded, 32 * (ph.ln + 1))
            link(v.scalar_tensor_tensor(shift[:, :], mod_of(1), 1.0, gain[:, :], ALU.add, ALU.mult))
            link(v.scalar_tensor_tensor(c_mod[:, D:], c_mod[:, D:], 1.0, gain[:, :], ALU.add, ALU.mult))
            dve.wait_ge(rstd_ready, ph.pow0 + 1)
            modulate(link, X, HM, 32, shift[:, :], mod_of(0))
            dve.sem_inc(h_ready, 1)
            dve.sem_inc(ln_used, 1)
            modulate(link, g_cx, g_cx, 34, c_mod[:, D:], c_mod[:, 0:D])
            dve.sem_inc(cx_ready, 1)
            transpose_vector(dve, ph.xt, XT)
            transpose_vector(dve, ph.xt + 1, g_hct)
            dve.wait_ge(freed, ph.slot0 + 4)
            for i, bank in enumerate((pa, pb)):
                link(v.tensor_copy(g_v[:, 2 * i:2 * i + 2, :], bank[:, :, 256:512]))
                link(v.tensor_copy(g_k[:, 2 * i:2 * i + 2, :, 0, :], bank[:, :, 0:256].rearrange("p t (j e) -> p t j e", j=NKV)))
            dve.wait_ge(q_copied, 1)
            keys = work[:, 0:2048].rearrange("p (n u e) -> p n u e", u=2, e=HD)[:, :, 0, :]
            rows = [HM[:, 0, :].rearrange("p (h e) -> p h e", e=HD), HM[:, 1, :].rearrange("p (h e) -> p h e", e=HD), keys]
            sq = g_tmp.rearrange("p (h e) -> p h e", e=HD)
            for i, x in enumerate(rows):
                link(v.tensor_tensor(sq, x, x, ALU.mult))
                link(v.tensor_reduce(stat[:, 16 * i:16 * i + 16], sq, AX.X, ALU.add))
            link(v.tensor_scalar(stat[:, 0:48], stat[:, 0:48], 1.0 / HD, RMS_EPS, ALU.mult, ALU.add))
            dve.sem_inc(var_ready, 1)
            dve.wait_ge(rstd_ready, ph.pow0 + 2)
            for i, x in enumerate(rows):
                link(v.tensor_tensor(x, x, bc(stat[:, 16 * i:16 * i + 16].unsqueeze(2), [P, 16, HD]), ALU.mult))
                link(v.tensor_tensor(x, x, bc(g_gain[:, i // 2, :].unsqueeze(1), [P, 16, HD]), ALU.mult))
            for t in range(TT):
                for x in (rows[t], keys[:, t * NKV:(t + 1) * NKV, :]):
                    n = x.shape[1]
                    x5 = x.rearrange("p h (a u e) -> p h a u e", a=2, u=2)
                    x1, x2 = x5[:, :, :, 0, :], x5[:, :, :, 1, :]
                    cos, sin = (bc(g_rope[:, t, s, :, :].unsqueeze(1), [P, n, 2, 16]) for s in range(2))
                    u1, u2 = (g_tmp[:, o:o + 32 * n].rearrange("p (h a e) -> p h a e", h=n, a=2) for o in (0, 512))
                    link(v.tensor_tensor(u1, x1, sin, ALU.mult))
                    link(v.tensor_tensor(u2, x2, sin, ALU.mult))
                    link(v.tensor_tensor(x1, x1, cos, ALU.mult))
                    link(v.tensor_tensor(x2, x2, cos, ALU.mult))
                    link(v.tensor_tensor(x1, x1, u2, ALU.subtract))
                    link(v.tensor_tensor(x2, x2, u1, ALU.add))
            link(v.tensor_copy(work[:, 0:2048].rearrange("p (n u e) -> p n u e", u=2, e=HD)[:, :, 1, :], keys))
            dve.sem_inc(qk_ready, 1)
            dve.wait_ge(qkt_ps, 1)
            v.tensor_copy(g_q[:, 4:8, :], acc[:, 1, :].rearrange("p (k c) -> p k c", c=TOK))
            v.tensor_copy(g_kt[:, 2:4, :], pb[:, :, :]).then_inc(qkt_copied, 1)
            att_vector(dve, ph.att0, gqa_spec())
            heads_vector(dve, ph)
            dve.wait_ge(freed, ph.slot0 + 6)
            gated_vector(dve, link, 2)

        GD = D // 4
        area = Area(work)
        f_tab_flat = area.take(2, 4 * TOK)
        f_tab = f_tab_flat.rearrange("p t (s n) -> p t s n", s=4)
        f_a = area.take(KC, 2 * TOK)
        f_ps, f_copied, f_done = sem("dft_ps"), sem("dft_copied"), sem("dft_done")

        def fourier_sync(sp, ph):
            stream_sync(sp, a["fourier_w_o_2"][0], ph.slot0, 2, 4, D)

        def fourier_pool(pool, ph):
            pool.wait_ge(phase_done, ph.i)
            pool.dma_start(f_tab_flat, a["dft"].rearrange("(t p) n -> p t n", p=P)).then_inc(small, 16)
            gain_pool(pool, ph.ln, a["norm_mix_2"][ph.layer])
            pow_pool(pool, ph.pow0, slice(32, 34))

        def fourier_tensor(pe, ph):
            input_wait(pe, ph)
            pe.wait_ge(small, ph.small)
            for c in range(KC):
                if c >= 4:
                    pe.wait_ge(f_copied, c - 3)
                for t in range(TT):
                    last = nc.tensor.matmul((pa, pb)[c // 2 % 2][:, c % 2, :], HM[:, t, c * P:(c + 1) * P], f_tab[:, t, 0:2, :],
                                            start=(t == 0), stop=(t == 1))
                last.then_inc(f_ps, 1)
            pe.wait_ge(f_copied, KC)
            for c in range(KC):
                g = c // 2
                for i in range(2):
                    for s in range(2):
                        last = nc.tensor.matmul(acc[:, c // 4, (c % 4) * TOK:(c % 4 + 1) * TOK], f_tab[:, i, 2 + s, (c % 2) * P:(c % 2 + 1) * P],
                                                f_a[:, 2 * g + i, s * TOK:(s + 1) * TOK], start=(i + s == 0), stop=(i + s == 2))
            last.then_inc(f_done, 1)
            out_tensor(pe, ph, ph.slot0)

        def fourier_scalar(act, ph):
            act.wait_ge(f_done, 1)
            nc.scalar.copy(XT[:, 0:4, :], acc[:, 0, :].rearrange("p (k c) -> p k c", c=TOK)).then_inc(heads_copied, 1)

        def fourier_vector(dve, ph, link):
            v = nc.vector
            norm_vector(dve, ph, link, 0)
            for c in range(KC):
                dve.wait_ge(f_ps, c + 1)
                v.tensor_copy(f_a[:, c, :], (pa, pb)[c // 2 % 2][:, c % 2, :]).then_inc(f_copied, 1)
            dve.wait_ge(f_done, 1)
            v.tensor_copy(XT[:, 4:8, :], acc[:, 1, :].rearrange("p (k c) -> p k c", c=TOK)).then_inc(heads_copied, 1)
            dve.wait_ge(freed, ph.slot0 + 2)
            gated_vector(dve, link, 2)

        NM, NOPE, ROPE, MV = 8, 64, 32, 64
        HQ = NOPE + ROPE
        GW = D // 2
        NGM = GW // P
        QR, KVR = D // 4, D // 8
        LAT = QR + KVR + ROPE
        AB_IN = 2 * GW + LAT
        wide = Area(mod)
        b_q = wide.take(TT, NM, HQ)
        b_k = wide.take(TT, NM, HQ)
        b_u = wide.take(NGM, TOK)
        b_v = wide.take(TT, GW)
        b_latt = wide.take(3, TOK)
        area = Area(work)
        b_qt = area.take(NM, TOK)
        b_kt = area.take(NM, TOK)
        b_wuq = area.take(2, NM * HQ)
        b_bs = area.take(NGM, P)
        area.at = 8720
        b_wst = area.take(NGM, P)
        b_vals = area.take(TT, NM * MV)
        b_qg = area.take(QR)
        b_kvg = area.take(KVR)
        b_kr = area.take(TT, ROPE)
        b_cos = area.take(TT, ROPE // 2)
        b_sin = area.take(TT, ROPE // 2)
        b_ang = area.take(2, TT, ROPE // 2)
        b_turn = area.take(2, TT, ROPE // 2)
        b_freq = area.take(ROPE // 2)
        b_pos = area.take(TT)
        hm = Area(HM[:, :, :].rearrange("p t d -> p (t d)"))
        b_lat = hm.take(TT, LAT)
        b_wuk = hm.take(NM * NOPE)
        b_wuv = hm.take(NM * MV)
        b_posi = hm.take(TT).bitcast(I32)
        b_ws = t_pt
        b_mask = t_d[:, 0, 0, :]
        b_rot = t_e
        ws_ps, ws_ready = sem("mixing_t_ps"), sem("mixing_ready")
        ang_ready, trig_ready, gelu_ready = sem("angles_ready"), sem("trig_ready"), sem("gelu_ready")
        vn_ready, gm_ps, gm_read = sem("gmlp_normed"), sem("gmlp_ps"), sem("gmlp_read")
        lat_ready, latt_ps, latt_copied = sem("latents_ready"), sem("latents_t_ps"), sem("latents_t_copied")
        up_done, up_copied = sem("up_done"), sem("up_copied")
        b_qk, b_qkt, b_qktc = sem("mla_qk_ready"), sem("mla_qkt_ps"), sem("mla_qkt_copied")
        TWO_PI = (6.28125, 1.93500518798828125e-3, 3.0198368e-7)
        MAGIC = 1.5 * 2.0 ** 23

        def ab_spec():
            def scores(i):
                yield slice(0, P), b_qt[0:HQ, i, 0:P], b_kt[0:HQ, i, 0:P]
                yield slice(P, 3 * P), b_qt[0:HQ, i, P:TOK], b_kt[0:HQ, i, :]

            def values(i, weights):
                r = slice(64 * (i % 2), 64 * (i % 2) + 64)
                at = (i // 2) * TOK
                v = b_vals[:, :, i * MV:(i + 1) * MV]
                yield acc[r, 0, at:at + P], v[:, 0, :], weights[:, 0:P], True, True
                yield acc[r, 0, at + P:at + TOK], v[:, 0, :], weights[:, P:2 * P], True, False
                yield acc[r, 0, at + P:at + TOK], v[:, 1, :], weights[:, 2 * P:3 * P], False, True
            return dict(n=NM, scores=scores, values=values, blocks=[0, 1, 1], segs=[(0, P), (P, 3 * P)],
                        mask=causal[:, :], scale=HQ ** -0.5, gate=None)

        def ab_sync(sp, ph):
            stream_sync(sp, a["ab_w_in"][0], ph.slot0, 4, 2, AB_IN)
            stream_sync(sp, a["ab_w_o"][0], ph.slot0 + 4, 2, 4, D)

        def ab_pool(pool, ph):
            for dst, src in (
                    (b_posi, a["pos_cols"]), (b_freq, a["freqs"][0].partition_broadcast(P)),
                    (b_ws.rearrange("p a (g s) -> p (a g) s", g=4)[:, 0:NGM, :], a["ab_gm_ws"][0].rearrange("g t s -> t g s")),
                    (b_wuq, a["ab_mla_w_uq"][0].rearrange("(c p) n -> p c n", p=P)),
                    (b_wuk, a["ab_mla_w_uk"][0]), (b_wuv, a["ab_mla_w_uv"][0]),
                    (b_qg, a["ab_mla_q_norm"][0].partition_broadcast(P)), (b_kvg, a["ab_mla_kv_norm"][0].partition_broadcast(P)),
                    (b_bs, a["ab_gm_bs"][0].partition_broadcast(P))):
                pool.dma_start(dst, src).then_inc(small, 16)
            pool.dma_start(gain[:, 0:GW], a["ab_gm_ln_g"][0].partition_broadcast(P)).then_inc(ln_loaded, 16)
            pool.dma_start(gain[:, GW:D], a["ab_gm_ln_b"][0].partition_broadcast(P)).then_inc(ln_loaded, 16)
            pow_pool(pool, ph.pow0, slice(0, 6))
            gain_pool(pool, ph.res, a["ln1_g"][0], a["ln1_b"][0])
            pow_pool(pool, ph.pow0 + 1, slice(32, 34))

        def ab_tensor(pe, ph):
            input_wait(pe, ph)
            transpose_tensor(pe, X)
            pe.wait_ge(small, ph.small)
            ws = b_ws.rearrange("p a (g s) -> p (a g) s", g=4)
            for g in range(NGM):
                last = nc.tensor.transpose(acc[:, 0, g * P:(g + 1) * P], ws[:, g, :], ident[:, :])
            last.then_inc(ws_ps, 1)
            pe.wait_ge(xt_ready, 2 * (ph.xt + 1))
            pe.wait_ge(ws_ready, 1)
            for k in range(KC):
                q = ph.slot0 + k // 2
                if k % 2 == 0:
                    slot_wait(pe, q)
                w = ring[:, q % RING, 0:2 * AB_IN].rearrange("p (k c) -> p k c", k=2)[:, k % 2, :]
                fl = dict(start=(k == 0), stop=(k == KC - 1), skip_group_check=True)
                for m in range(NGM):
                    nc.tensor.matmul(pa[:, m // 2, (m % 2) * TOK:(m % 2 + 1) * TOK], w[:, m * P:(m + 1) * P], XT[:, k, :],
                                     start=(k == 0 and m % 2 == 0), stop=(k == KC - 1), skip_group_check=True)
                for t in range(TT):
                    lat = XT[:, k, t * P:(t + 1) * P]
                    nc.tensor.matmul(acc[:, t, 0:GW], lat, w[:, GW:2 * GW], **fl)
                    last = nc.tensor.matmul(acc[:, t, 512:512 + LAT], lat, w[:, 2 * GW:AB_IN], **fl)
                if k % 2:
                    last.then_inc(freed, 1)
            pe.wait_ge(lat_ready, 1)
            flat = pb[:, :, :].rearrange("p a c -> p (a c)")
            for c in range(3):
                for t in range(TT):
                    last = nc.tensor.transpose(flat[:, c * TOK + t * P:c * TOK + (t + 1) * P], b_lat[:, t, c * P:(c + 1) * P], ident[:, :])
            last.then_inc(latt_ps, 1)
            pe.wait_ge(latt_copied, 1)
            for t in range(TT):
                for h in range(2):
                    for c in range(2):
                        nc.tensor.matmul(acc[:, t, 512 * h:512 * h + NM * HQ // 2], b_latt[:, c, t * P:(t + 1) * P],
                                         b_wuq[:, c, h * NM * HQ // 2:(h + 1) * NM * HQ // 2], start=(c == 0), stop=(c == 1))
                nc.tensor.matmul(pb[:, t, :], b_latt[:, 2, t * P:(t + 1) * P], b_wuk, start=True, stop=True)
            pe.wait_ge(vn_ready, 1)
            for g in range(NGM):
                for n in range(TT):
                    last = nc.tensor.matmul(pa[:, g // 2, (g % 2) * TOK + n * P:(g % 2) * TOK + (n + 1) * P],
                                            b_v[:, n, g * P:(g + 1) * P], b_wst[:, g, :], start=True, stop=True)
            last.then_inc(gm_ps, 1)
            pe.wait_ge(gm_read, 1)
            for t in range(TT):
                last = nc.tensor.matmul(pa[:, t, :], b_latt[:, 2, t * P:(t + 1) * P], b_wuv, start=True, stop=True)
            last.then_inc(up_done, 1)
            pe.wait_ge(b_qk, 1)
            for h in range(NM):
                for t in range(TT):
                    at = (h % 4) * TOK + t * P
                    nc.tensor.transpose(acc[0:HQ, h // 4, at:at + P], b_q[:, t, h, :], ident[:, :])
                    at = (h % 2) * TOK + t * P
                    last = nc.tensor.transpose((pa, pb)[h // 4][0:HQ, h // 2 % 2, at:at + P], b_k[:, t, h, :], ident[:, :])
            last.then_inc(b_qkt, 1)
            pe.wait_ge(b_qktc, 2)
            att_tensor(pe, ph.att0, ab_spec())
            out_tensor(pe, ph, ph.slot0 + 4)

        def ab_scalar(act, ph):
            transpose_scalar(act, ph.xt, XT)
            act.wait_ge(ang_ready, 1)
            nc.scalar.activation(b_sin, b_ang[:, 0, :, :], ACT.Sin)
            nc.scalar.activation(b_cos, b_ang[:, 1, :, :], ACT.Sin).then_inc(trig_ready, 1)
            act.wait_ge(freed, ph.slot0 + 4)
            for t in range(TT):
                nc.scalar.activation(b_v[:, t, :], acc[:, t, 0:GW], ACT.Gelu_apprx_tanh)
            nc.scalar.activation(b_u, pa[:, :, :].rearrange("p a (m c) -> p (a m) c", m=2), ACT.Gelu_apprx_tanh).then_inc(gelu_ready, 1)
            act.wait_ge(latt_ps, 1)
            nc.scalar.copy(b_latt, pb[:, :, :].rearrange("p a (m c) -> p (a m) c", m=2)[:, 0:3, :]).then_inc(latt_copied, 1)
            act.wait_ge(up_done, 1)
            for t in range(TT):
                nc.scalar.copy(b_q[:, t, :, :].rearrange("p (a h) e -> p a (h e)", a=2),
                               acc[:, t, :].rearrange("p (a c) -> p a c", a=2)[:, :, 0:NM * HQ // 2])
            nc.scalar.copy(b_vals, pa[:, :, :]).then_inc(up_copied, 1)
            act.wait_ge(b_qkt, 1)
            for i in range(2):
                last = nc.scalar.copy(b_qt[0:HQ, 4 * i:4 * i + 4, :], acc[0:HQ, i, :].rearrange("p (h c) -> p h c", c=TOK))
            last.then_inc(b_qktc, 1)
            att_scalar(act, ph.att0, ab_spec())
            heads_scalar(act, ph)

        def ab_vector(dve, ph, link):
            v = nc.vector
            transpose_vector(dve, ph.xt, XT)
            dve.wait_ge(small, ph.small)
            link(v.tensor_copy(b_pos, b_posi))
            for i in range(2):
                link(v.tensor_tensor(b_ang[:, i, :, :], bc(b_pos.unsqueeze(2), [P, TT, ROPE // 2]), bc(b_freq.unsqueeze(1), [P, TT, ROPE // 2]), ALU.mult))
            link(v.tensor_scalar(b_turn[:, 0, :, :], b_ang[:, 0, :, :], 1 / (2 * np.pi), MAGIC, ALU.mult, ALU.add))
            link(v.tensor_scalar(b_turn[:, 1, :, :], b_ang[:, 1, :, :], 1 / (2 * np.pi), 0.25, ALU.mult, ALU.add))
            link(v.tensor_scalar(b_turn[:, 1, :, :], b_turn[:, 1, :, :], MAGIC, None, ALU.add))
            link(v.tensor_scalar(b_turn, b_turn, MAGIC, None, ALU.subtract))
            for part in TWO_PI:
                link(v.scalar_tensor_tensor(b_ang.rearrange("p i t e -> p (i t e)"), b_turn.rearrange("p i t e -> p (i t e)"), -part,
                                            b_ang.rearrange("p i t e -> p (i t e)"), ALU.mult, ALU.add))
            link(v.tensor_scalar(b_ang[:, 1, :, :], b_ang[:, 1, :, :], float(np.pi / 2), None, ALU.add))
            link(v.tensor_scalar(b_ang, b_ang, 3.1415925, -3.1415925, ALU.min, ALU.max))
            dve.sem_inc(ang_ready, 1)
            link(v.tensor_tensor(b_mask, before[:, :], ident[:, :], ALU.add))
            dve.wait_ge(ws_ps, 1)
            link(v.tensor_tensor(b_wst, acc[:, 0, 0:GW].rearrange("p (g t) -> p g t", g=NGM), bc(b_mask.unsqueeze(1), [P, NGM, P]), ALU.mult))
            dve.sem_inc(ws_ready, 1)
            dve.wait_ge(freed, ph.slot0 + 4)
            for t in range(TT):
                last = v.tensor_copy(b_lat[:, t, :], acc[:, t, 512:512 + LAT])
            link(last)
            junk = b_rot
            for t in range(TT):
                for lo, n, col in ((0, QR, 2), (QR, KVR, 4)):
                    x = b_lat[:, t, lo:lo + n]
                    link(v.tensor_tensor_reduce(out=junk[:, t, 0:n], in0=x, in1=x, scale=1.0 / n, scalar=0.0,
                                                op0=ALU.mult, op1=ALU.add, accum_out=stat[:, col + t:col + t + 1]))
            dve.wait_ge(gelu_ready, 1)
            for t in range(TT):
                last = v.bn_stats(stat[:, 8 + 6 * t:14 + 6 * t], b_v[:, t, :])
            link(last)
            for t in range(TT):
                last = v.bn_aggr(stat[:, 24 + 2 * t:26 + 2 * t], stat[:, 8 + 6 * t:14 + 6 * t])
            link(last)
            mv = stat[:, 24:28].rearrange("p (t s) -> p t s", s=2)
            link(v.tensor_copy(stat[:, 0:2], mv[:, :, 1]))
            v.tensor_scalar(stat[:, 0:6], stat[:, 0:6], LN_EPS, None, ALU.add).then_inc(var_ready, 1)
            dve.wait_ge(rstd_ready, ph.pow0 + 1)
            for t in range(TT):
                for lo, n, col in ((0, QR, 2), (QR, KVR, 4)):
                    x = b_lat[:, t, lo:lo + n]
                    link(v.scalar_tensor_tensor(x, x, stat[:, col + t:col + t + 1], b_qg if lo == 0 else b_kvg, ALU.mult, ALU.mult))
            dve.sem_inc(lat_ready, 1)
            for t in range(TT):
                last = v.tensor_scalar(b_v[:, t, :], b_v[:, t, :], mv[:, t, 0:1], stat[:, t:t + 1], ALU.subtract, ALU.mult)
            link(last)
            dve.wait_ge(ln_loaded, 32 * (ph.ln + 1))
            link(v.tensor_tensor(b_v, b_v, bc(gain[:, 0:GW].unsqueeze(1), [P, TT, GW]), ALU.mult))
            link(v.tensor_tensor(b_v, b_v, bc(gain[:, GW:D].unsqueeze(1), [P, TT, GW]), ALU.add))
            dve.sem_inc(ln_used, 1)
            dve.sem_inc(vn_ready, 1)
            dve.wait_ge(trig_ready, 1)

            def rotate(dst1, dst2, x1, x2, cos, sin, u1, u2):
                link(v.tensor_tensor(u1, x1, sin, ALU.mult))
                link(v.tensor_tensor(u2, x2, sin, ALU.mult))
                link(v.tensor_tensor(dst1, x1, cos, ALU.mult))
                link(v.tensor_tensor(dst2, x2, cos, ALU.mult))
                link(v.tensor_tensor(dst1, dst1, u2, ALU.subtract))
                link(v.tensor_tensor(dst2, dst2, u1, ALU.add))
            R2 = ROPE // 2
            x = b_lat[:, :, QR + KVR:LAT]
            u = [b_rot[:, i, 0:TT * R2].rearrange("p (t e) -> p t e", t=TT) for i in range(2)]
            rotate(b_kr[:, :, 0:R2], b_kr[:, :, R2:], x[:, :, 0:R2], x[:, :, R2:], b_cos, b_sin, *u)
            dve.wait_ge(gm_ps, 1)
            y = XT[:, 0:NGM, :]
            link(v.tensor_tensor(y.rearrange("p g (n t) -> p g n t", n=TT), pa[:, :, :].rearrange("p a (m n t) -> p (a m) n t", m=2, n=TT),
                                 bc(b_bs.unsqueeze(2), [P, NGM, TT, P]), ALU.add))
            dve.sem_inc(gm_read, 1)
            link(v.tensor_tensor(y, y, b_u, ALU.mult))
            dve.wait_ge(up_done, 1)
            for t in range(TT):
                link(v.tensor_copy(b_k[:, t, :, 0:NOPE], pb[:, t, :].rearrange("p (h e) -> p h e", e=NOPE)))
            link(v.tensor_copy(b_k[:, :, :, NOPE:HQ], bc(b_kr.unsqueeze(2), [P, TT, NM, ROPE])))
            dve.wait_ge(up_copied, 1)
            x1, x2 = b_q[:, :, :, NOPE:NOPE + R2], b_q[:, :, :, NOPE + R2:HQ]
            u = [b_rot[:, i, 0:TT * NM * R2].rearrange("p (t h e) -> p t h e", t=TT, h=NM) for i in range(2)]
            cs = [bc(z.unsqueeze(2), [P, TT, NM, R2]) for z in (b_cos, b_sin)]
            rotate(x1, x2, x1, x2, *cs, *u)
            dve.sem_inc(b_qk, 1)
            dve.wait_ge(b_qkt, 1)
            for i, bank in enumerate((pa, pb)):
                last = v.tensor_copy(b_kt[0:HQ, 4 * i:4 * i + 4, :], bank[0:HQ, :, :].rearrange("p a (h c) -> p (a h) c", h=2))
            last.then_inc(b_qktc, 1)
            att_vector(dve, ph.att0, ab_spec())
            heads_vector(dve, ph)
            dve.wait_ge(freed, ph.slot0 + 6)
            ln_vector(dve, ph, link)

        SH, SG, SD = 16, 2, 64
        CL, CS = 32, 16
        NB = TOK // CS - CL // CS + 1
        HID = 256
        SQ = SH * SD
        C_IN = SQ + 6 * SG * SD + 3 * SH
        CC = CL * SD // P
        VW = 3 * P + 3 * SH
        wide = Area(mod)
        n_pct = wide.take(TT * SH, P, rows=NB)
        n_qt = wide.take(KC, TOK)
        hm = Area(HM[:, :, :].rearrange("p t d -> p (t d)"))
        n_kt = hm.take(2, SG, TOK)
        n_v = hm.take(TT, VW)
        area = Area(work)
        n_ft = area.take(2, CC, SG * NB)
        n_hid = area.take(2, HID)
        n_hidt = area.take(2, 2, SG * NB)
        n_kc = area.take(SG * NB)
        n_vc = area.take(SG, SD, rows=NB)
        n_e = area.take(TT, SH, NB)
        n_open = area.take(TT, NB)
        n_shut = area.take(TT, NB)
        n_w2 = area.take(2, 2, SD)
        n_pos = area.take(2 * CC)
        n_gb = area.take(3 * SH)
        n_gate = area.take(TT, 3 * SH)
        n_max = area.take(TT, SH)
        n_sum = area.take(TT, SH)
        assert area.at <= 6144
        n_first, n_second, n_ftr, n_hps, n_hcp, n_htps, n_htcp = (sem(n) for n in (
            "nsa_projected", "nsa_copied", "blocks_ready", "hidden_ps", "hidden_copied", "hidden_t_ps", "hidden_t_copied"))
        n_cps, n_ccp, n_sps, n_xin, n_xout, n_pr, n_tps, n_tcp, n_opened, n_gin, n_gout, n_vr = (sem(n) for n in (
            "compressed_ps", "compressed_copied", "block_scores_ps", "block_exp_in", "block_exp_out", "block_weights_ready",
            "block_weights_ps", "block_weights_copied", "masks_ready", "gates_in", "gates_out", "token_values_ready"))

        def nsa_spec():
            def scores(i):
                h, br = i // 2, i % 2
                r = slice(64 * (h % 2), 64 * (h % 2) + 64)
                key = n_kt[r, br, h // (SH // SG), :]
                yield slice(0, P), n_qt[r, h // 2, 0:P], key[:, 0:P]
                yield slice(P, 3 * P), n_qt[r, h // 2, P:TOK], key

            def values(i, weights):
                h, br = i // 2, i % 2
                g = h // (SH // SG)
                r = slice(64 * (h % 2), 64 * (h % 2) + 64)
                at = (h // 2 % 4) * TOK
                d0, d1 = acc[r, h // 8, at:at + P], acc[r, h // 8, at + P:at + TOK]
                v = n_v[:, :, br * 2 * P + g * SD:br * 2 * P + (g + 1) * SD]
                if br == 0:
                    yield d0, n_vc[:, g, :], n_pct[:, h, :], True, False
                    yield d1, n_vc[:, g, :], n_pct[:, SH + h, :], False, False
                yield d0, v[:, 0, :], weights[:, 0:P], False, br == 1
                yield d1, v[:, 0, :], weights[:, P:2 * P], False, False
                yield d1, v[:, 1, :], weights[:, 2 * P:3 * P], False, br == 1
            return dict(n=2 * SH, scores=scores, values=values, blocks=[0, 1, 1], segs=[(0, P), (P, 3 * P)],
                        mask=causal[:, :], scale=SD ** -0.5,
                        gate=lambda i: n_gate[:, :, (i % 2 + 1) * SH + i // 2])

        def nsa_sync(sp, ph):
            stream_sync(sp, a["c_w_in"][0], ph.slot0, 4, 2, C_IN)
            for i, w in enumerate((a["c_w_ck1"][0], a["c_w_cv1"][0])):
                stream_sync(sp, w, ph.slot0 + 4 + i, 1, CC, HID)
            stream_sync(sp, a["c_w_o"][0], ph.slot0 + 6, 2, 4, D)

        def nsa_pool(pool, ph):
            pool.wait_ge(phase_done, ph.i)
            for dst, src in ((n_w2[:, 0, :, :], a["c_w_ck2"][0].rearrange("(c p) n -> p c n", p=P)),
                             (n_w2[:, 1, :, :], a["c_w_cv2"][0].rearrange("(c p) n -> p c n", p=P)),
                             (n_pos, a["cmp_pos_cols"]), (n_gb, a["c_gate_b"][0].partition_broadcast(P))):
                pool.dma_start(dst, src).then_inc(small, 16)
            nc.gpsimd.memset(n_open, 1.0).then_inc(n_opened, 1)
            nc.gpsimd.memset(n_shut, 0.0).then_inc(n_opened, 1)
            pool.wait_ge(n_opened, 2)
            for m, fill in ((n_open, 0.0), (n_shut, NEG)):
                nc.gpsimd.affine_select(out=m, in_=m, compare_op=ALU.is_ge, fill=fill, base=-(CL - 1),
                                        pattern=[[P, TT], [-CS, NB]], channel_multiplier=1).then_inc(n_opened, 1)
            gain_pool(pool, ph.ln, a["ln1_g"][ph.layer], a["ln1_b"][ph.layer])
            pow_pool(pool, ph.pow0, slice(32, 34))

        def nsa_tensor(pe, ph):
            input_wait(pe, ph)
            transpose_tensor(pe, X)
            pe.wait_ge(xt_ready, 2 * (ph.xt + 1))

            def w_of(k):
                return ring[:, (ph.slot0 + k // 2) % RING, 0:2 * C_IN].rearrange("p (k c) -> p k c", k=2)[:, k % 2, :]
            for k in range(KC):
                if k % 2 == 0:
                    slot_wait(pe, ph.slot0 + k // 2)
                w = w_of(k)
                end = dict(stop=(k == KC - 1), skip_group_check=True)
                for m in range(KC):
                    nc.tensor.matmul(acc[:, m // 4, (m % 4) * TOK:(m % 4 + 1) * TOK], w[:, m * P:(m + 1) * P], XT[:, k, :],
                                     start=(k == 0 and m % 2 == 0), **end)
                for i in range(2):
                    for g in range(SG):
                        c0 = SQ + (2 + 2 * i) * P + g * SD
                        for u in range(2):
                            nc.tensor.matmul(pa[u * SD:(u + 1) * SD, i, g * TOK:(g + 1) * TOK], w[:, c0:c0 + SD], XT[:, k, :],
                                             start=(k == 0 and g == 0), **end)
                for i in range(2):
                    for g in range(SG):
                        c0 = SQ + i * P + g * SD
                        for u in range(2):
                            last = nc.tensor.matmul(pb[u * SD:(u + 1) * SD, i, g * TOK:(g + 1) * TOK - u], w[:, c0:c0 + SD], XT[:, k, u:TOK],
                                                    start=(k == 0 and g == 0), **end)
            last.then_inc(n_first, 1)
            pe.wait_ge(n_second, 1)
            for k in range(KC):
                w = w_of(k)
                for t in range(TT):
                    last = nc.tensor.matmul(pa[:, t, 0:VW], XT[:, k, t * P:(t + 1) * P], w[:, C_IN - VW:C_IN], start=(k == 0), stop=(k == KC - 1))
                if k % 2:
                    last.then_inc(freed, 1)
            pe.wait_ge(n_ftr, 1)
            for i in range(2):
                slot_wait(pe, ph.slot0 + 4 + i)
                w = ring[:, (ph.slot0 + 4 + i) % RING, :].rearrange("p (c n) -> p c n", c=CC)
                for c in range(CC):
                    last = nc.tensor.matmul(pb[0:SG * NB, i, 0:HID], n_ft[:, i, c, :], w[:, c, :], start=(c == 0), stop=(c == CC - 1))
                last.then_inc(freed, 1)
            pe.wait_ge(n_hcp, 1)
            for i in range(2):
                for c in range(2):
                    last = nc.tensor.transpose(pb[:, 0, (2 * i + c) * 32:(2 * i + c) * 32 + SG * NB], n_hid[0:SG * NB, i, c * P:(c + 1) * P],
                                               ident[0:SG * NB, 0:SG * NB])
            last.then_inc(n_htps, 1)
            pe.wait_ge(n_htcp, 1)
            pe.wait_ge(small, ph.small)
            for u in range(2):
                for c in range(2):
                    nc.tensor.matmul(pb[u * SD:(u + 1) * SD, 1, 0:SG * NB], n_w2[:, 0, c, :], n_hidt[:, 0, c, :], start=(c == 0), stop=(c == 1))
            for g in range(SG):
                for c in range(2):
                    last = nc.tensor.matmul(pb[0:NB, 1, (g + 1) * SD:(g + 2) * SD], n_hidt[:, 1, c, g * NB:(g + 1) * NB], n_w2[:, 1, c, :],
                                            start=(c == 0), stop=(c == 1))
            last.then_inc(n_cps, 1)
            pe.wait_ge(n_ccp, 2)
            pe.wait_ge(n_vr, 1)
            for t in range(TT):
                for h in range(SH):
                    r = slice(64 * (h % 2), 64 * (h % 2) + 64)
                    g = h // (SH // SG)
                    last = nc.tensor.matmul(pa[:, h % 2, (t * SH + h) // 2 * NB:((t * SH + h) // 2 + 1) * NB], n_qt[r, h // 2, t * P:(t + 1) * P],
                                            n_kc[r, g * NB:(g + 1) * NB], start=True, stop=True)
            last.then_inc(n_sps, 1)
            pe.wait_ge(n_pr, 1)
            for t in range(TT):
                if t:
                    pe.wait_ge(n_tcp, 2)
                for h in range(SH):
                    last = nc.tensor.transpose(acc[0:NB, h // 8, (h % 8) * P:(h % 8 + 1) * P], n_e[:, t, h, :], ident[:, :])
                last.then_inc(n_tps, 1)
            pe.wait_ge(n_tcp, 4)
            att_tensor(pe, ph.att0, nsa_spec())
            out_tensor(pe, ph, ph.slot0 + 6)

        def nsa_scalar(act, ph):
            transpose_scalar(act, ph.xt, XT)
            act.wait_ge(n_first, 1)
            for i in range(TT):
                last = nc.scalar.copy(n_qt[:, 4 * i:4 * i + 4, :], acc[:, i, :].rearrange("p (k c) -> p k c", c=TOK))
            last.then_inc(n_ccp, 1)
            act.wait_ge(n_gin, 1)
            nc.scalar.activation(n_gate, n_gate, ACT.Sigmoid).then_inc(n_gout, 1)
            act.wait_ge(freed, ph.slot0 + 6)
            nc.scalar.activation(n_hid[0:SG * NB, :, :], pb[0:SG * NB, :, 0:HID], ACT.Gelu_apprx_tanh).then_inc(n_hcp, 1)
            act.wait_ge(n_xin, 1)
            nc.scalar.activation(n_e, n_e, ACT.Exp).then_inc(n_xout, 1)
            for t in range(TT):
                act.wait_ge(n_tps, t + 1)
                nc.scalar.copy(n_pct[:, t * SH:t * SH + 8, :], acc[0:NB, 0, :].rearrange("p (h c) -> p h c", c=P)).then_inc(n_tcp, 1)
            att_scalar(act, ph.att0, nsa_spec())
            heads_scalar(act, ph)

        def nsa_vector(dve, ph, link):
            v = nc.vector
            transpose_vector(dve, ph.xt, XT)
            dve.wait_ge(n_first, 1)
            v.tensor_copy(n_kt, pa[:, :, :].rearrange("p i (g c) -> p i g c", g=SG)).then_inc(n_second, 1)
            dve.wait_ge(small, ph.small)
            for i in range(2):
                for g in range(SG):
                    seen = pb[:, i, g * TOK:(g + 1) * TOK]
                    src = bass.AP(seen.tensor, seen.offset, [list(seen.ap[0]), [2, CC], [CS, NB]])
                    last = v.tensor_tensor(n_ft[:, i, :, g * NB:(g + 1) * NB], src, bc(n_pos[:, i * CC:(i + 1) * CC].unsqueeze(2), [P, CC, NB]), ALU.add)
            last.then_inc(n_ftr, 1)
            dve.wait_ge(freed, ph.slot0 + 4)
            for t in range(TT):
                last = v.tensor_copy(n_v[:, t, :], pa[:, t, 0:VW])
            last.then_inc(n_vr, 1)
            dve.wait_ge(n_vr, 1)
            v.tensor_tensor(n_gate, n_v[:, :, 3 * P:VW], bc(n_gb.unsqueeze(1), [P, TT, 3 * SH]), ALU.add).then_inc(n_gin, 1)
            dve.wait_ge(n_htps, 1)
            v.tensor_copy(n_hidt, pb[:, 0, 0:128].rearrange("p (i c n) -> p i c n", i=2, c=2)[:, :, :, 0:SG * NB]).then_inc(n_htcp, 1)
            dve.wait_ge(n_cps, 1)
            v.tensor_copy(n_vc, pb[0:NB, 1, SD:3 * SD].rearrange("p (g e) -> p g e", g=SG))
            v.tensor_copy(n_kc, pb[:, 1, 0:SG * NB]).then_inc(n_ccp, 1)
            dve.wait_ge(n_sps, 1)
            dve.wait_ge(n_opened, 4)
            for t in range(TT):
                for u in range(2):
                    half_n = SH // 2 * NB
                    last = v.scalar_tensor_tensor(n_e[:, t, u::2, :], pa[:, u, t * half_n:(t + 1) * half_n].rearrange("p (h n) -> p h n", n=NB),
                                                  SD ** -0.5, bc(n_shut[:, t, :].unsqueeze(1), [P, SH // 2, NB]), ALU.mult, ALU.add)
            link(last)
            link(v.tensor_reduce(n_max, n_e, AX.X, ALU.max))
            v.tensor_tensor(n_e, n_e, bc(n_max.unsqueeze(3), [P, TT, SH, NB]), ALU.subtract).then_inc(n_xin, 1)
            dve.wait_ge(n_xout, 1)
            link(v.tensor_reduce(n_sum, n_e, AX.X, ALU.add))
            dve.wait_ge(n_gout, 1)
            link(v.reciprocal(n_sum, n_sum))
            link(v.tensor_tensor(n_sum, n_gate[:, :, 0:SH], n_sum, ALU.mult))
            link(v.tensor_tensor(n_e, n_e, bc(n_sum.unsqueeze(3), [P, TT, SH, NB]), ALU.mult))
            link(v.tensor_tensor(n_e, n_e, bc(n_open.unsqueeze(2), [P, TT, SH, NB]), ALU.mult))
            dve.sem_inc(n_pr, 1)
            for t in range(TT):
                dve.wait_ge(n_tps, t + 1)
                v.tensor_copy(n_pct[:, t * SH + 8:(t + 1) * SH, :], acc[0:NB, 1, :].rearrange("p (h c) -> p h c", c=P)).then_inc(n_tcp, 1)
            att_vector(dve, ph.att0, nsa_spec())
            heads_vector(dve, ph)
            dve.wait_ge(freed, ph.slot0 + 8)
            ln_vector(dve, ph, link)

        block = ctx.enter_context(nc.Block())
        last_ph = plan[-1]
        final = last_ph.kind not in ("ab", "nsa") and last_ph.fn != FN1

        @block.sync
        def _(sp):
            if plan[0].kind == "moe":
                for s in full:
                    sp.sem_inc(s, FILL)
            sp.dma_start(X[:, :, :], a["x"].rearrange("(t p) d -> p t d", p=P)).then_inc(x_loaded, 16)
            for ph in plan:
                dict(ab=ab_sync, nsa=nsa_sync, mod=mod_sync, gqa=gqa_sync, fourier=fourier_sync, moe=moe_sync)[ph.kind](sp, ph)
            sp.wait_ge(phase_done, len(plan) + final)
            sp.dma_start(out.rearrange("(t p) d -> p t d", p=P), X[:, :, :]).then_inc(out_done, 16)
            sp.wait_ge(out_done, 16)

        @block.gpsimd
        def _(pool):
            tables_pool(pool, Link(pool, poo))
            for ph in plan:
                if ph.kind == "moe":
                    router_pool(pool, ph)
                    if ph.fn == FN1:
                        gain_pool(pool, ph.ln, a["ln2_g"][ph.layer], a["ln2_b"][ph.layer])
                    else:
                        gain_pool(pool, ph.ln, a["norm_ffn_2"][ph.layer])
                    pow_pool(pool, ph.pow0, slice(32, 34))
                else:
                    dict(ab=ab_pool, nsa=nsa_pool, mod=mod_pool, gqa=gqa_pool, fourier=fourier_pool)[ph.kind](pool, ph)
            if final:
                gain_pool(pool, last_ph.ln + 1, a["final_norm_2"])
                pow_pool(pool, last_ph.pow0 + last_ph.npow, slice(32, 34))

        @block.tensor
        def _(pe):
            if plan[0].kind == "moe":
                pe.sem_inc(freed, RING)
            pe.sem_inc(xfreed, CREDIT)
            for r in R:
                for s in r.values():
                    pe.sem_inc(s, START)
            for ph in plan:
                if ph.kind == "moe":
                    input_wait(pe, ph)
                    transpose_tensor(pe, source(ph))
                    moe_tensor(pe, ph)
                else:
                    dict(ab=ab_tensor, nsa=nsa_tensor, mod=mod_tensor, gqa=gqa_tensor, fourier=fourier_tensor)[ph.kind](pe, ph)

        @block.scalar
        def _(act):
            for ph in plan:
                if ph.kind == "moe":
                    transpose_scalar(act, ph.xt, XT)
                    router_scalar(act, ph)
                    moe_other(act, ph, lambda r, t, g, up, every: round_scalar(act, ph, r, t, up, every))
                else:
                    dict(ab=ab_scalar, nsa=nsa_scalar, mod=mod_scalar, gqa=gqa_scalar, fourier=fourier_scalar)[ph.kind](act, ph)

        @block.vector
        def _(dve):
            link = Link(dve, vec)
            dve.wait_ge(x_loaded, 16)
            dve.wait_ge(consts, CONSTS)
            for ph in plan:
                if ph.kind == "moe":
                    if ph.fn == FN2:
                        norm_vector(dve, ph, link, 3)
                    transpose_vector(dve, ph.xt, XT)
                    router_vector(dve, ph, link)
                    moe_other(dve, ph, lambda r, t, g, up, every: round_vector(dve, ph, r, t, g, every), last=True)
                    if ph.fn == FN1:
                        ln_vector(dve, ph, link)
                    else:
                        gated_vector(dve, link, 5)
                else:
                    dict(ab=ab_vector, nsa=nsa_vector, mod=mod_vector, gqa=gqa_vector, fourier=fourier_vector)[ph.kind](dve, ph, link)
                dve.sem_inc(phase_done, 1)
            if final:
                squares(link, X, HM, 32, D)
                dve.sem_inc(var_ready, 1)
                dve.wait_ge(ln_loaded, 32 * (last_ph.ln + 2))
                dve.wait_ge(rstd_ready, last_ph.pow0 + last_ph.npow + 1)
                for t in range(TT):
                    link(nc.vector.scalar_tensor_tensor(X[:, t, :], X[:, t, :], stat[:, 32 + t:33 + t], gain[:, :], ALU.mult, ALU.mult))
                dve.sem_inc(phase_done, 1)


def make_plan(kinds):
    plan = []
    slot = RING if kinds[0][0] == "moe" else 0
    moe = xt = h = ln = pow_ = small = att = mix = 0
    for i, (kind, layer, fn) in enumerate(kinds):
        ph = Phase(kind, layer, fn)
        ph.i = i
        block1 = kind in ("ab", "nsa") or fn == FN1
        if not block1 and kind != "mod":
            h += 1
        ph.slot0, ph.moe, ph.xt, ph.h, ph.ln, ph.pow0, ph.att0, ph.mix = slot, moe, xt, h, ln, pow_, att, mix
        ph.npow = {"ab": 2, "nsa": 1, "moe": 1, "gqa": 2, "fourier": 1, "mod": 0}[kind]
        ph.natt = {"ab": 8, "nsa": 32, "gqa": 32}.get(kind, 0)
        small += 16 * {"ab": 9, "nsa": 4, "moe": 0, "gqa": 4, "fourier": 1, "mod": 2}[kind]
        ph.small = small
        slot += ph.slots()
        moe += kind == "moe"
        xt += {"mod": 0, "fourier": 0, "gqa": 2}.get(kind, 1)
        pow_ += ph.npow
        att += ph.natt
        mix += kind in ("ab", "nsa", "gqa", "fourier")
        ph.res = ln + (kind == "ab")
        ln += {"mod": 0, "ab": 2}.get(kind, 1)
        h += block1
        plan.append(ph)
    return plan


def axis_tables():
    n = 16
    inv = np.float32(10000.0) ** (-np.arange(n, dtype=np.float32) / np.float32(n))
    tok = np.arange(TOK)
    ang = np.stack([(tok // 64).astype(np.float32)[:, None] * inv, (tok % 64).astype(np.float32)[:, None] * inv], 1)
    return np.stack([np.cos(ang), np.sin(ang)], 1).reshape(TOK, 4 * n).astype(np.float32)


def dft_tables():
    i = np.arange(TOK)
    ang = 2 * np.pi * (np.outer(i, i) % TOK) / TOK
    c, s = np.cos(ang) / 16, np.sin(ang) / 16
    return np.concatenate([c, s, c, -s], 1).astype(np.float32)


def by_feature(c, c_ctx):
    return np.ascontiguousarray(np.stack([c.reshape(KC, P), c_ctx.reshape(KC, P)]).transpose(2, 0, 1).reshape(P, 2 * KC))


def latent_freqs():
    return np.exp(np.float32(-np.log(10000.0)) * np.arange(16, dtype=np.float32) / np.float32(16)).astype(np.float32)[None]


def position_columns(cmp_pos):
    return np.ascontiguousarray(cmp_pos.reshape(2, 16, P).transpose(2, 0, 1).reshape(P, 32))


KINDS = [("ab", 0, 0), ("moe", 0, FN1), ("nsa", 1, 0), ("moe", 1, FN1),
         ("mod", 0, 0), ("gqa", 0, 0), ("moe", 0, FN2), ("mod", 1, 0), ("fourier", 1, 0), ("moe", 1, FN2)]
AS_THEY_ARE = """ab_w_in ab_gm_ln_g ab_gm_ln_b ab_gm_ws ab_gm_bs ab_mla_q_norm ab_mla_kv_norm ab_mla_w_uq ab_mla_w_uk
ab_mla_w_uv ab_w_o c_w_in c_w_ck1 c_w_ck2 c_w_cv1 c_w_cv2 c_gate_b c_w_o moe_w_rg moe_b_rg moe_w_re moe_b_re
moe_w_gate moe_w_up moe_w_down ln1_g ln1_b ln2_g ln2_b ctx_2 w_mod_2 b_mod_2 norm_mix_2 norm_ffn_2 attn_w_qkv_2
attn_q_norm_2 attn_k_norm_2 attn_w_o_2 fourier_w_o_2 moe_w_rg_2 moe_b_rg_2 moe_w_re_2 moe_b_re_2 moe_w1_2 moe_w3_2
moe_w2_2 final_norm_2""".split()


def kernel(**inputs):
    import concourse.bacc as bacc
    from concourse.bass_utils import run_bass_kernel_spmd

    nc = bacc.Bacc("TRN2", target_bir_lowering=False, num_devices=1)
    given = {n: np.ascontiguousarray(inputs[n]) for n in AS_THEY_ARE}
    given["x"] = np.ascontiguousarray(inputs["x"]).reshape(TOK, D)
    given["pos_cols"] = np.ascontiguousarray(np.asarray(inputs["positions"]).reshape(TT, P).T)
    given["cond"] = by_feature(np.asarray(inputs["c_2"]), np.asarray(inputs["c_ctx_2"]))
    given["cmp_pos_cols"] = position_columns(np.asarray(inputs["c_cmp_pos"]))
    given["freqs"] = latent_freqs()
    given["rope_axes"] = axis_tables()
    given["dft"] = dft_tables()
    a = {n: nc.dram_tensor(f"in_{n}", v.shape, mybir.dt.from_np(v.dtype), kind="ExternalInput").ap() for n, v in given.items()}
    out = nc.dram_tensor("out", (TOK, D), F32, kind="ExternalOutput").ap()
    build_model(nc, a, out, make_plan(KINDS))
    r = run_bass_kernel_spmd(nc, [{f"in_{n}": v for n, v in given.items()}], core_ids=[0])
    return r.results[0]["out"].reshape(1, TOK, D)
```

```python
from contextlib import ExitStack

import numpy as np

import concourse.bass as bass
from concourse import mybir

F32 = mybir.dt.float32
I32 = mybir.dt.int32
ALU = mybir.AluOpType
ACT = mybir.ActivationFunctionType
AX = mybir.AxisListType

P = 128
D = 1024
TOK = 256
TT = TOK // P
KC = D // P
NEG = -1e30

RING = 6
SLOT = 4096
FILL = 32

NG, EPG = 4, 8
NE = NG * EPG
CAP = 32
SIDE = P // CAP
ROUNDS = NE // SIDE
MAXPASS = TOK // CAP
START = 1
UNITS = 12
CREDIT = 4
XSLOTS = 2


FN1, FN2 = D // 4, D // 2
ALPHA = (2.0 * 2) ** 0.25
LN_EPS, RMS_EPS = 1e-5, 1e-6
CONSTS = 9


class Phase:

    def __init__(self, kind, layer, fn=0):
        self.kind, self.layer, self.fn = kind, layer, fn
        self.slot0 = 0
        self.moe = 0
        self.xt = 0
        self.h = 0
        self.ln = 0
        self.rms = 0

    def slots(self):
        if self.kind == "moe":
            return ROUNDS * moe_slots(self.fn)
        return {"ab": 6, "nsa": 20, "mod": 0, "gqa": 18, "fourier": 2}[self.kind]


def moe_slots(fn):
    return (2 * D * fn * SIDE + fn * D * SIDE) // (P * SLOT)




def build_model(nc, a, out, plan):
    with ExitStack() as ctx:
        def sb(name, shape, dt=F32):
            return ctx.enter_context(nc.sbuf_tensor(name, shape, dt))

        def sem(name):
            return ctx.enter_context(nc.semaphore(name))

        ring = sb("ring", [P, RING, SLOT])
        X = sb("X", [P, TT, D])
        XT = sb("XT", [P, KC, TOK])
        HM = sb("HM", [P, TT, D])
        gain = sb("gain", [P, D])
        shift = sb("shift", [P, D])
        mod = sb("mod", [P, 6 * D])
        mod_rows = sb("mod_rows", [P, 512])
        select = sb("select", [P, 16])
        work = sb("work", [P, 11300])
        wr = sb("wr", [P, KC, 4 + NE])
        br = sb("br", [P, 4 + NE])
        ident = sb("ident", [P, P])
        ones = sb("ones", [P, P])
        zeros = sb("zeros", [P, P])
        before = sb("before", [P, P])
        causal = sb("causal", [P, P])
        iota = sb("iota", [P, CAP])
        iota_i = sb("iota_i", [P, CAP], I32)
        thresh = sb("thresh", [P, MAXPASS - 1])
        stat = sb("stat", [P, 64])
        half = sb("half", [P, 64])
        extra_f = sb("extra_f", [P, 4])
        extra_i = sb("extra_i", [1, 4, 2], I32)

        acc = ctx.enter_context(nc.psum_tensor("acc", [P, TT, D], F32))
        pa = ctx.enter_context(nc.psum_tensor("pa", [P, 2, 512], F32))
        pb = ctx.enter_context(nc.psum_tensor("pb", [P, 2, 512], F32))

        x_loaded = sem("x_loaded")
        select_loaded = sem("select_loaded")
        consts = sem("consts")
        full = [sem(f"slot{i}_full") for i in range(RING)]
        freed = sem("slot_freed")
        h_ready = sem("h_ready")
        xt_ps = sem("xt_ps")
        xt_ready = sem("xt_ready")
        vec = sem("vec_step")
        sca = sem("sca_step")
        poo = sem("pool_step")
        ln_loaded = sem("ln_loaded")
        ln_used = sem("ln_used")
        var_ready = sem("var_ready")
        rstd_ready = sem("rstd_ready")
        mix_done = sem("mix_done")
        small = sem("small_loaded")
        out_done = sem("out_done")
        phase_done = sem("phase_done")
        S = {}

        def sg(name):
            if name not in S:
                S[name] = sem(name)
            return S[name]

        class Link:

            def __init__(self, eng, s):
                self.eng, self.s, self.n = eng, s, 0

            def __call__(self, ins):
                self.n += 1
                ins.then_inc(self.s, 1)
                self.eng.wait_ge(self.s, self.n)

        def slot_wait(eng, q):
            eng.wait_ge(full[q % RING], FILL * (q // RING + 1))

        def slot_fill(sp, q, parts):
            if q >= RING:
                sp.wait_ge(freed, q - RING + 1)
            for dst, src in parts:
                sp.dma_start(dst, src).then_inc(full[q % RING], 16)

        def bc(v, shape):
            return v.to_broadcast(shape)

        class Area:

            def __init__(self, t):
                self.t, self.at = t, 0

            def take(self, *shape, rows=P):
                n = 1
                for s in shape:
                    n *= s
                v = self.t[0:rows, self.at:self.at + n]
                self.at += n
                assert self.at <= self.t.shape[1], (self.at, self.t.shape)
                if len(shape) == 1:
                    return v
                names = " ".join(f"d{i}" for i in range(len(shape)))
                return v.rearrange(f"p ({names}) -> p {names}", **{f"d{i}": s for i, s in enumerate(shape) if i})

        def source(ph):
            return X if ph.kind in ("ab", "nsa") or (ph.kind == "moe" and ph.fn == FN1) else HM

        def by_chunk(v):
            return v[:, :, :].rearrange("p a (k c) -> p (a k) c", c=P)

        def input_wait(eng, ph):
            if ph.h == 0:
                eng.wait_ge(x_loaded, 16)
                eng.wait_ge(consts, CONSTS)
            else:
                eng.wait_ge(h_ready, ph.h)

        def transpose_tensor(pe, src):
            for t in range(TT):
                dst = by_chunk((pa, pb)[t])
                for k in range(KC):
                    last = nc.tensor.transpose(dst[:, k, :], src[:, t, k * P:(k + 1) * P], ident[:, :])
                last.then_inc(xt_ps, 1)

        def transpose_scalar(act, n, dst):
            act.wait_ge(xt_ps, 2 * n + 1)
            nc.scalar.copy(dst[:, :, 0:P], by_chunk(pa)).then_inc(xt_ready, 1)

        def transpose_vector(dve, n, dst):
            dve.wait_ge(xt_ps, 2 * n + 2)
            nc.vector.tensor_copy(dst[:, :, P:TOK], by_chunk(pb)).then_inc(xt_ready, 1)

        def gain_pool(pool, n, g, b=None):
            if n:
                pool.wait_ge(ln_used, n)
            if b is None:
                pool.dma_start(gain[:, :], g.partition_broadcast(P)).then_inc(ln_loaded, 32)
                return
            pool.dma_start(gain[:, :], g.partition_broadcast(P)).then_inc(ln_loaded, 16)
            pool.dma_start(shift[:, :], b.partition_broadcast(P)).then_inc(ln_loaded, 16)

        def pow_pool(pool, n, cols):
            pool.wait_ge(var_ready, n + 1)
            nc.gpsimd.tensor_tensor(stat[:, cols], stat[:, cols], half[:, 0:cols.stop - cols.start],
                                    ALU.pow).then_inc(rstd_ready, 1)

        def ln_vector(dve, ph, link):
            for t in range(TT):
                link(nc.vector.scalar_tensor_tensor(X[:, t, :], X[:, t, :], ALPHA, acc[:, t, :], ALU.mult, ALU.add))
            st = stat[:, 0:24].rearrange("p (t h s) -> p t h s", t=TT, h=2)
            for t in range(TT):
                for h in range(2):
                    last = nc.vector.bn_stats(st[:, t, h, :], X[:, t, h * 512:(h + 1) * 512])
            link(last)
            mv = stat[:, 24:28].rearrange("p (t s) -> p t s", s=2)
            for t in range(TT):
                last = nc.vector.bn_aggr(mv[:, t, :], st[:, t, :, :].rearrange("p h s -> p (h s)"))
            link(last)
            nc.vector.tensor_scalar(stat[:, 32:34], mv[:, :, 1], LN_EPS, None, ALU.add).then_inc(var_ready, 1)
            dve.wait_ge(rstd_ready, ph.pow0 + ph.npow)
            for t in range(TT):
                last = nc.vector.tensor_scalar(X[:, t, :], X[:, t, :], mv[:, t, 0:1], stat[:, 32 + t:33 + t],
                                               ALU.subtract, ALU.mult)
            link(last)
            dve.wait_ge(ln_loaded, 32 * (ph.res + 1))
            link(nc.vector.tensor_tensor(X[:, :, :], X[:, :, :], bc(gain[:, :].unsqueeze(1), [P, TT, D]), ALU.mult))
            link(nc.vector.tensor_tensor(X[:, :, :], X[:, :, :], bc(shift[:, :].unsqueeze(1), [P, TT, D]), ALU.add))
            dve.sem_inc(ln_used, 1)
            dve.sem_inc(h_ready, 1)

        def squares(link, x, junk, col, n):
            for t in range(TT):
                link(nc.vector.tensor_tensor_reduce(out=junk[:, t, :], in0=x[:, t, :], in1=x[:, t, :], scale=1.0 / n, scalar=0.0,
                                                    op0=ALU.mult, op1=ALU.add, accum_out=stat[:, col + t:col + t + 1]))
            link(nc.vector.tensor_scalar(stat[:, col:col + TT], stat[:, col:col + TT], RMS_EPS, None, ALU.add))

        def modulate(link, x, dst, col, scale1, sh):
            for t in range(TT):
                link(nc.vector.scalar_tensor_tensor(dst[:, t, :], x[:, t, :], stat[:, col + t:col + t + 1], scale1, ALU.mult, ALU.mult))
            link(nc.vector.tensor_tensor(dst[:, :, :], dst[:, :, :], bc(sh.unsqueeze(1), [P, TT, D]), ALU.add))

        def mod_of(i):
            return mod[:, i * D:(i + 1) * D]

        def norm_vector(dve, ph, link, which):
            squares(link, X, HM, 32, D)
            dve.sem_inc(var_ready, 1)
            dve.wait_ge(ln_loaded, 32 * (ph.ln + 1))
            link(nc.vector.scalar_tensor_tensor(shift[:, :], mod_of(which + 1), 1.0, gain[:, :], ALU.add, ALU.mult))
            dve.wait_ge(rstd_ready, ph.pow0 + 1)
            modulate(link, X, HM, 32, shift[:, :], mod_of(which))
            dve.sem_inc(h_ready, 1)
            dve.sem_inc(ln_used, 1)

        def gated_vector(dve, link, which):
            link(nc.vector.tensor_tensor(HM[:, :, :], acc[:, :, :], bc(mod_of(which).unsqueeze(1), [P, TT, D]), ALU.mult))
            link(nc.vector.tensor_tensor(X[:, :, :], X[:, :, :], HM[:, :, :], ALU.add))

        area = Area(work)
        m_xg = XT[:, :, 0:P]
        m_p = area.take(TT, P)
        m_pw = area.take(TT, P)
        m_pwt = area.take(TOK)
        m_silu = area.take(512)
        m_hh = area.take(512)
        m_ht = area.take(4, P)
        m_yg = XT[:, :, P:TOK]
        m_log = area.take(TT, 4 + NE)
        m_rank = area.take(TT, NE)
        m_w = area.take(TT, NE)
        m_a = area.take(TT, NE)
        m_t = [area.take(TT, NE) for _ in range(4)]
        m_g = [area.take(TT, NG) for _ in range(3)]
        m_s = area.take(16, TT)
        xring = area.take(XSLOTS, SLOT)

        R = [{n: sem(f"{n}{k}") for n in (
            "p_ready", "pw_ready", "rank_next", "gathered", "xg_copied", "pwt_ps", "pwt_copied", "silu_done", "hh_ready", "ht_ps", "ht_copied", "y_copied", "added")} for k in ("", "_x")]
        xfull = [sem(f"xslot{i}_full") for i in range(XSLOTS)]
        xfreed = sem("xslot_freed")
        logits_done, ranks_done = sem("logits_done"), sem("ranks_done")
        assign_ready, extra_ready = sem("assign_ready"), sem("extra_ready")
        rexp_in, rexp_out = sem("router_exp_in"), sem("router_exp_out")
        wr_loaded = sem("router_loaded")

        def moe_names(ph):
            if ph.fn == FN1:
                return a["moe_w_gate"][ph.layer], a["moe_w_up"][ph.layer], a["moe_w_down"][ph.layer]
            return a["moe_w1_2"][ph.layer], a["moe_w3_2"][ph.layer], a["moe_w2_2"][ph.layer]

        def router_pool(pool, ph):
            s = "" if ph.fn == FN1 else "_2"
            if ph.moe:
                pool.wait_ge(assign_ready, ph.moe)
            for lo, hi, n in ((0, NG, "g"), (NG, NG + NE, "e")):
                pool.dma_start(wr[:, :, lo:hi], a[f"moe_w_r{n}{s}"][ph.layer].rearrange("(k p) n -> p k n", p=P)).then_inc(wr_loaded, 16)
                pool.dma_start(br[:, lo:hi], a[f"moe_b_r{n}{s}"][ph.layer].partition_broadcast(P)).then_inc(wr_loaded, 16)

        def router_tensor(pe, ph):
            pe.wait_ge(xt_ready, 2 * (ph.xt + 1))
            pe.wait_ge(wr_loaded, 64 * (ph.moe + 1))
            for t in range(TT):
                for k in range(KC):
                    last = nc.tensor.matmul(pa[:, t, 0:NG + NE], XT[:, k, t * P:(t + 1) * P], wr[:, k, :],
                                            start=(k == 0), stop=(k == KC - 1))
            last.then_inc(logits_done, 1)
            for t in range(TT):
                for h in range(2):
                    nc.tensor.matmul(acc[:, t, h * 512:(h + 1) * 512], zeros[:, :], source(ph)[:, t, h * 512:(h + 1) * 512],
                                     start=True, stop=True)
            pe.wait_ge(assign_ready, ph.moe + 1)
            nc.tensor.matmul(pb[:, 0, 0:NE], before[:, :], m_a[:, 0, :], start=True, stop=True)
            nc.tensor.matmul(pb[:, 0, NE:2 * NE], before[:, :], m_a[:, 1, :], start=True, stop=False)
            nc.tensor.matmul(pb[:, 0, NE:2 * NE], ones[:, :], m_a[:, 0, :], start=False, stop=True)
            nc.tensor.matmul(pb[:, 1, 0:NE], ones[:, :], m_a[:, 0, :], start=True, stop=False)
            nc.tensor.matmul(pb[:, 1, 0:NE], ones[:, :], m_a[:, 1, :], start=False, stop=True).then_inc(ranks_done, 1)

        def router_scalar(act, ph):
            n = 2 * ph.moe
            act.wait_ge(rexp_in, n + 1)
            nc.scalar.activation(m_g[1], m_g[1], ACT.Exp).then_inc(rexp_out, 1)
            act.wait_ge(rexp_in, n + 2)
            nc.scalar.activation(m_s[:, 4, :], m_s[:, 4, :], ACT.Exp).then_inc(rexp_out, 1)

        def router_vector(dve, ph, link):
            v = nc.vector

            def first_of(out_, x, m, iv, tmp, n):
                link(v.tensor_tensor(tmp, x, bc(m.unsqueeze(2), [P, TT, n]), ALU.is_equal))
                link(v.scalar_tensor_tensor(tmp, tmp, -64.0, bc(iv.unsqueeze(1), [P, TT, n]), ALU.mult, ALU.add))
                link(v.tensor_reduce(m_s[:, 15, :], tmp, AX.X, ALU.min))
                link(v.tensor_tensor(out_, tmp, bc(m_s[:, 15, :].unsqueeze(2), [P, TT, n]), ALU.is_equal))

            dve.wait_ge(logits_done, ph.moe + 1)
            link(v.tensor_tensor(m_log, pa[:, :, 0:NG + NE], bc(br[:, :].unsqueeze(1), [P, TT, NG + NE]), ALU.add))
            lg, le = m_log[:, :, 0:NG], m_log[:, :, NG:]
            gmax, l1, l2, gw, w1, w2 = (m_s[:, i, :] for i in range(6))
            l1, l2, gw, w1, w2 = (m_s[:, i, :] for i in (1, 2, 3, 5, 6))
            dif = m_s[:, 4, :]
            link(v.tensor_reduce(gmax, lg, AX.X, ALU.max))
            first_of(m_g[0], lg, gmax, iota[:, 0:NG], m_g[2], NG)
            v.tensor_tensor(m_g[1], lg, bc(gmax.unsqueeze(2), [P, TT, NG]), ALU.subtract).then_inc(rexp_in, 1)
            link(v.tensor_scalar(m_g[2], m_g[0], 1.0, -NEG, ALU.subtract, ALU.mult))
            lm, o1, o2, tmp = m_t
            link(v.tensor_tensor(lm.rearrange("p t (g e) -> p t g e", g=NG), le.rearrange("p t (g e) -> p t g e", g=NG),
                                 bc(m_g[2].unsqueeze(3), [P, TT, NG, EPG]), ALU.add))
            link(v.tensor_reduce(l1, lm, AX.X, ALU.max))
            first_of(o1, lm, l1, iota[:, 0:NE], tmp, NE)
            link(v.scalar_tensor_tensor(lm, o1, 3 * NEG, lm, ALU.mult, ALU.add))
            link(v.tensor_reduce(l2, lm, AX.X, ALU.max))
            first_of(o2, lm, l2, iota[:, 0:NE], tmp, NE)
            v.tensor_tensor(dif, l2, l1, ALU.subtract).then_inc(rexp_in, 1)
            v.tensor_tensor(m_a, o1, o2, ALU.add).then_inc(assign_ready, 1)
            dve.wait_ge(rexp_out, 2 * ph.moe + 2)
            link(v.tensor_reduce(gw, m_g[1], AX.X, ALU.add))
            link(v.tensor_scalar(w1, dif, 1.0, None, ALU.add))
            link(v.tensor_tensor(w1, w1, gw, ALU.mult))
            link(v.reciprocal(w1, w1))
            link(v.tensor_tensor(w2, w1, dif, ALU.mult))
            link(v.tensor_tensor(o1, o1, bc(w1.unsqueeze(2), [P, TT, NE]), ALU.mult))
            link(v.tensor_tensor(o2, o2, bc(w2.unsqueeze(2), [P, TT, NE]), ALU.mult))
            link(v.tensor_tensor(m_w, o1, o2, ALU.add))
            dve.wait_ge(ranks_done, ph.moe + 1)
            link(v.scalar_tensor_tensor(m_rank, pb[:, 0, 0:2 * NE].rearrange("p (t e) -> p t e", t=TT), 1.0, m_a,
                                        ALU.add, ALU.mult))
            link(v.tensor_scalar(m_rank, m_rank, 1.0, None, ALU.subtract))
            link(v.tensor_reduce(extra_f[:, 2:3], pb[:, 1, 0:NE], AX.X, ALU.max))
            link(v.tensor_scalar(m_s[:, 8:12, :].rearrange("p a b -> p (a b)")[:, 0:MAXPASS - 1], thresh[:, :], extra_f[:, 2:3], None, ALU.is_lt))
            link(v.tensor_reduce(extra_f[:, 0:1], m_s[:, 8:12, :].rearrange("p a b -> p (a b)")[:, 0:MAXPASS - 1], AX.X, ALU.add))
            link(v.tensor_copy(extra_i[0:1, ph.moe, :], extra_f[0:1, 0:2]))
            link(v.tensor_tensor(extra_f[:, 1:2], extra_f[:, 1:2], extra_f[:, 0:1], ALU.add))
            dve.sem_inc(extra_ready, 1)

        def round_sync(sp, ph, g, wait_free, fills, slot_of, inc):
            gate, up, down = moe_names(ph)
            ex = bass.ds(g * SIDE, SIDE)
            n = moe_slots(ph.fn)
            n_down = ph.fn // P
            rows = SLOT // (2 * SIDE * ph.fn)
            for i in range(n):
                dst = slot_of(i)
                wait_free(i)
                if i < n - n_down:
                    for m, w in enumerate((gate, up)):
                        src = w[ex].rearrange("j (c p r) f -> c p j (r f)", p=P, r=rows)[i]
                        sp.dma_start(dst[:, m * SLOT // 2:(m + 1) * SLOT // 2].rearrange("p (j f) -> p j f", j=SIDE), src).then_inc(fills(i), inc)
                else:
                    for m in range(2):
                        c = i - (n - n_down)
                        src = down[bass.ds(g * SIDE + m * 2, 2), c * P:(c + 1) * P, :].rearrange("j p f -> p j f")
                        sp.dma_start(dst[:, m * SLOT // 2:(m + 1) * SLOT // 2].rearrange("p (j f) -> p j f", j=2), src).then_inc(fills(i), inc)

        def round_tensor(pe, ph, r, t, wait_full, free, slot_of):
            fn = ph.fn
            src = source(ph)
            rows = SLOT // (2 * SIDE * fn)
            n_down = fn // P
            n_up = moe_slots(fn) - n_down
            xg_ps = pa[:, :, :].rearrange("p a (k c) -> p (a k) c", c=P)
            hbank = (pb[:, 0, 0:fn], pb[:, 1, 0:fn])
            pe.wait_ge(r["p_ready"], t + 1 + START)
            pe.wait_ge(r["y_copied"], 2 * t + START)
            for c in range(n_up):
                for q in range(rows):
                    for tt in range(TT):
                        lhs = src[:, tt, c * P * rows:(c + 1) * P * rows].rearrange("p (f r) -> p f r", r=rows)[:, :, q]
                        last = nc.tensor.matmul(xg_ps[:, c * rows + q, :], lhs, m_p[:, tt, :], start=(tt == 0), stop=(tt == TT - 1))
            last.then_inc(r["gathered"], 1)
            pe.wait_ge(r["pw_ready"], t + 1 + START)
            pe.wait_ge(r["hh_ready"], t + START)
            for tt in range(TT):
                last = nc.tensor.transpose(pb[:, 1, tt * P:(tt + 1) * P], m_pw[:, tt, :], ident[:, :])
            last.then_inc(r["pwt_ps"], 1)
            pe.wait_ge(r["pwt_copied"], t + 1 + START)
            pe.wait_ge(r["ht_copied"], t + START)
            pe.wait_ge(r["xg_copied"], 2 * (t + 1) + START)
            for c in range(n_up):
                wait_full(c)
                slot = slot_of(c).rearrange("p (m j r f) -> p m j r f", m=2, j=SIDE, r=rows)
                for q in range(rows):
                    k = c * rows + q
                    for m in range(2):
                        for j in range(SIDE):
                            last = nc.tensor.matmul(hbank[m][j * CAP:(j + 1) * CAP, :], m_xg[:, k, j * CAP:(j + 1) * CAP],
                                                    slot[:, m, j, q, :], start=(k == 0), stop=(k == KC - 1))
                last.then_inc(*free)
            pe.wait_ge(r["hh_ready"], t + 1 + START)
            for c in range(n_down):
                last = nc.tensor.transpose(pb[:, 0, c * P:(c + 1) * P], m_hh[:, c * P:(c + 1) * P], ident[:, :])
            last.then_inc(r["ht_ps"], 1)
            pe.wait_ge(r["ht_copied"], t + 1 + START)
            for c in range(n_down):
                wait_full(n_up + c)
                slot = slot_of(n_up + c).rearrange("p (j f) -> p j f", j=SIDE)
                for h in range(2):
                    for j in range(SIDE):
                        last = nc.tensor.matmul(pa[j * CAP:(j + 1) * CAP, h, :], m_ht[:, c, j * CAP:(j + 1) * CAP],
                                                slot[:, j, h * 512:(h + 1) * 512], start=(c == 0), stop=(c == n_down - 1))
                last.then_inc(*free)
            pe.wait_ge(r["y_copied"], 2 * (t + 1) + START)
            for tt in range(TT):
                for h in range(2):
                    last = nc.tensor.matmul(acc[:, tt, h * 512:(h + 1) * 512], m_pwt[:, tt * P:(tt + 1) * P],
                                            m_yg[:, 4 * h:4 * h + 4, :], start=False, stop=True, skip_group_check=True)
            last.then_inc(r["added"], 1)

        def round_scalar(act, ph, r, t, freed_up, freed_all):
            fn = ph.fn
            act.wait_ge(r["gathered"], t + 1 + START)
            nc.scalar.copy(m_xg[:, 0:4, :], pa[:, 0, :].rearrange("p (k c) -> p k c", c=P)).then_inc(r["xg_copied"], 1)
            freed_up(act)
            nc.scalar.activation(m_silu[:, 0:fn], pb[:, 0, 0:fn], ACT.Silu).then_inc(r["silu_done"], 1)
            freed_all(act)
            nc.scalar.copy(m_yg[:, 0:4, :], pa[:, 0, :].rearrange("p (k c) -> p k c", c=P)).then_inc(r["y_copied"], 1)

        def round_vector(dve, ph, r, t, g, freed_all):
            fn = ph.fn
            v = nc.vector
            ex = bass.ds(g * SIDE, SIDE)
            shape = [P, TT, SIDE, CAP]
            dve.wait_ge(r["rank_next"], t + START)
            dve.wait_ge(r["gathered"], t + START)
            one = m_p.rearrange("p t (j s) -> p t j s", j=SIDE)
            gated = m_pw.rearrange("p t (j s) -> p t j s", j=SIDE)
            v.tensor_tensor(one, bc(iota[:, :].unsqueeze(1).unsqueeze(1), shape),
                            bc(m_rank[:, :, ex].unsqueeze(3), shape), ALU.is_equal).then_inc(r["p_ready"], 1)
            dve.wait_ge(r["p_ready"], t + 1 + START)
            dve.wait_ge(r["pwt_ps"], t + START)
            v.tensor_tensor(gated, one, bc(m_w[:, :, ex].unsqueeze(3), shape), ALU.mult).then_inc(r["pw_ready"], 1)
            v.tensor_scalar(m_rank[:, :, ex], m_rank[:, :, ex], float(CAP), None, ALU.subtract).then_inc(r["rank_next"], 1)
            dve.wait_ge(r["gathered"], t + 1 + START)
            v.tensor_copy(m_xg[:, 4:8, :], pa[:, 1, :].rearrange("p (k c) -> p k c", c=P)).then_inc(r["xg_copied"], 1)
            dve.wait_ge(r["pwt_ps"], t + 1 + START)
            v.tensor_copy(m_pwt, pb[:, 1, 0:TOK]).then_inc(r["pwt_copied"], 1)
            dve.wait_ge(r["silu_done"], t + 1 + START)
            v.tensor_tensor(m_hh[:, 0:fn], m_silu[:, 0:fn], pb[:, 1, 0:fn], ALU.mult).then_inc(r["hh_ready"], 1)
            dve.wait_ge(r["ht_ps"], t + 1 + START)
            v.tensor_copy(m_ht[:, 0:fn // P, :], pb[:, 0, 0:fn].rearrange("p (c s) -> p c s", s=P)).then_inc(r["ht_copied"], 1)
            freed_all(dve)
            v.tensor_copy(m_yg[:, 4:8, :], pa[:, 1, :].rearrange("p (k c) -> p k c", c=P)).then_inc(r["y_copied"], 1)

        def moe_sync(sp, ph):
            n = moe_slots(ph.fn)
            with sp.Fori(0, ROUNDS) as g:
                def wait_free(i):
                    sp.wait_ge(freed, ph.slot0 + g * n + i - RING + 1)
                round_sync(sp, ph, g, wait_free, lambda i: full[(ph.slot0 + i) % RING],
                           lambda i: ring[:, (ph.slot0 + i) % RING, :], 16)
            sp.wait_ge(extra_ready, ph.moe + 1)
            more = sp.value_load(extra_i[0:1, ph.moe, 0:1], min_val=0, max_val=MAXPASS - 1)
            base = sp.value_load(extra_i[0:1, ph.moe, 1:2], min_val=0, max_val=4 * (MAXPASS - 1))
            unit = UNITS // n
            with sp.If(more > 0):
                with sp.Fori(0, more) as ps:
                    with sp.Fori(0, ROUNDS) as g:
                        t = (base + ps) * ROUNDS + g

                        def wait_free(i):
                            sp.wait_ge(xfreed, t * UNITS + (CREDIT + unit * (i + 1 - XSLOTS)))
                        round_sync(sp, ph, g, wait_free, lambda i: xfull[i % XSLOTS],
                                   lambda i: xring[:, i % XSLOTS, :], 16 * unit)

        def moe_tensor(pe, ph):
            n = moe_slots(ph.fn)
            router_tensor(pe, ph)
            with pe.Fori(0, ROUNDS) as g:
                def wait_full(i):
                    q = ph.slot0 + i
                    pe.wait_ge(full[q % RING], g * (FILL * (n // RING)) + FILL * (q // RING + 1))
                round_tensor(pe, ph, R[0], g + ROUNDS * ph.moe, wait_full, (freed, 1),
                             lambda i: ring[:, (ph.slot0 + i) % RING, :])
            pe.wait_ge(extra_ready, ph.moe + 1)
            more = pe.value_load(extra_i[0:1, ph.moe, 0:1], min_val=0, max_val=MAXPASS - 1)
            base = pe.value_load(extra_i[0:1, ph.moe, 1:2], min_val=0, max_val=4 * (MAXPASS - 1))
            unit = UNITS // n
            with pe.If(more > 0):
                pe.wait_ge(R[0]["y_copied"], 2 * ROUNDS * (ph.moe + 1) + START)
                with pe.Fori(0, more) as ps:
                    with pe.Fori(0, ROUNDS) as g:
                        t = (base + ps) * ROUNDS + g

                        def wait_full(i):
                            pe.wait_ge(xfull[i % XSLOTS], t * (FILL * UNITS // XSLOTS) + 32 * unit * (i // XSLOTS + 1))
                        round_tensor(pe, ph, R[1], t, wait_full, (xfreed, unit), lambda i: xring[:, i % XSLOTS, :])

        def moe_other(eng, ph, body, last=False):
            n = moe_slots(ph.fn)
            up = n - ph.fn // P
            with eng.Fori(0, ROUNDS) as g:
                body(R[0], g + ROUNDS * ph.moe, g,
                     lambda e: e.wait_ge(freed, ph.slot0 + g * n + up),
                     lambda e: e.wait_ge(freed, ph.slot0 + g * n + n))
            if last:
                eng.wait_ge(R[0]["added"], ROUNDS * (ph.moe + 1) + START)
            eng.wait_ge(extra_ready, ph.moe + 1)
            more = eng.value_load(extra_i[0:1, ph.moe, 0:1], min_val=0, max_val=MAXPASS - 1)
            base = eng.value_load(extra_i[0:1, ph.moe, 1:2], min_val=0, max_val=4 * (MAXPASS - 1))
            unit = UNITS // n
            with eng.If(more > 0):
                eng.wait_ge(R[0]["added"], ROUNDS * (ph.moe + 1) + START)
                eng.wait_ge(R[0]["rank_next"], ROUNDS * (ph.moe + 1) + START)
                with eng.Fori(0, more) as ps:
                    with eng.Fori(0, ROUNDS) as g:
                        t = (base + ps) * ROUNDS + g
                        body(R[1], t, g,
                             lambda e: e.wait_ge(xfreed, t * UNITS + (CREDIT + unit * up)),
                             lambda e: e.wait_ge(xfreed, t * UNITS + (CREDIT + UNITS)))
            if last:
                eng.wait_ge(R[1]["added"], (base + more) * ROUNDS + START)

        def tables_pool(pool, link):
            g = nc.gpsimd
            g.memset(ones[:, :], 1.0).then_inc(consts, 1)
            g.memset(zeros[:, :], 0.0).then_inc(consts, 1)
            g.memset(half[:, :], -0.5).then_inc(consts, 1)
            g.memset(mod_rows[:, :], 0.0).then_inc(consts, 1)
            link(g.memset(ident[:, :], 0.0))
            g.affine_select(out=ident[:, :], in_=ident[:, :], compare_op=ALU.not_equal, fill=1.0, base=0,
                            pattern=[[-1, P]], channel_multiplier=1).then_inc(consts, 1)
            link(g.memset(before[:, :], 1.0))
            g.affine_select(out=before[:, :], in_=before[:, :], compare_op=ALU.is_gt, fill=0.0, base=0,
                            pattern=[[1, P]], channel_multiplier=-1).then_inc(consts, 1)
            link(g.memset(causal[:, :], 0.0))
            g.affine_select(out=causal[:, :], in_=causal[:, :], compare_op=ALU.is_ge, fill=NEG, base=0,
                            pattern=[[-1, P]], channel_multiplier=1).then_inc(consts, 1)
            link(g.iota(iota_i[:, :], pattern=[[1, CAP]], base=0, channel_multiplier=0))
            g.tensor_copy(iota[:, :], iota_i[:, :]).then_inc(consts, 1)
            link(g.tensor_copy(thresh[:, :], iota_i[:, 0:MAXPASS - 1]))
            link(g.tensor_scalar(thresh[:, :], thresh[:, :], 1.0, float(CAP), ALU.add, ALU.mult))
            g.memset(extra_f[:, :], 0.0).then_inc(consts, 1)

        MODC = 6 * D // 512
        CTXC = 2 * D // 512
        area = Area(work)
        area.at = 8208
        d_cond = area.take(KC, CAP)
        d_raw = area.take(2 * KC)
        d_sel = Area(work).take(MODC + CTXC, P)
        c_mod = work[:, 9200:9200 + 2 * D]
        d_bank = acc[:, 0, 512:D]
        cond_ready, cond_silu = sem("cond_ready"), sem("cond_silu")
        part_copied, row_ps, row_copied, sel_ready = sem("part_copied"), sem("row_ps"), sem("row_copied"), sem("selectors_ready")
        rows_moved = [sem(f"rows_moved{i}") for i in range(2)]

        def rows_count(layer, n):
            done = 0
            for l in range(layer + 1):
                for m in range(n % 2, MODC if l < layer else n + 1, 2):
                    done += 32 if l == 0 and m < CTXC else 16
            return done

        def d_part(n, early):
            return work[:, 5120 + n % 2 * 512:5632 + n % 2 * 512] if n >= early else work[:, 6144 + n % 2 * 512:6656 + n % 2 * 512]

        def w_mod_sync(sp, ph, layer):
            w = a["w_mod_2"][layer]
            for n in range(MODC):
                q = ph.slot_mod + n
                dst = ring[:, q % RING, :].rearrange("p (k c) -> p k c", k=KC)
                src = w[:, n * 512:(n + 1) * 512].rearrange("(k p) c -> p k c", p=P)
                slot_fill(sp, q, [(dst[:, 0:4, :], src[:, 0:4, :]), (dst[:, 4:8, :], src[:, 4:8, :])])

        def cond_pool(pool, layer):
            pool.dma_start(d_raw, a["cond"]).then_inc(small, 16)
            pool.dma_start(mod_rows[64:64 + MODC, :], a["b_mod_2"][layer].rearrange("(n c) -> n c", c=512)).then_inc(small, 16)

        def cond_vector(dve, layer):
            nc.vector.memset(d_cond, 0.0).then_inc(cond_ready, 1)

        def cond_scalar(act, ph, layer):
            act.wait_ge(small, ph.small)
            act.wait_ge(cond_ready, layer + 1)
            nc.scalar.activation(d_cond[:, :, 0:2], d_raw.rearrange("p (c k) -> p k c", c=2), ACT.Silu).then_inc(cond_silu, 1)

        def block_tensor(pe, ph, layer, n):
            if n == 0:
                pe.wait_ge(cond_silu, layer + 1)
            else:
                pe.wait_ge(part_copied, MODC * layer + n)
            q = ph.slot_mod + n
            slot_wait(pe, q)
            w = ring[:, q % RING, :].rearrange("p (k c) -> p k c", k=KC)
            for r in range(2):
                for j in range(SIDE):
                    k = SIDE * r + j
                    last = nc.tensor.matmul(d_bank[j * CAP:(j + 1) * CAP, :], d_cond[:, k, :], w[:, k, :], start=(r == 0), stop=(r == 1))
            last.then_inc(freed, 1)

        def block_scalar(act, ph, layer, n, early):
            act.wait_ge(freed, ph.slot_mod + n + 1)
            if n >= 2:
                act.wait_ge(rows_moved[n % 2], rows_count(layer, n - 2))
            nc.scalar.copy(d_part(n, early), d_bank).then_inc(part_copied, 1)

        def rows_pool(pool, layer, early):
            for n in range(MODC):
                pool.wait_ge(part_copied, MODC * layer + n + 1)
                part = d_part(n, early)
                pool.dma_start(mod_rows[4 * n:4 * n + 4, :], part[0:P:CAP, :]).then_inc(rows_moved[n % 2], 16)
                if layer == 0 and n < CTXC:
                    pool.dma_start(mod_rows[48 + 4 * n:52 + 4 * n, :], part[1:P:CAP, :]).then_inc(rows_moved[n % 2], 16)

        def mod_blocks(ph):
            return list(range(MODC)) + (list(range(MODC, MODC + CTXC)) if ph.layer == 0 else [])

        def mod_bank(i):
            return (pa, pb)[i // 2 % 2][:, i % 2, :]

        def mod_tensor(pe, ph):
            pe.wait_ge(phase_done, ph.i)
            pe.wait_ge(sel_ready, ph.layer + 1)
            for n in (MODC - 2, MODC - 1):
                pe.wait_ge(rows_moved[n % 2], rows_count(ph.layer, n))
            for n in mod_blocks(ph):
                if n >= 4:
                    pe.wait_ge(row_copied, ph.rows0 + n - 3)
                nc.tensor.matmul(mod_bank(n), d_sel[:, n, :], mod_rows[:, :], start=True, stop=True).then_inc(row_ps, 1)

        def mod_copy(eng, copy, ph, u):
            for n in mod_blocks(ph):
                if n % 2 == u:
                    eng.wait_ge(row_ps, ph.rows0 + n + 1)
                    if n:
                        eng.wait_ge(row_copied, ph.rows0 + n)
                    dst = mod[:, n * 512:(n + 1) * 512] if n < MODC else c_mod[:, (n - MODC) * 512:(n - MODC + 1) * 512]
                    copy(dst, mod_bank(n)).then_inc(row_copied, 1)

        def mod_scalar(act, ph):
            mod_copy(act, nc.scalar.copy, ph, 1)

        def mod_vector(dve, ph, link):
            nc.vector.tensor_copy(d_sel, bc(select[:, :].unsqueeze(2), [P, MODC + CTXC, P])).then_inc(sel_ready, 1)
            mod_copy(dve, nc.vector.tensor_copy, ph, 0)
            dve.wait_ge(row_copied, ph.rows0 + len(mod_blocks(ph)))

        def weights_of(w, cols, kk, i):
            return w[i * kk * P:(i + 1) * kk * P, cols].rearrange("(k p) c -> p k c", p=P)

        def stream_sync(sp, w, q0, n, kk, width):
            for i in range(n):
                dst = ring[:, (q0 + i) % RING, 0:kk * width].rearrange("p (k c) -> p k c", k=kk)
                src = weights_of(w, slice(0, width), kk, i)
                h = kk // 2
                slot_fill(sp, q0 + i, [(dst[:, 0:h, :], src[:, 0:h, :]), (dst[:, h:kk, :], src[:, h:kk, :])])

        area = Area(work)
        area.at = 6144
        t_e = area.take(2, 2 * 512)
        t_m = area.take(2, 4)
        t_s = area.take(2, 4)
        s_done, s_masked, s_max, s_exp = sem("scores_done"), sem("scores_masked"), sem("scores_max"), sem("scores_exp")
        s_sumr, s_norm, s_pt, s_ptc, s_pv = sem("sum_inverse"), sem("weights_ready"), sem("weights_ps"), sem("weights_copied"), sem("values_done")
        s_gated, s_out = sem("gated_inverse"), sem("heads_copied")

        def s_banks(i):
            return (pa, pb)[i % 2]

        CAUSAL = dict(rows=[(0, 0, P), (512, 2, TOK)], blocks=[(0, 0), (P, 512), (2 * P, P), (3 * P, 512 + TOK), (512, 512 + P), (512 + P, 512 + TOK + P)])
        WHOLE = dict(rows=[(0, 0, 512)], blocks=[(b * P, b * P) for b in range(8)])

        def pair_rows(v, lo, w):
            return v[:, lo:lo + 2 * w].rearrange("p (u w) -> p u w", u=2)

        def att_tensor(pe, ph, sp):
            n0, n = ph.att0, ph.natt
            for i in range(n + 3):
                if i < n:
                    if i >= 2:
                        pe.wait_ge(s_exp, n0 + i - 1)
                    for dst, lhs, rhs in sp["scores"](i, s_banks(i)):
                        last = nc.tensor.matmul(dst, lhs, rhs, start=True, stop=True)
                    last.then_inc(s_done, 1)
                j = i - 2
                if 0 <= j < n:
                    pe.wait_ge(s_norm, n0 + j + 1)
                    if j >= 1:
                        pe.wait_ge(s_ptc, n0 + j)
                    for dst, src in sp["blocks"]:
                        last = nc.tensor.transpose(acc[:, 1, dst:dst + P], t_e[:, j % 2, src:src + P], ident[:, :])
                    last.then_inc(s_pt, 1)
                j = i - 3
                if j >= 0:
                    pe.wait_ge(s_ptc, n0 + j + 1)
                    done = j // sp["per_pair"]
                    if j % sp["per_pair"] == 0 and done:
                        pe.wait_ge(s_out, ph.out0 + ph.nout - n // sp["per_pair"] + done)
                    for dst, lhs, rhs, first, end in sp["values"](j, sp["pt"][:, j % 2, :]):
                        last = nc.tensor.matmul(dst, lhs, rhs, start=first, stop=end, skip_group_check=True)
                    last.then_inc(s_pv, 1)
                if sp["extra"]:
                    sp["extra"](pe, i)

        def att_scalar(act, ph, sp):
            n0, n = ph.att0, ph.natt
            w = len(sp["blocks"]) * P
            for i in range(n + 3):
                if i < n:
                    act.wait_ge(s_max, n0 + i + 1)
                    if i >= 2:
                        act.wait_ge(s_pt, n0 + i - 1)
                    flat = s_banks(i)[:, :, :].rearrange("p a c -> p (a c)")
                    for lo, k, width in sp["rows"]:
                        for u in range(2):
                            c = slice(lo + u * width, lo + (u + 1) * width)
                            last = nc.scalar.activation(t_e[:, i % 2, c], flat[:, c], ACT.Exp, bias=t_m[:, i % 2, k + u:k + u + 1],
                                                        accum_out=t_s[:, i % 2, k + u:k + u + 1])
                    last.then_inc(s_exp, 1)
                j = i - 2
                if 0 <= j < n:
                    act.wait_ge(s_pt, n0 + j + 1)
                    if j >= 2:
                        act.wait_ge(s_pv, n0 + j - 1)
                    nc.scalar.copy(sp["pt"][:, j % 2, 0:w], acc[:, 1, 0:w]).then_inc(s_ptc, 1)
                j = i - 3
                if j >= 0 and j % sp["per_pair"] == sp["per_pair"] - 1:
                    act.wait_ge(s_pv, n0 + j + 1)
                    nc.scalar.copy(sp["out"][:, j // sp["per_pair"], :], acc[:, 0, 0:TOK]).then_inc(s_out, 1)
                if sp["extra"]:
                    sp["extra"](act, i)

        def att_vector(dve, ph, sp):
            n0, n = ph.att0, ph.natt
            v = nc.vector
            for i in range(n + 1):
                if i < n:
                    dve.wait_ge(s_done, n0 + i + 1)
                    flat = s_banks(i)[:, :, :].rearrange("p a c -> p (a c)")
                    if sp["masked"]:
                        for lo, k, width in sp["rows"]:
                            x = pair_rows(flat, lo, width)[:, :, width - P:width]
                            last = v.tensor_tensor(x, x, bc(causal[:, :].unsqueeze(1), [P, 2, P]), ALU.add)
                        last.then_inc(s_masked, 1)
                        dve.wait_ge(s_masked, ph.masked0 + i + 1)
                    if i >= 2:
                        dve.wait_ge(s_exp, n0 + i - 1)
                    for lo, k, width in sp["rows"]:
                        last = v.tensor_reduce(t_m[:, i % 2, k:k + 2], pair_rows(flat, lo, width), AX.X, ALU.max, negate=True)
                    last.then_inc(s_max, 1)
                j = i - 1
                if j >= 0:
                    dve.wait_ge(s_exp, n0 + j + 1)
                    sums = t_s[:, j % 2, 0:2 * len(sp["rows"])]
                    v.reciprocal(sums, sums).then_inc(s_sumr, 1)
                    dve.wait_ge(s_sumr, n0 + j + 1)
                    if sp["gate"]:
                        sums = sums.rearrange("p (t u) -> p t u", u=2)
                        v.tensor_tensor(sums, sums, sp["gate"](j), ALU.mult).then_inc(s_gated, 1)
                        dve.wait_ge(s_gated, j + 1)
                    for lo, k, width in sp["rows"]:
                        x = pair_rows(t_e[:, j % 2, :], lo, width)
                        last = v.tensor_tensor(x, x, bc(t_s[:, j % 2, k:k + 2].unsqueeze(2), [P, 2, width]), ALU.mult)
                    last.then_inc(s_norm, 1)

        def out_tensor(pe, ph, q0, src=XT):
            pe.wait_ge(s_out, ph.out0 + ph.nout)
            for c in range(KC):
                if c % 4 == 0:
                    slot_wait(pe, q0 + c // 4)
                w = ring[:, (q0 + c // 4) % RING, :].rearrange("p (k c) -> p k c", k=4)[:, c % 4, :]
                for t in range(TT):
                    for h in range(2):
                        last = nc.tensor.matmul(acc[:, t, h * 512:(h + 1) * 512], src[:, c, t * P:(t + 1) * P], w[:, h * 512:(h + 1) * 512],
                                                start=(c == 0), stop=(c == KC - 1))
                if c == 3:
                    last.then_inc(freed, 1)
            last.then_inc(freed, 1)

        NH, HD, NKV = 16, 64, 4
        NKEY = 2 * TOK
        area = Area(work)
        g_cx = area.take(TT, D)
        g_k = work[:, 0:2048].rearrange("p (t j u e) -> p t j u e", t=4, j=NKV, u=2)
        g_hct = area.take(KC, TOK)
        g_q = g_hct
        g_v = area.take(4, NKV * HD)
        g_tmp = area.take(D)
        area.at = 8800
        g_rope_flat = area.take(TT, 64)
        g_rope = g_rope_flat.rearrange("p t (s a e) -> p t s a e", s=2, a=2)
        g_gain = area.take(2, HD)
        g_kte = work[:, 9200:11248].rearrange("p (j t) -> p j t", j=NKV)
        g_kto = XT[:, :, :].rearrange("p (j a) t -> p j (a t)", j=NKV)
        g_out = HM[:, :, :].rearrange("p t (k c) -> p (t k) c", c=TOK)
        cx_ready, kt_cleared, q_copied = sem("context_ready"), sem("keys_cleared"), sem("q_copied")
        qk_ready, qkt_ps, qkt_copied = sem("qk_ready"), sem("qkt_ps"), sem("qkt_copied")

        G_EARLY = 8

        def gqa_spec(extra=None):
            def scores(i, banks):
                pair, t = i // TT, i % TT
                for u, keys in enumerate((g_kte, g_kto)):
                    yield banks[:, u, :], g_q[:, pair, t * P:(t + 1) * P], keys[:, 2 * pair // (NH // NKV), :]

            def values(i, weights):
                pair, t = i // TT, i % TT
                j = 2 * pair // (NH // NKV)
                for b in range(4):
                    for u in range(2):
                        yield (acc[u * HD:(u + 1) * HD, 0, t * P:(t + 1) * P], g_v[:, b, j * HD:(j + 1) * HD],
                               weights[:, (4 * u + b) * P:(4 * u + b + 1) * P], b == 0, b == 3)
            return dict(WHOLE, scores=scores, values=values, masked=False, gate=None, per_pair=TT, extra=extra, out=g_out,
                        pt=work[:, 0:2048].rearrange("p (a c) -> p a c", a=2))

        def gqa_sync(sp, ph):
            stream_sync(sp, a["attn_w_qkv_2"][0], ph.slot0, 4, 2, D + 2 * NKV * HD)
            w_mod_sync(sp, ph, 1)
            stream_sync(sp, a["attn_w_o_2"][0], ph.slot_mod + MODC, 2, 4, D)

        def gqa_pool(pool, ph):
            pool.wait_ge(phase_done, ph.i)
            pool.dma_start(g_cx, a["ctx_2"][0].rearrange("(t p) d -> p t d", p=P)).then_inc(small, 16)
            pool.dma_start(g_rope_flat, a["rope_axes"].rearrange("(t p) e -> p t e", p=P)).then_inc(small, 16)
            pool.dma_start(g_gain[:, 0, :], a["attn_q_norm_2"][0].partition_broadcast(P)).then_inc(small, 16)
            pool.dma_start(g_gain[:, 1, :], a["attn_k_norm_2"][0].partition_broadcast(P)).then_inc(small, 16)
            cond_pool(pool, 1)
            gain_pool(pool, ph.ln, a["norm_mix_2"][ph.layer])
            pow_pool(pool, ph.pow0, slice(32, 36))
            pool.wait_ge(freed, ph.slot0 + 4)
            nc.gpsimd.memset(g_kte[HD:P, :, :], 0.0).then_inc(kt_cleared, 1)
            pool.wait_ge(kt_cleared, 1)
            nc.gpsimd.memset(g_kto[0:HD, :, :], 0.0).then_inc(kt_cleared, 1)
            pool.wait_ge(kt_cleared, 2)
            pow_pool(pool, ph.pow0 + 1, slice(0, 48))
            rows_pool(pool, 1, G_EARLY)

        def gqa_tensor(pe, ph):
            input_wait(pe, ph)
            transpose_tensor(pe, HM)
            pe.wait_ge(cx_ready, 1)
            pe.wait_ge(xt_ready, 2 * (ph.xt + 1))
            transpose_tensor(pe, g_cx)
            pe.wait_ge(xt_ready, 2 * (ph.xt + 2))
            for k in range(KC):
                q = ph.slot0 + k // 2
                if k % 2 == 0:
                    slot_wait(pe, q)
                w = ring[:, q % RING, 0:3072].rearrange("p (k c) -> p k c", k=2)[:, k % 2, :]
                for t in range(TT):
                    fl = dict(start=(k == 0), stop=(k == KC - 1))
                    lat = XT[:, k, t * P:(t + 1) * P]
                    for h in range(2):
                        nc.tensor.matmul(acc[:, t, h * 512:(h + 1) * 512], lat, w[:, h * 512:(h + 1) * 512], **fl)
                    nc.tensor.matmul(pa[:, t, :], lat, w[:, D:D + 512], **fl)
                    last = nc.tensor.matmul(pb[:, t, :], g_hct[:, k, t * P:(t + 1) * P], w[:, D:D + 512], **fl)
                if k % 2:
                    last.then_inc(freed, 1)
            pe.wait_ge(q_copied, 1)
            for n in range(G_EARLY):
                block_tensor(pe, ph, 1, n)
            pe.wait_ge(part_copied, MODC + G_EARLY)
            pe.wait_ge(qk_ready, 1)
            for c in range(KC):
                for t in range(TT):
                    last = nc.tensor.transpose(acc[:, c // 4, (c % 4) * TOK + t * P:(c % 4) * TOK + (t + 1) * P],
                                               HM[:, t, c * P:(c + 1) * P], ident[:, :])
            for j in range(NKV):
                for t in range(4):
                    last = nc.tensor.transpose((pa, pb)[j // 2][:, j % 2, t * P:(t + 1) * P],
                                               work[:, (t * NKV + j) * P:(t * NKV + j + 1) * P], ident[:, :])
            last.then_inc(qkt_ps, 1)
            pe.wait_ge(qkt_copied, 2)
            pe.wait_ge(kt_cleared, 2)
            att_tensor(pe, ph, gqa_spec(lambda e, i: G_EARLY <= i + G_EARLY - 3 < MODC and block_tensor(e, ph, 1, i + G_EARLY - 3)))
            out_tensor(pe, ph, ph.slot_mod + MODC, g_out)

        def gqa_scalar(act, ph):
            transpose_scalar(act, ph.xt, XT)
            transpose_scalar(act, ph.xt + 1, g_hct)
            cond_scalar(act, ph, 1)
            act.wait_ge(freed, ph.slot0 + 4)
            for t in range(TT):
                last = nc.scalar.copy(HM[:, t, :], acc[:, t, :])
            last.then_inc(q_copied, 1)
            for n in range(G_EARLY):
                block_scalar(act, ph, 1, n, G_EARLY)
            for n in (G_EARLY - 2, G_EARLY - 1):
                act.wait_ge(rows_moved[n % 2], rows_count(1, n))
            act.wait_ge(qkt_ps, 1)
            nc.scalar.mul(g_q[:, 0:4, :], acc[:, 0, :].rearrange("p (k c) -> p k c", c=TOK), HD ** -0.5)
            nc.scalar.copy(g_kte[0:HD, 0:2, :], pa[0:HD, :, :])
            nc.scalar.copy(g_kto[HD:P, 0:2, :], pa[HD:P, :, :]).then_inc(qkt_copied, 1)
            att_scalar(act, ph, gqa_spec(lambda e, i: G_EARLY <= i + G_EARLY - 3 < MODC and block_scalar(e, ph, 1, i + G_EARLY - 3, G_EARLY)))

        def gqa_vector(dve, ph, link):
            v = nc.vector
            cond_vector(dve, 1)
            dve.wait_ge(small, ph.small)
            squares(link, X, HM, 32, D)
            for t in range(TT):
                link(v.tensor_tensor_reduce(out=HM[:, t, :], in0=g_cx[:, t, :], in1=g_cx[:, t, :], scale=1.0 / D, scalar=0.0,
                                            op0=ALU.mult, op1=ALU.add, accum_out=stat[:, 34 + t:35 + t]))
            link(v.tensor_scalar(stat[:, 34:36], stat[:, 34:36], RMS_EPS, None, ALU.add))
            dve.sem_inc(var_ready, 1)
            dve.wait_ge(ln_loaded, 32 * (ph.ln + 1))
            link(v.scalar_tensor_tensor(shift[:, :], mod_of(1), 1.0, gain[:, :], ALU.add, ALU.mult))
            link(v.scalar_tensor_tensor(c_mod[:, D:], c_mod[:, D:], 1.0, gain[:, :], ALU.add, ALU.mult))
            dve.wait_ge(rstd_ready, ph.pow0 + 1)
            modulate(link, X, HM, 32, shift[:, :], mod_of(0))
            dve.sem_inc(h_ready, 1)
            dve.sem_inc(ln_used, 1)
            modulate(link, g_cx, g_cx, 34, c_mod[:, D:], c_mod[:, 0:D])
            dve.sem_inc(cx_ready, 1)
            transpose_vector(dve, ph.xt, XT)
            transpose_vector(dve, ph.xt + 1, g_hct)
            dve.wait_ge(freed, ph.slot0 + 4)
            for i, bank in enumerate((pa, pb)):
                link(v.tensor_copy(g_v[:, 2 * i:2 * i + 2, :], bank[:, :, 256:512]))
                link(v.tensor_copy(g_k[:, 2 * i:2 * i + 2, :, 0, :], bank[:, :, 0:256].rearrange("p t (j e) -> p t j e", j=NKV)))
            dve.wait_ge(q_copied, 1)
            keys = work[:, 0:2048].rearrange("p (n u e) -> p n u e", u=2, e=HD)[:, :, 0, :]
            rows = [HM[:, 0, :].rearrange("p (h e) -> p h e", e=HD), HM[:, 1, :].rearrange("p (h e) -> p h e", e=HD), keys]
            sq = g_tmp.rearrange("p (h e) -> p h e", e=HD)
            for i, x in enumerate(rows):
                link(v.tensor_tensor(sq, x, x, ALU.mult))
                link(v.tensor_reduce(stat[:, 16 * i:16 * i + 16], sq, AX.X, ALU.add))
            link(v.tensor_scalar(stat[:, 0:48], stat[:, 0:48], 1.0 / HD, RMS_EPS, ALU.mult, ALU.add))
            dve.sem_inc(var_ready, 1)
            dve.wait_ge(rstd_ready, ph.pow0 + 2)
            for i, x in enumerate(rows):
                link(v.tensor_tensor(x, x, bc(stat[:, 16 * i:16 * i + 16].unsqueeze(2), [P, 16, HD]), ALU.mult))
                link(v.tensor_tensor(x, x, bc(g_gain[:, i // 2, :].unsqueeze(1), [P, 16, HD]), ALU.mult))
            for t in range(TT):
                for x in (rows[t], keys[:, t * NKV:(t + 1) * NKV, :]):
                    n = x.shape[1]
                    x5 = x.rearrange("p h (a u e) -> p h a u e", a=2, u=2)
                    x1, x2 = x5[:, :, :, 0, :], x5[:, :, :, 1, :]
                    cos, sin = (bc(g_rope[:, t, s, :, :].unsqueeze(1), [P, n, 2, 16]) for s in range(2))
                    u1, u2 = (g_tmp[:, o:o + 32 * n].rearrange("p (h a e) -> p h a e", h=n, a=2) for o in (0, 512))
                    link(v.tensor_tensor(u1, x1, sin, ALU.mult))
                    link(v.tensor_tensor(u2, x2, sin, ALU.mult))
                    link(v.tensor_tensor(x1, x1, cos, ALU.mult))
                    link(v.tensor_tensor(x2, x2, cos, ALU.mult))
                    link(v.tensor_tensor(x1, x1, u2, ALU.subtract))
                    link(v.tensor_tensor(x2, x2, u1, ALU.add))
            link(v.tensor_copy(work[:, 0:2048].rearrange("p (n u e) -> p n u e", u=2, e=HD)[:, :, 1, :], keys))
            dve.sem_inc(qk_ready, 1)
            dve.wait_ge(qkt_ps, 1)
            v.tensor_scalar(g_q[:, 4:8, :], acc[:, 1, :].rearrange("p (k c) -> p k c", c=TOK), HD ** -0.5, None, ALU.mult)
            v.tensor_copy(g_kte[0:HD, 2:4, :], pb[0:HD, :, :])
            v.tensor_copy(g_kto[HD:P, 2:4, :], pb[HD:P, :, :]).then_inc(qkt_copied, 1)
            att_vector(dve, ph, gqa_spec())
            dve.wait_ge(freed, ph.slot_mod + MODC + 2)
            gated_vector(dve, link, 2)

        GD = D // 4
        area = Area(work)
        f_tab_flat = area.take(2, 4 * TOK)
        f_tab = f_tab_flat.rearrange("p t (s n) -> p t s n", s=4)
        f_a = area.take(KC, 2 * TOK)
        f_ps, f_copied, f_done = sem("dft_ps"), sem("dft_copied"), sem("dft_done")

        def fourier_sync(sp, ph):
            stream_sync(sp, a["fourier_w_o_2"][0], ph.slot0, 2, 4, D)

        def fourier_pool(pool, ph):
            pool.wait_ge(phase_done, ph.i)
            pool.dma_start(f_tab_flat, a["dft"].rearrange("(t p) n -> p t n", p=P)).then_inc(small, 16)
            gain_pool(pool, ph.ln, a["norm_mix_2"][ph.layer])
            pow_pool(pool, ph.pow0, slice(32, 34))

        def fourier_tensor(pe, ph):
            input_wait(pe, ph)
            pe.wait_ge(small, ph.small)
            for c in range(KC):
                if c >= 4:
                    pe.wait_ge(f_copied, c - 3)
                for t in range(TT):
                    last = nc.tensor.matmul((pa, pb)[c // 2 % 2][:, c % 2, :], HM[:, t, c * P:(c + 1) * P], f_tab[:, t, 0:2, :],
                                            start=(t == 0), stop=(t == 1))
                last.then_inc(f_ps, 1)
            pe.wait_ge(f_copied, KC)
            for c in range(KC):
                g = c // 2
                for i in range(2):
                    for s in range(2):
                        last = nc.tensor.matmul(acc[:, c // 4, (c % 4) * TOK:(c % 4 + 1) * TOK], f_tab[:, i, 2 + s, (c % 2) * P:(c % 2 + 1) * P],
                                                f_a[:, 2 * g + i, s * TOK:(s + 1) * TOK], start=(i + s == 0), stop=(i + s == 2))
            last.then_inc(f_done, 1)
            out_tensor(pe, ph, ph.slot0)

        def fourier_scalar(act, ph):
            act.wait_ge(f_done, 1)
            nc.scalar.copy(XT[:, 0:4, :], acc[:, 0, :].rearrange("p (k c) -> p k c", c=TOK)).then_inc(s_out, 1)

        def fourier_vector(dve, ph, link):
            v = nc.vector
            norm_vector(dve, ph, link, 0)
            for c in range(KC):
                dve.wait_ge(f_ps, c + 1)
                v.tensor_copy(f_a[:, c, :], (pa, pb)[c // 2 % 2][:, c % 2, :]).then_inc(f_copied, 1)
            dve.wait_ge(f_done, 1)
            v.tensor_copy(XT[:, 4:8, :], acc[:, 1, :].rearrange("p (k c) -> p k c", c=TOK)).then_inc(s_out, 1)
            dve.wait_ge(freed, ph.slot0 + 2)
            gated_vector(dve, link, 2)

        NM, NOPE, ROPE, MV = 8, 64, 32, 64
        HQ = NOPE + ROPE
        GW = D // 2
        NGM = GW // P
        QR, KVR = D // 4, D // 8
        LAT = QR + KVR + ROPE
        AB_IN = 2 * GW + LAT
        wide = Area(mod)
        b_q = wide.take(TT, NM, HQ)
        b_k = wide.take(TT, NM, HQ)
        b_u = wide.take(NGM, TOK)
        b_v = wide.take(TT, GW)
        b_latt = wide.take(3, TOK)
        area = Area(work)
        b_qt = area.take(NM, TOK)
        b_kt = area.take(NM, TOK)
        b_wuq = area.take(2, NM * HQ)
        b_bs = area.take(NGM, P)
        area.at = 8720
        b_wst = area.take(NGM, P)
        b_vals = area.take(TT, NM * MV)
        b_qg = area.take(QR)
        b_kvg = area.take(KVR)
        b_kr = area.take(TT, ROPE)
        b_cos = area.take(TT, ROPE // 2)
        b_sin = area.take(TT, ROPE // 2)
        b_ang = area.take(2, TT, ROPE // 2)
        b_turn = area.take(2, TT, ROPE // 2)
        b_freq = area.take(ROPE // 2)
        b_pos = area.take(TT)
        hm = Area(HM[:, :, :].rearrange("p t d -> p (t d)"))
        b_lat = hm.take(TT, LAT)
        b_wuk = hm.take(NM * NOPE)
        b_wuv = hm.take(NM * MV)
        b_posi = hm.take(TT).bitcast(I32)
        area = Area(work)
        area.at = 6144
        b_rot = area.take(2, 512)
        b_ws = area.take(NGM, P)
        b_mask = area.take(P)
        pad_cleared = sem("padding_cleared")
        ws_ps, ws_ready = sem("mixing_t_ps"), sem("mixing_ready")
        ang_ready, trig_ready, gelu_ready = sem("angles_ready"), sem("trig_ready"), sem("gelu_ready")
        vn_ready, gm_ps, gm_read = sem("gmlp_normed"), sem("gmlp_ps"), sem("gmlp_read")
        lat_ready, latt_ps, latt_copied = sem("latents_ready"), sem("latents_t_ps"), sem("latents_t_copied")
        up_done, up_copied = sem("up_done"), sem("up_copied")
        b_qk, b_qkt, b_qktc = sem("mla_qk_ready"), sem("mla_qkt_ps"), sem("mla_qkt_copied")
        TWO_PI = (6.28125, 1.93500518798828125e-3, 3.0198368e-7)
        MAGIC = 1.5 * 2.0 ** 23

        def ab_spec():
            def scores(i, banks):
                for t in range(TT):
                    for u in range(2):
                        w = (t + 1) * P
                        yield banks[:, t, u * w:(u + 1) * w], b_qt[:, 2 * i + u, t * P:(t + 1) * P], b_kt[:, 2 * i + u, 0:w]

            def values(i, weights):
                for t in range(TT):
                    for u in range(2):
                        w = TOK - t * P
                        yield (acc[u * MV:(u + 1) * MV, 0, t * P:TOK], b_vals[:, t, (2 * i + u) * MV:(2 * i + u + 1) * MV],
                               weights[:, t * 512 + u * w:t * 512 + (u + 1) * w], t == 0, t == 1)
            return dict(CAUSAL, scores=scores, values=values, masked=True, gate=None, per_pair=1, extra=None, out=XT[:, NGM:KC, :],
                        pt=work[:, 4096:6144].rearrange("p (a c) -> p a c", a=2))

        def ab_sync(sp, ph):
            stream_sync(sp, a["ab_w_in"][0], ph.slot0, 4, 2, AB_IN)
            stream_sync(sp, a["ab_w_o"][0], ph.slot0 + 4, 2, 4, D)

        def ab_pool(pool, ph):
            for dst, src in (
                    (b_posi, a["pos_cols"]), (b_freq, a["freqs"][0].partition_broadcast(P)),
                    (b_ws, a["ab_gm_ws"][0].rearrange("g t s -> t g s")),
                    (b_wuq, a["ab_mla_w_uq"][0].rearrange("(c p) n -> p c n", p=P)),
                    (b_wuk, a["ab_mla_w_uk"][0]), (b_wuv, a["ab_mla_w_uv"][0]),
                    (b_qg, a["ab_mla_q_norm"][0].partition_broadcast(P)), (b_kvg, a["ab_mla_kv_norm"][0].partition_broadcast(P)),
                    (b_bs, a["ab_gm_bs"][0].partition_broadcast(P))):
                pool.dma_start(dst, src).then_inc(small, 16)
            pool.dma_start(gain[:, 0:GW], a["ab_gm_ln_g"][0].partition_broadcast(P)).then_inc(ln_loaded, 16)
            pool.dma_start(gain[:, GW:D], a["ab_gm_ln_b"][0].partition_broadcast(P)).then_inc(ln_loaded, 16)
            pool.wait_ge(consts, CONSTS)
            nc.gpsimd.memset(b_qt[HQ:P, :, :], 0.0).then_inc(pad_cleared, 1)
            pool.wait_ge(pad_cleared, 1)
            nc.gpsimd.memset(b_kt[HQ:P, :, :], 0.0).then_inc(pad_cleared, 1)
            pool.wait_ge(pad_cleared, 2)
            pow_pool(pool, ph.pow0, slice(0, 6))
            gain_pool(pool, ph.res, a["ln1_g"][0], a["ln1_b"][0])
            pow_pool(pool, ph.pow0 + 1, slice(32, 34))

        def ab_tensor(pe, ph):
            input_wait(pe, ph)
            transpose_tensor(pe, X)
            pe.wait_ge(small, ph.small)
            for g in range(NGM):
                last = nc.tensor.transpose(acc[:, 0, g * P:(g + 1) * P], b_ws[:, g, :], ident[:, :])
            last.then_inc(ws_ps, 1)
            pe.wait_ge(xt_ready, 2 * (ph.xt + 1))
            pe.wait_ge(ws_ready, 1)
            for k in range(KC):
                q = ph.slot0 + k // 2
                if k % 2 == 0:
                    slot_wait(pe, q)
                w = ring[:, q % RING, 0:2 * AB_IN].rearrange("p (k c) -> p k c", k=2)[:, k % 2, :]
                fl = dict(start=(k == 0), stop=(k == KC - 1), skip_group_check=True)
                for m in range(NGM):
                    nc.tensor.matmul(pa[:, m // 2, (m % 2) * TOK:(m % 2 + 1) * TOK], w[:, m * P:(m + 1) * P], XT[:, k, :],
                                     start=(k == 0 and m % 2 == 0), stop=(k == KC - 1), skip_group_check=True)
                for t in range(TT):
                    lat = XT[:, k, t * P:(t + 1) * P]
                    nc.tensor.matmul(acc[:, t, 0:GW], lat, w[:, GW:2 * GW], **fl)
                    last = nc.tensor.matmul(acc[:, t, 512:512 + LAT], lat, w[:, 2 * GW:AB_IN], **fl)
                if k % 2:
                    last.then_inc(freed, 1)
            pe.wait_ge(lat_ready, 1)
            flat = pb[:, :, :].rearrange("p a c -> p (a c)")
            for c in range(3):
                for t in range(TT):
                    last = nc.tensor.transpose(flat[:, c * TOK + t * P:c * TOK + (t + 1) * P], b_lat[:, t, c * P:(c + 1) * P], ident[:, :])
            last.then_inc(latt_ps, 1)
            pe.wait_ge(latt_copied, 1)
            for t in range(TT):
                for h in range(2):
                    for c in range(2):
                        nc.tensor.matmul(acc[:, t, 512 * h:512 * h + NM * HQ // 2], b_latt[:, c, t * P:(t + 1) * P],
                                         b_wuq[:, c, h * NM * HQ // 2:(h + 1) * NM * HQ // 2], start=(c == 0), stop=(c == 1))
                nc.tensor.matmul(pb[:, t, :], b_latt[:, 2, t * P:(t + 1) * P], b_wuk, start=True, stop=True)
            pe.wait_ge(vn_ready, 1)
            for g in range(NGM):
                for n in range(TT):
                    last = nc.tensor.matmul(pa[:, g // 2, (g % 2) * TOK + n * P:(g % 2) * TOK + (n + 1) * P],
                                            b_v[:, n, g * P:(g + 1) * P], b_wst[:, g, :], start=True, stop=True)
            last.then_inc(gm_ps, 1)
            pe.wait_ge(gm_read, 1)
            for t in range(TT):
                last = nc.tensor.matmul(pa[:, t, :], b_latt[:, 2, t * P:(t + 1) * P], b_wuv, start=True, stop=True)
            last.then_inc(up_done, 1)
            pe.wait_ge(b_qk, 1)
            for h in range(NM):
                for t in range(TT):
                    at = (h % 4) * TOK + t * P
                    nc.tensor.transpose(acc[0:HQ, h // 4, at:at + P], b_q[:, t, h, :], ident[:, :])
                    at = (h % 2) * TOK + t * P
                    last = nc.tensor.transpose((pa, pb)[h // 4][0:HQ, h // 2 % 2, at:at + P], b_k[:, t, h, :], ident[:, :])
            last.then_inc(b_qkt, 1)
            pe.wait_ge(b_qktc, 2)
            pe.wait_ge(pad_cleared, 2)
            att_tensor(pe, ph, ab_spec())
            out_tensor(pe, ph, ph.slot0 + 4)

        def ab_scalar(act, ph):
            transpose_scalar(act, ph.xt, XT)
            act.wait_ge(ang_ready, 1)
            nc.scalar.activation(b_sin, b_ang[:, 0, :, :], ACT.Sin)
            nc.scalar.activation(b_cos, b_ang[:, 1, :, :], ACT.Sin).then_inc(trig_ready, 1)
            act.wait_ge(freed, ph.slot0 + 4)
            for t in range(TT):
                nc.scalar.activation(b_v[:, t, :], acc[:, t, 0:GW], ACT.Gelu_apprx_tanh)
            nc.scalar.activation(b_u, pa[:, :, :].rearrange("p a (m c) -> p (a m) c", m=2), ACT.Gelu_apprx_tanh).then_inc(gelu_ready, 1)
            act.wait_ge(latt_ps, 1)
            nc.scalar.copy(b_latt, pb[:, :, :].rearrange("p a (m c) -> p (a m) c", m=2)[:, 0:3, :]).then_inc(latt_copied, 1)
            act.wait_ge(up_done, 1)
            for t in range(TT):
                nc.scalar.copy(b_q[:, t, :, :].rearrange("p (a h) e -> p a (h e)", a=2),
                               acc[:, t, :].rearrange("p (a c) -> p a c", a=2)[:, :, 0:NM * HQ // 2])
            nc.scalar.copy(b_vals, pa[:, :, :]).then_inc(up_copied, 1)
            act.wait_ge(b_qkt, 1)
            for i in range(2):
                last = nc.scalar.mul(b_qt[0:HQ, 4 * i:4 * i + 4, :], acc[0:HQ, i, :].rearrange("p (h c) -> p h c", c=TOK), HQ ** -0.5)
            last.then_inc(b_qktc, 1)
            att_scalar(act, ph, ab_spec())

        def ab_vector(dve, ph, link):
            v = nc.vector
            transpose_vector(dve, ph.xt, XT)
            dve.wait_ge(small, ph.small)
            link(v.tensor_copy(b_pos, b_posi))
            for i in range(2):
                link(v.tensor_tensor(b_ang[:, i, :, :], bc(b_pos.unsqueeze(2), [P, TT, ROPE // 2]), bc(b_freq.unsqueeze(1), [P, TT, ROPE // 2]), ALU.mult))
            link(v.tensor_scalar(b_turn[:, 0, :, :], b_ang[:, 0, :, :], 1 / (2 * np.pi), MAGIC, ALU.mult, ALU.add))
            link(v.tensor_scalar(b_turn[:, 1, :, :], b_ang[:, 1, :, :], 1 / (2 * np.pi), 0.25, ALU.mult, ALU.add))
            link(v.tensor_scalar(b_turn[:, 1, :, :], b_turn[:, 1, :, :], MAGIC, None, ALU.add))
            link(v.tensor_scalar(b_turn, b_turn, MAGIC, None, ALU.subtract))
            for part in TWO_PI:
                link(v.scalar_tensor_tensor(b_ang.rearrange("p i t e -> p (i t e)"), b_turn.rearrange("p i t e -> p (i t e)"), -part,
                                            b_ang.rearrange("p i t e -> p (i t e)"), ALU.mult, ALU.add))
            link(v.tensor_scalar(b_ang[:, 1, :, :], b_ang[:, 1, :, :], float(np.pi / 2), None, ALU.add))
            link(v.tensor_scalar(b_ang, b_ang, 3.1415925, -3.1415925, ALU.min, ALU.max))
            dve.sem_inc(ang_ready, 1)
            link(v.tensor_tensor(b_mask, before[:, :], ident[:, :], ALU.add))
            dve.wait_ge(ws_ps, 1)
            link(v.tensor_tensor(b_wst, acc[:, 0, 0:GW].rearrange("p (g t) -> p g t", g=NGM), bc(b_mask.unsqueeze(1), [P, NGM, P]), ALU.mult))
            dve.sem_inc(ws_ready, 1)
            dve.wait_ge(freed, ph.slot0 + 4)
            for t in range(TT):
                last = v.tensor_copy(b_lat[:, t, :], acc[:, t, 512:512 + LAT])
            link(last)
            junk = b_rot
            for t in range(TT):
                for lo, n, col in ((0, QR, 2), (QR, KVR, 4)):
                    x = b_lat[:, t, lo:lo + n]
                    link(v.tensor_tensor_reduce(out=junk[:, t, 0:n], in0=x, in1=x, scale=1.0 / n, scalar=0.0,
                                                op0=ALU.mult, op1=ALU.add, accum_out=stat[:, col + t:col + t + 1]))
            dve.wait_ge(gelu_ready, 1)
            for t in range(TT):
                last = v.bn_stats(stat[:, 8 + 6 * t:14 + 6 * t], b_v[:, t, :])
            link(last)
            for t in range(TT):
                last = v.bn_aggr(stat[:, 24 + 2 * t:26 + 2 * t], stat[:, 8 + 6 * t:14 + 6 * t])
            link(last)
            mv = stat[:, 24:28].rearrange("p (t s) -> p t s", s=2)
            link(v.tensor_copy(stat[:, 0:2], mv[:, :, 1]))
            v.tensor_scalar(stat[:, 0:6], stat[:, 0:6], LN_EPS, None, ALU.add).then_inc(var_ready, 1)
            dve.wait_ge(rstd_ready, ph.pow0 + 1)
            for t in range(TT):
                for lo, n, col in ((0, QR, 2), (QR, KVR, 4)):
                    x = b_lat[:, t, lo:lo + n]
                    link(v.scalar_tensor_tensor(x, x, stat[:, col + t:col + t + 1], b_qg if lo == 0 else b_kvg, ALU.mult, ALU.mult))
            dve.sem_inc(lat_ready, 1)
            for t in range(TT):
                last = v.tensor_scalar(b_v[:, t, :], b_v[:, t, :], mv[:, t, 0:1], stat[:, t:t + 1], ALU.subtract, ALU.mult)
            link(last)
            dve.wait_ge(ln_loaded, 32 * (ph.ln + 1))
            link(v.tensor_tensor(b_v, b_v, bc(gain[:, 0:GW].unsqueeze(1), [P, TT, GW]), ALU.mult))
            link(v.tensor_tensor(b_v, b_v, bc(gain[:, GW:D].unsqueeze(1), [P, TT, GW]), ALU.add))
            dve.sem_inc(ln_used, 1)
            dve.sem_inc(vn_ready, 1)
            dve.wait_ge(trig_ready, 1)

            def rotate(dst1, dst2, x1, x2, cos, sin, u1, u2):
                link(v.tensor_tensor(u1, x1, sin, ALU.mult))
                link(v.tensor_tensor(u2, x2, sin, ALU.mult))
                link(v.tensor_tensor(dst1, x1, cos, ALU.mult))
                link(v.tensor_tensor(dst2, x2, cos, ALU.mult))
                link(v.tensor_tensor(dst1, dst1, u2, ALU.subtract))
                link(v.tensor_tensor(dst2, dst2, u1, ALU.add))
            R2 = ROPE // 2
            x = b_lat[:, :, QR + KVR:LAT]
            u = [b_rot[:, i, 0:TT * R2].rearrange("p (t e) -> p t e", t=TT) for i in range(2)]
            rotate(b_kr[:, :, 0:R2], b_kr[:, :, R2:], x[:, :, 0:R2], x[:, :, R2:], b_cos, b_sin, *u)
            dve.wait_ge(gm_ps, 1)
            y = XT[:, 0:NGM, :]
            link(v.tensor_tensor(y.rearrange("p g (n t) -> p g n t", n=TT), pa[:, :, :].rearrange("p a (m n t) -> p (a m) n t", m=2, n=TT),
                                 bc(b_bs.unsqueeze(2), [P, NGM, TT, P]), ALU.add))
            dve.sem_inc(gm_read, 1)
            link(v.tensor_tensor(y, y, b_u, ALU.mult))
            dve.sem_inc(s_out, 1)
            dve.wait_ge(up_done, 1)
            for t in range(TT):
                link(v.tensor_copy(b_k[:, t, :, 0:NOPE], pb[:, t, :].rearrange("p (h e) -> p h e", e=NOPE)))
            link(v.tensor_copy(b_k[:, :, :, NOPE:HQ], bc(b_kr.unsqueeze(2), [P, TT, NM, ROPE])))
            dve.wait_ge(up_copied, 1)
            x1, x2 = b_q[:, :, :, NOPE:NOPE + R2], b_q[:, :, :, NOPE + R2:HQ]
            u = [b_rot[:, i, 0:TT * NM * R2].rearrange("p (t h e) -> p t h e", t=TT, h=NM) for i in range(2)]
            cs = [bc(z.unsqueeze(2), [P, TT, NM, R2]) for z in (b_cos, b_sin)]
            rotate(x1, x2, x1, x2, *cs, *u)
            dve.sem_inc(b_qk, 1)
            dve.wait_ge(b_qkt, 1)
            for i, bank in enumerate((pa, pb)):
                last = v.tensor_copy(b_kt[0:HQ, 4 * i:4 * i + 4, :], bank[0:HQ, :, :].rearrange("p a (h c) -> p (a h) c", h=2))
            last.then_inc(b_qktc, 1)
            att_vector(dve, ph, ab_spec())
            dve.wait_ge(freed, ph.slot0 + 6)
            ln_vector(dve, ph, link)

        SH, SG, SD = 16, 2, 64
        CL, CS = 32, 16
        NB = TOK // CS - CL // CS + 1
        HID = 256
        SQ = SH * SD
        C_IN = SQ + 6 * SG * SD + 3 * SH
        CC = CL * SD // P
        VW = 3 * P + 3 * SH
        wide = Area(mod)
        n_pct = wide.take(SH, TOK)
        n_qt = wide.take(KC, TOK)
        hm = Area(HM[:, :, :].rearrange("p t d -> p (t d)"))
        n_kt = hm.take(2, 2, SG, TOK)
        area = Area(work)
        n_v = area.take(TT, VW)
        n_ft = area.take(2, CC, SG * NB)
        n_hid = area.take(2, HID)
        n_hidt = area.take(2, 2, SG * NB)
        n_kc = area.take(SG * NB)
        n_vc = area.take(SG, SD)
        n_e = area.take(TT, SH, NB)
        n_open = area.take(TT, NB)
        n_shut = area.take(TT, NB)
        n_w2 = area.take(2, 2, SD)
        n_pos = area.take(2 * CC)
        n_gb = area.take(3 * SH)
        n_gate = area.take(TT, 3 * SH)
        n_max = area.take(TT, SH)
        n_sum = area.take(TT, SH)
        assert area.at <= 5120
        n_cleared = sem("nsa_cleared")
        n_first, n_second, n_ftr, n_hps, n_hcp, n_htps, n_htcp = (sem(n) for n in (
            "nsa_projected", "nsa_copied", "blocks_ready", "hidden_ps", "hidden_copied", "hidden_t_ps", "hidden_t_copied"))
        n_cps, n_ccp, n_sps, n_xin, n_xout, n_pr, n_tps, n_tcp, n_opened, n_gin, n_gout, n_vr = (sem(n) for n in (
            "compressed_ps", "compressed_copied", "block_scores_ps", "block_exp_in", "block_exp_out", "block_weights_ready",
            "block_weights_ps", "block_weights_copied", "masks_ready", "gates_in", "gates_out", "token_values_ready"))

        N_EARLY = 5

        def nsa_spec(extra=None):
            def scores(i, banks):
                pair, br = i // 2, i % 2
                for t in range(TT):
                    w = (t + 1) * P
                    yield banks[:, t, 0:2 * w], n_qt[:, pair, t * P:(t + 1) * P], n_kt[:, :, br, 2 * pair // (SH // SG), 0:w]

            def values(i, weights):
                pair, br = i // 2, i % 2
                g = 2 * pair // (SH // SG)
                dst = [acc[u * SD:(u + 1) * SD, 0, 0:TOK] for u in range(2)]
                if br == 0:
                    for u in range(2):
                        yield dst[u], n_vc[:, g, :], n_pct[:, 2 * pair + u, :], True, False
                for t in range(TT):
                    for u in range(2):
                        w = TOK - t * P
                        yield (dst[u][:, t * P:TOK], n_v[:, t, br * 2 * P + g * SD:br * 2 * P + (g + 1) * SD],
                               weights[:, t * 512 + u * w:t * 512 + (u + 1) * w], False, br == 1 and t == 1)
            return dict(CAUSAL, scores=scores, values=values, masked=True, per_pair=2, extra=extra, out=XT,
                        pt=work[:, 9200:11248].rearrange("p (a c) -> p a c", a=2),
                        gate=lambda i: n_gate[:, :, (i % 2 + 1) * SH + i // 2 * 2:(i % 2 + 1) * SH + i // 2 * 2 + 2])

        def nsa_sync(sp, ph):
            stream_sync(sp, a["c_w_in"][0], ph.slot0, 4, 2, C_IN)
            for i, w in enumerate((a["c_w_ck1"][0], a["c_w_cv1"][0])):
                stream_sync(sp, w, ph.slot0 + 4 + i, 1, CC, HID)
            w_mod_sync(sp, ph, 0)
            stream_sync(sp, a["c_w_o"][0], ph.slot_mod + MODC, 2, 4, D)

        def nsa_pool(pool, ph):
            pool.wait_ge(phase_done, ph.i)
            for dst, src in ((n_w2[:, 0, :, :], a["c_w_ck2"][0].rearrange("(c p) n -> p c n", p=P)),
                             (n_w2[:, 1, :, :], a["c_w_cv2"][0].rearrange("(c p) n -> p c n", p=P)),
                             (n_pos, a["cmp_pos_cols"]), (n_gb, a["c_gate_b"][0].partition_broadcast(P))):
                pool.dma_start(dst, src).then_inc(small, 16)
            cond_pool(pool, 0)
            nc.gpsimd.memset(n_open, 1.0).then_inc(n_opened, 1)
            nc.gpsimd.memset(n_shut, 0.0).then_inc(n_opened, 1)
            pool.wait_ge(n_opened, 2)
            for m, fill in ((n_open, 0.0), (n_shut, NEG)):
                nc.gpsimd.affine_select(out=m, in_=m, compare_op=ALU.is_ge, fill=fill, base=-(CL - 1),
                                        pattern=[[P, TT], [-CS, NB]], channel_multiplier=1).then_inc(n_opened, 1)
            for i, z in enumerate((n_vc, n_kt[SD:P, 0, :, :, :], n_kt[0:SD, 1, :, :, :], n_pct)):
                nc.gpsimd.memset(z, 0.0).then_inc(n_cleared, 1)
                pool.wait_ge(n_cleared, i + 1)
            gain_pool(pool, ph.ln, a["ln1_g"][ph.layer], a["ln1_b"][ph.layer])
            rows_pool(pool, 0, N_EARLY)
            pow_pool(pool, ph.pow0, slice(32, 34))

        def nsa_tensor(pe, ph):
            input_wait(pe, ph)
            transpose_tensor(pe, X)
            pe.wait_ge(xt_ready, 2 * (ph.xt + 1))

            def w_of(k):
                return ring[:, (ph.slot0 + k // 2) % RING, 0:2 * C_IN].rearrange("p (k c) -> p k c", k=2)[:, k % 2, :]
            for k in range(KC):
                if k % 2 == 0:
                    slot_wait(pe, ph.slot0 + k // 2)
                w = w_of(k)
                end = dict(stop=(k == KC - 1), skip_group_check=True)
                for m in range(KC):
                    nc.tensor.matmul(acc[:, m // 4, (m % 4) * TOK:(m % 4 + 1) * TOK], w[:, m * P:(m + 1) * P], XT[:, k, :],
                                     start=(k == 0 and m % 2 == 0), **end)
                for i in range(2):
                    for g in range(SG):
                        c0 = SQ + (2 + 2 * i) * P + g * SD
                        for u in range(2):
                            nc.tensor.matmul(pa[u * SD:(u + 1) * SD, i, g * TOK:(g + 1) * TOK], w[:, c0:c0 + SD], XT[:, k, :],
                                             start=(k == 0 and g == 0), **end)
                for i in range(2):
                    for g in range(SG):
                        c0 = SQ + i * P + g * SD
                        for u in range(2):
                            last = nc.tensor.matmul(pb[u * SD:(u + 1) * SD, i, g * TOK:(g + 1) * TOK - u], w[:, c0:c0 + SD], XT[:, k, u:TOK],
                                                    start=(k == 0 and g == 0), **end)
            last.then_inc(n_first, 1)
            pe.wait_ge(n_second, 1)
            for k in range(KC):
                w = w_of(k)
                for t in range(TT):
                    last = nc.tensor.matmul(pa[:, t, 0:VW], XT[:, k, t * P:(t + 1) * P], w[:, C_IN - VW:C_IN], start=(k == 0), stop=(k == KC - 1))
                if k % 2:
                    last.then_inc(freed, 1)
            pe.wait_ge(n_ftr, 1)
            for i in range(2):
                slot_wait(pe, ph.slot0 + 4 + i)
                w = ring[:, (ph.slot0 + 4 + i) % RING, :].rearrange("p (c n) -> p c n", c=CC)
                for c in range(CC):
                    last = nc.tensor.matmul(pb[0:SG * NB, i, 0:HID], n_ft[:, i, c, :], w[:, c, :], start=(c == 0), stop=(c == CC - 1))
                last.then_inc(freed, 1)
            pe.wait_ge(n_hcp, 1)
            for i in range(2):
                for c in range(2):
                    last = nc.tensor.transpose(pb[:, 0, (2 * i + c) * 32:(2 * i + c) * 32 + SG * NB], n_hid[0:SG * NB, i, c * P:(c + 1) * P],
                                               ident[0:SG * NB, 0:SG * NB])
            last.then_inc(n_htps, 1)
            pe.wait_ge(n_htcp, 1)
            pe.wait_ge(small, ph.small)
            for u in range(2):
                for c in range(2):
                    nc.tensor.matmul(pb[u * SD:(u + 1) * SD, 1, 0:SG * NB], n_w2[:, 0, c, :], n_hidt[:, 0, c, :], start=(c == 0), stop=(c == 1))
            for g in range(SG):
                for c in range(2):
                    last = nc.tensor.matmul(pb[0:NB, 1, (g + 1) * SD:(g + 2) * SD], n_hidt[:, 1, c, g * NB:(g + 1) * NB], n_w2[:, 1, c, :],
                                            start=(c == 0), stop=(c == 1))
            last.then_inc(n_cps, 1)
            pe.wait_ge(n_ccp, 2)
            pe.wait_ge(n_vr, 1)
            for t in range(TT):
                for h in range(SH):
                    r = slice(64 * (h % 2), 64 * (h % 2) + 64)
                    g = h // (SH // SG)
                    last = nc.tensor.matmul(pa[:, h % 2, (t * SH + h) // 2 * NB:((t * SH + h) // 2 + 1) * NB], n_qt[r, h // 2, t * P:(t + 1) * P],
                                            n_kc[r, g * NB:(g + 1) * NB], start=True, stop=True)
            last.then_inc(n_sps, 1)
            for n in range(N_EARLY):
                block_tensor(pe, ph, 0, n)
            pe.wait_ge(part_copied, N_EARLY)
            pe.wait_ge(n_pr, 1)
            for t in range(TT):
                if t:
                    pe.wait_ge(n_tcp, 2)
                for h in range(SH):
                    last = nc.tensor.transpose(acc[0:NB, h // 8, (h % 8) * P:(h % 8 + 1) * P], n_e[:, t, h, :], ident[:, :])
                last.then_inc(n_tps, 1)
            pe.wait_ge(n_tcp, 4)
            pe.wait_ge(n_cleared, 4)
            att_tensor(pe, ph, nsa_spec(lambda e, i: N_EARLY <= i + N_EARLY - 3 < MODC and block_tensor(e, ph, 0, i + N_EARLY - 3)))
            out_tensor(pe, ph, ph.slot_mod + MODC)

        def nsa_scalar(act, ph):
            transpose_scalar(act, ph.xt, XT)
            act.wait_ge(n_first, 1)
            for i in range(TT):
                last = nc.scalar.mul(n_qt[:, 4 * i:4 * i + 4, :], acc[:, i, :].rearrange("p (k c) -> p k c", c=TOK), SD ** -0.5)
            last.then_inc(n_ccp, 1)
            cond_scalar(act, ph, 0)
            act.wait_ge(n_gin, 1)
            nc.scalar.activation(n_gate, n_gate, ACT.Sigmoid).then_inc(n_gout, 1)
            act.wait_ge(freed, ph.slot0 + 6)
            nc.scalar.activation(n_hid[0:SG * NB, :, :], pb[0:SG * NB, :, 0:HID], ACT.Gelu_apprx_tanh).then_inc(n_hcp, 1)
            act.wait_ge(n_xin, 1)
            nc.scalar.activation(n_e, n_e, ACT.Exp).then_inc(n_xout, 1)
            for n in range(N_EARLY):
                block_scalar(act, ph, 0, n, N_EARLY)
            for n in (N_EARLY - 2, N_EARLY - 1):
                act.wait_ge(rows_moved[n % 2], rows_count(0, n))
            act.wait_ge(n_cleared, 4)
            for t in range(TT):
                act.wait_ge(n_tps, t + 1)
                nc.scalar.copy(n_pct[0:NB, 0:8, t * P:(t + 1) * P], acc[0:NB, 0, :].rearrange("p (h c) -> p h c", c=P)).then_inc(n_tcp, 1)
            att_scalar(act, ph, nsa_spec(lambda e, i: N_EARLY <= i + N_EARLY - 3 < MODC and block_scalar(e, ph, 0, i + N_EARLY - 3, N_EARLY)))

        def nsa_vector(dve, ph, link):
            v = nc.vector
            transpose_vector(dve, ph.xt, XT)
            cond_vector(dve, 0)
            dve.wait_ge(n_first, 1)
            for u in range(2):
                r = slice(u * SD, (u + 1) * SD)
                last = v.tensor_copy(n_kt[r, u, :, :, :], pa[r, :, :].rearrange("p i (g c) -> p i g c", g=SG))
            last.then_inc(n_second, 1)
            dve.wait_ge(small, ph.small)
            for i in range(2):
                for g in range(SG):
                    seen = pb[:, i, g * TOK:(g + 1) * TOK]
                    src = bass.AP(seen.tensor, seen.offset, [list(seen.ap[0]), [2, CC], [CS, NB]])
                    last = v.tensor_tensor(n_ft[:, i, :, g * NB:(g + 1) * NB], src, bc(n_pos[:, i * CC:(i + 1) * CC].unsqueeze(2), [P, CC, NB]), ALU.add)
            last.then_inc(n_ftr, 1)
            dve.wait_ge(freed, ph.slot0 + 4)
            for t in range(TT):
                last = v.tensor_copy(n_v[:, t, :], pa[:, t, 0:VW])
            last.then_inc(n_vr, 1)
            dve.wait_ge(n_vr, 1)
            v.tensor_tensor(n_gate, n_v[:, :, 3 * P:VW], bc(n_gb.unsqueeze(1), [P, TT, 3 * SH]), ALU.add).then_inc(n_gin, 1)
            dve.wait_ge(n_htps, 1)
            v.tensor_copy(n_hidt, pb[:, 0, 0:128].rearrange("p (i c n) -> p i c n", i=2, c=2)[:, :, :, 0:SG * NB]).then_inc(n_htcp, 1)
            dve.wait_ge(n_cps, 1)
            dve.wait_ge(n_cleared, 4)
            v.tensor_copy(n_vc[0:NB, :, :], pb[0:NB, 1, SD:3 * SD].rearrange("p (g e) -> p g e", g=SG))
            v.tensor_copy(n_kc, pb[:, 1, 0:SG * NB]).then_inc(n_ccp, 1)
            dve.wait_ge(n_sps, 1)
            dve.wait_ge(n_opened, 4)
            for t in range(TT):
                for u in range(2):
                    half_n = SH // 2 * NB
                    last = v.scalar_tensor_tensor(n_e[:, t, u::2, :], pa[:, u, t * half_n:(t + 1) * half_n].rearrange("p (h n) -> p h n", n=NB),
                                                  1.0, bc(n_shut[:, t, :].unsqueeze(1), [P, SH // 2, NB]), ALU.mult, ALU.add)
            link(last)
            link(v.tensor_reduce(n_max, n_e, AX.X, ALU.max))
            v.tensor_tensor(n_e, n_e, bc(n_max.unsqueeze(3), [P, TT, SH, NB]), ALU.subtract).then_inc(n_xin, 1)
            dve.wait_ge(n_xout, 1)
            link(v.tensor_reduce(n_sum, n_e, AX.X, ALU.add))
            dve.wait_ge(n_gout, 1)
            link(v.reciprocal(n_sum, n_sum))
            link(v.tensor_tensor(n_sum, n_gate[:, :, 0:SH], n_sum, ALU.mult))
            link(v.tensor_tensor(n_e, n_e, bc(n_sum.unsqueeze(3), [P, TT, SH, NB]), ALU.mult))
            link(v.tensor_tensor(n_e, n_e, bc(n_open.unsqueeze(2), [P, TT, SH, NB]), ALU.mult))
            dve.sem_inc(n_pr, 1)
            for t in range(TT):
                dve.wait_ge(n_tps, t + 1)
                v.tensor_copy(n_pct[0:NB, 8:SH, t * P:(t + 1) * P], acc[0:NB, 1, :].rearrange("p (h c) -> p h c", c=P)).then_inc(n_tcp, 1)
            att_vector(dve, ph, nsa_spec())
            dve.wait_ge(freed, ph.slot_mod + MODC + 2)
            ln_vector(dve, ph, link)

        block = ctx.enter_context(nc.Block())
        last_ph = plan[-1]
        final = last_ph.kind not in ("ab", "nsa") and last_ph.fn != FN1

        @block.sync
        def _(sp):
            if plan[0].kind == "moe":
                for s in full:
                    sp.sem_inc(s, FILL)
            sp.dma_start(X[:, :, :], a["x"].rearrange("(t p) d -> p t d", p=P)).then_inc(x_loaded, 16)
            sp.dma_start(select[:, :], a["mod_select"]).then_inc(select_loaded, 16)
            for ph in plan:
                if ph.kind != "mod":
                    dict(ab=ab_sync, nsa=nsa_sync, gqa=gqa_sync, fourier=fourier_sync, moe=moe_sync)[ph.kind](sp, ph)
            sp.wait_ge(phase_done, len(plan) + final)
            sp.dma_start(out.rearrange("(t p) d -> p t d", p=P), X[:, :, :]).then_inc(out_done, 16)
            sp.wait_ge(out_done, 16)

        @block.gpsimd
        def _(pool):
            tables_pool(pool, Link(pool, poo))
            for ph in plan:
                if ph.kind == "moe":
                    router_pool(pool, ph)
                    if ph.fn == FN1:
                        gain_pool(pool, ph.ln, a["ln2_g"][ph.layer], a["ln2_b"][ph.layer])
                    else:
                        gain_pool(pool, ph.ln, a["norm_ffn_2"][ph.layer])
                    pow_pool(pool, ph.pow0, slice(32, 34))
                elif ph.kind != "mod":
                    dict(ab=ab_pool, nsa=nsa_pool, gqa=gqa_pool, fourier=fourier_pool)[ph.kind](pool, ph)
            if final:
                gain_pool(pool, last_ph.ln + 1, a["final_norm_2"])
                pow_pool(pool, last_ph.pow0 + last_ph.npow, slice(32, 34))

        @block.tensor
        def _(pe):
            if plan[0].kind == "moe":
                pe.sem_inc(freed, RING)
            pe.sem_inc(xfreed, CREDIT)
            for r in R:
                for s in r.values():
                    pe.sem_inc(s, START)
            for ph in plan:
                if ph.kind == "moe":
                    input_wait(pe, ph)
                    transpose_tensor(pe, source(ph))
                    moe_tensor(pe, ph)
                else:
                    dict(ab=ab_tensor, nsa=nsa_tensor, mod=mod_tensor, gqa=gqa_tensor, fourier=fourier_tensor)[ph.kind](pe, ph)

        @block.scalar
        def _(act):
            for ph in plan:
                if ph.kind == "moe":
                    transpose_scalar(act, ph.xt, XT)
                    router_scalar(act, ph)
                    moe_other(act, ph, lambda r, t, g, up, every: round_scalar(act, ph, r, t, up, every))
                else:
                    dict(ab=ab_scalar, nsa=nsa_scalar, mod=mod_scalar, gqa=gqa_scalar, fourier=fourier_scalar)[ph.kind](act, ph)

        @block.vector
        def _(dve):
            link = Link(dve, vec)
            dve.wait_ge(x_loaded, 16)
            dve.wait_ge(consts, CONSTS)
            dve.wait_ge(select_loaded, 16)
            for ph in plan:
                if ph.kind == "moe":
                    if ph.fn == FN2:
                        norm_vector(dve, ph, link, 3)
                    transpose_vector(dve, ph.xt, XT)
                    router_vector(dve, ph, link)
                    moe_other(dve, ph, lambda r, t, g, up, every: round_vector(dve, ph, r, t, g, every), last=True)
                    if ph.fn == FN1:
                        ln_vector(dve, ph, link)
                    else:
                        gated_vector(dve, link, 5)
                else:
                    dict(ab=ab_vector, nsa=nsa_vector, mod=mod_vector, gqa=gqa_vector, fourier=fourier_vector)[ph.kind](dve, ph, link)
                dve.sem_inc(phase_done, 1)
            if final:
                squares(link, X, HM, 32, D)
                dve.sem_inc(var_ready, 1)
                dve.wait_ge(ln_loaded, 32 * (last_ph.ln + 2))
                dve.wait_ge(rstd_ready, last_ph.pow0 + last_ph.npow + 1)
                for t in range(TT):
                    link(nc.vector.scalar_tensor_tensor(X[:, t, :], X[:, t, :], stat[:, 32 + t:33 + t], gain[:, :], ALU.mult, ALU.mult))
                dve.sem_inc(phase_done, 1)


def make_plan(kinds):
    plan = []
    slot = RING if kinds[0][0] == "moe" else 0
    moe = xt = h = ln = pow_ = small = att = out_ = masked = rows = 0
    for i, (kind, layer, fn) in enumerate(kinds):
        ph = Phase(kind, layer, fn)
        ph.i = i
        block1 = kind in ("ab", "nsa") or fn == FN1
        if not block1 and kind != "mod":
            h += 1
        ph.slot0, ph.moe, ph.xt, ph.h, ph.ln, ph.pow0, ph.att0, ph.out0, ph.masked0 = slot, moe, xt, h, ln, pow_, att, out_, masked
        ph.npow = {"ab": 2, "nsa": 1, "moe": 1, "gqa": 2, "fourier": 1, "mod": 0}[kind]
        ph.natt = {"ab": 4, "nsa": 16, "gqa": 16}.get(kind, 0)
        ph.slot_mod = slot + {"nsa": 6, "gqa": 4}.get(kind, 0)
        ph.rows0 = rows
        rows += {0: 16, 1: 12}[layer] if kind == "mod" else 0
        ph.nout = {"ab": 5, "nsa": 8, "gqa": 8, "fourier": 2}.get(kind, 0)
        small += 16 * {"ab": 9, "nsa": 6, "moe": 0, "gqa": 6, "fourier": 1, "mod": 0}[kind]
        ph.small = small
        slot += ph.slots()
        moe += kind == "moe"
        xt += {"mod": 0, "fourier": 0, "gqa": 2}.get(kind, 1)
        pow_ += ph.npow
        att += ph.natt
        out_ += ph.nout
        masked += ph.natt if kind in ("ab", "nsa") else 0
        ph.res = ln + (kind == "ab")
        ln += {"mod": 0, "ab": 2}.get(kind, 1)
        h += block1
        plan.append(ph)
    return plan


def axis_tables():
    n = 16
    inv = np.float32(10000.0) ** (-np.arange(n, dtype=np.float32) / np.float32(n))
    tok = np.arange(TOK)
    ang = np.stack([(tok // 64).astype(np.float32)[:, None] * inv, (tok % 64).astype(np.float32)[:, None] * inv], 1)
    return np.stack([np.cos(ang), np.sin(ang)], 1).reshape(TOK, 4 * n).astype(np.float32)


def dft_tables():
    i = np.arange(TOK)
    ang = 2 * np.pi * (np.outer(i, i) % TOK) / TOK
    c, s = np.cos(ang) / 16, np.sin(ang) / 16
    return np.concatenate([c, s, c, -s], 1).astype(np.float32)


def mod_selectors():
    p = np.arange(P)[:, None]
    n = np.arange(16)[None]
    return (((p // 4 == n) & (p < 64)) | (p == 64 + n % 12) ).astype(np.float32)


def by_feature(c, c_ctx):
    return np.ascontiguousarray(np.stack([c.reshape(KC, P), c_ctx.reshape(KC, P)]).transpose(2, 0, 1).reshape(P, 2 * KC))


def latent_freqs():
    return np.exp(np.float32(-np.log(10000.0)) * np.arange(16, dtype=np.float32) / np.float32(16)).astype(np.float32)[None]


def position_columns(cmp_pos):
    return np.ascontiguousarray(cmp_pos.reshape(2, 16, P).transpose(2, 0, 1).reshape(P, 32))


KINDS = [("ab", 0, 0), ("moe", 0, FN1), ("nsa", 1, 0), ("moe", 1, FN1),
         ("mod", 0, 0), ("gqa", 0, 0), ("moe", 0, FN2), ("mod", 1, 0), ("fourier", 1, 0), ("moe", 1, FN2)]
AS_THEY_ARE = """ab_w_in ab_gm_ln_g ab_gm_ln_b ab_gm_ws ab_gm_bs ab_mla_q_norm ab_mla_kv_norm ab_mla_w_uq ab_mla_w_uk
ab_mla_w_uv ab_w_o c_w_in c_w_ck1 c_w_ck2 c_w_cv1 c_w_cv2 c_gate_b c_w_o moe_w_rg moe_b_rg moe_w_re moe_b_re
moe_w_gate moe_w_up moe_w_down ln1_g ln1_b ln2_g ln2_b ctx_2 w_mod_2 b_mod_2 norm_mix_2 norm_ffn_2 attn_w_qkv_2
attn_q_norm_2 attn_k_norm_2 attn_w_o_2 fourier_w_o_2 moe_w_rg_2 moe_b_rg_2 moe_w_re_2 moe_b_re_2 moe_w1_2 moe_w3_2
moe_w2_2 final_norm_2""".split()


def kernel(**inputs):
    import concourse.bacc as bacc
    from concourse.bass_utils import run_bass_kernel_spmd

    nc = bacc.Bacc("TRN2", target_bir_lowering=False, num_devices=1)
    given = {n: np.ascontiguousarray(inputs[n]) for n in AS_THEY_ARE}
    given["x"] = np.ascontiguousarray(inputs["x"]).reshape(TOK, D)
    given["pos_cols"] = np.ascontiguousarray(np.asarray(inputs["positions"]).reshape(TT, P).T)
    given["cond"] = by_feature(np.asarray(inputs["c_2"]), np.asarray(inputs["c_ctx_2"]))
    given["cmp_pos_cols"] = position_columns(np.asarray(inputs["c_cmp_pos"]))
    given["mod_select"] = mod_selectors()
    given["freqs"] = latent_freqs()
    given["rope_axes"] = axis_tables()
    given["dft"] = dft_tables()
    a = {n: nc.dram_tensor(f"in_{n}", v.shape, mybir.dt.from_np(v.dtype), kind="ExternalInput").ap() for n, v in given.items()}
    out = nc.dram_tensor("out", (TOK, D), F32, kind="ExternalOutput").ap()
    build_model(nc, a, out, make_plan(KINDS))
    r = run_bass_kernel_spmd(nc, [{f"in_{n}": v for n, v in given.items()}], core_ids=[0])
    return r.results[0]["out"].reshape(1, TOK, D)
```

```python
from contextlib import ExitStack

import numpy as np

import concourse.bass as bass
from concourse import mybir

F32 = mybir.dt.float32
I32 = mybir.dt.int32
ALU = mybir.AluOpType
ACT = mybir.ActivationFunctionType
AX = mybir.AxisListType

P = 128
D = 1024
TOK = 256
TT = TOK // P
KC = D // P
NEG = -1e30

RING = 6
SLOT = 4096
FILL = 32

NG, EPG = 4, 8
NE = NG * EPG
CAP = 32
SIDE = P // CAP
ROUNDS = NE // SIDE
MAXPASS = TOK // CAP
START = 1
UNITS = 12
CREDIT = 4
XSLOTS = 2


FN1, FN2 = D // 4, D // 2
ALPHA = (2.0 * 2) ** 0.25
LN_EPS, RMS_EPS = 1e-5, 1e-6
CONSTS = 9


class Phase:

    def __init__(self, kind, layer, fn=0):
        self.kind, self.layer, self.fn = kind, layer, fn
        self.slot0 = 0
        self.moe = 0
        self.xt = 0
        self.h = 0
        self.lnh = 0
        self.ln = 0
        self.x0 = 0
        self.out0 = 0
        self.nout = 0
        self.att0 = 0
        self.natt = 0
        self.masked0 = 0
        self.mix = 0
        self.rows0 = 0
        self.slot_mod = 0

    def slots(self):
        if self.kind == "moe":
            return ROUNDS * moe_slots(self.fn)
        return {"ab": 6, "nsa": 20, "mod": 0, "gqa": 18, "fourier": 2}[self.kind]


def moe_slots(fn):
    return (2 * D * fn * SIDE + fn * D * SIDE) // (P * SLOT)




def build_model(nc, a, out, plan):
    with ExitStack() as ctx:
        def sb(name, shape, dt=F32):
            return ctx.enter_context(nc.sbuf_tensor(name, shape, dt))

        def sem(name):
            return ctx.enter_context(nc.semaphore(name))

        ring = sb("ring", [P, RING, SLOT])
        X = sb("X", [P, TT, D])
        XT = sb("XT", [P, KC, TOK])
        HM = sb("HM", [P, TT, D])
        gain = sb("gain", [P, D])
        shift = sb("shift", [P, D])
        mod = sb("mod", [P, 6 * D])
        mod_rows = sb("mod_rows", [P, 512])
        select = sb("select", [P, 16])
        early = sb("early", [P, D])
        raw = sb("raw", [P, 2 * KC])
        rope = sb("rope", [P, TT * 64])
        hgain = sb("hgain", [P, 2, 64])
        work = sb("work", [P, 11248])
        wr = sb("wr", [P, KC, 4 + NE])
        br = sb("br", [4 + NE, 1])
        ident = sb("ident", [P, P])
        ones = sb("ones", [P, P])
        zeros = sb("zeros", [P, P])
        before = sb("before", [P, P])
        causal = sb("causal", [P, P])
        iota = sb("iota", [P, CAP])
        iota_i = sb("iota_i", [P, CAP], I32)
        thresh = sb("thresh", [P, MAXPASS - 1])
        stat = sb("stat", [P, 64])
        half = sb("half", [P, 64])
        extra_f = sb("extra_f", [P, 4])
        extra_i = sb("extra_i", [1, 4, 2], I32)

        acc = ctx.enter_context(nc.psum_tensor("acc", [P, TT, D], F32))
        pa = ctx.enter_context(nc.psum_tensor("pa", [P, 2, 512], F32))
        pb = ctx.enter_context(nc.psum_tensor("pb", [P, 2, 512], F32))

        x_loaded = sem("x_loaded")
        select_loaded = sem("select_loaded")
        consts = sem("consts")
        full = [sem(f"slot{i}_full") for i in range(RING)]
        freed = sem("slot_freed")
        h_ready = sem("h_ready")
        xt_ps = sem("xt_ps")
        xt_ready = sem("xt_ready")
        vec = sem("vec_step")
        eps_added = sem("eps_added")
        squared = sem("squared")
        x_ready = sem("x_ready")
        poo = sem("pool_step")
        ln_loaded = sem("ln_loaded")
        ln_used = sem("ln_used")
        var_ready = sem("var_ready")
        rstd_ready = sem("rstd_ready")
        mix_done = sem("mix_done")
        small = sem("small_loaded")
        result_ready = sem("result_ready")
        out_done = sem("out_done")
        phase_done = sem("phase_done")
        S = {}

        def sg(name):
            if name not in S:
                S[name] = sem(name)
            return S[name]

        class Link:

            def __init__(self, eng, s):
                self.eng, self.s, self.n = eng, s, 0

            def __call__(self, ins):
                self.n += 1
                ins.then_inc(self.s, 1)
                self.eng.wait_ge(self.s, self.n)

        def slot_wait(eng, q):
            eng.wait_ge(full[q % RING], FILL * (q // RING + 1))

        def slot_fill(sp, q, parts):
            if q >= RING:
                sp.wait_ge(freed, q - RING + 1)
            for dst, src in parts:
                sp.dma_start(dst, src).then_inc(full[q % RING], 16)

        def bc(v, shape):
            return v.to_broadcast(shape)

        class Area:

            def __init__(self, t):
                self.t, self.at = t, 0

            def take(self, *shape, rows=P):
                n = 1
                for s in shape:
                    n *= s
                v = self.t[0:rows, self.at:self.at + n]
                self.at += n
                assert self.at <= self.t.shape[1], (self.at, self.t.shape)
                if len(shape) == 1:
                    return v
                names = " ".join(f"d{i}" for i in range(len(shape)))
                return v.rearrange(f"p ({names}) -> p {names}", **{f"d{i}": s for i, s in enumerate(shape) if i})

        def source(ph):
            return X if ph.kind in ("ab", "nsa") or (ph.kind == "moe" and ph.fn == FN1) else HM

        def by_chunk(v):
            return v[:, :, :].rearrange("p a (k c) -> p (a k) c", c=P)

        def input_wait(eng, ph, t=TT - 1):
            if ph.h == 0:
                eng.wait_ge(x_loaded, 16)
                eng.wait_ge(consts, CONSTS)
            else:
                eng.wait_ge(h_ready, TT * (ph.h - 1) + t + 1)

        def transpose_tensor(pe, src, ph=None):
            for t in range(TT):
                if ph:
                    input_wait(pe, ph, t)
                dst = by_chunk((pa, pb)[t])
                for k in range(KC):
                    last = nc.tensor.transpose(dst[:, k, :], src[:, t, k * P:(k + 1) * P], ident[:, :])
                last.then_inc(xt_ps, 1)

        def transpose_scalar(act, n, dst):
            act.wait_ge(xt_ps, 2 * n + 1)
            nc.scalar.copy(dst[:, :, 0:P], by_chunk(pa)).then_inc(xt_ready, 1)

        def transpose_vector(dve, n, dst):
            dve.wait_ge(xt_ps, 2 * n + 2)
            nc.vector.tensor_copy(dst[:, :, P:TOK], by_chunk(pb)).then_inc(xt_ready, 1)

        def gain_pool(pool, n, g, b=None):
            if n:
                pool.wait_ge(ln_used, n)
            if b is None:
                pool.dma_start(gain[:, :], g.partition_broadcast(P)).then_inc(ln_loaded, 32)
                return
            pool.dma_start(gain[:, :], g.partition_broadcast(P)).then_inc(ln_loaded, 16)
            pool.dma_start(shift[:, :], b.partition_broadcast(P)).then_inc(ln_loaded, 16)

        class Tally:

            def __init__(self):
                self.n = 0

            def next(self):
                self.n += 1
                return self.n

        served, awaited, squares = Tally(), Tally(), Tally()

        def pow_pool(pool, cols, eps=None):
            n = served.next()
            pool.wait_ge(var_ready, n)
            x = stat[:, cols]
            if eps is not None:
                nc.gpsimd.tensor_scalar(x, x, eps, None, ALU.add).then_inc(eps_added, 1)
                pool.wait_ge(eps_added, n)
            else:
                pool.sem_inc(eps_added, 1)
            nc.gpsimd.tensor_tensor(x, x, half[:, 0:cols.stop - cols.start], ALU.pow).then_inc(rstd_ready, 1)

        def tile_pows(pool, eps, between=None):
            for t in range(TT):
                if t and between:
                    between(pool)
                pow_pool(pool, slice(32 + t, 33 + t), eps)

        def rstd_wait(dve):
            dve.wait_ge(rstd_ready, awaited.next())

        def ln_vector(dve, ph, link, mixed=False):
            dve.wait_ge(ln_loaded, 32 * (ph.ln + 1))
            v = nc.vector
            for t in range(TT):
                if mixed:
                    dve.wait_ge(mix_done, TT * ph.mix + t + 1)
                x = X[:, t, :]
                st, mv = stat[:, 12 * t:12 * t + 12], stat[:, 24 + 2 * t:26 + 2 * t]
                link(v.scalar_tensor_tensor(x, x, ALPHA, acc[:, t, :], ALU.mult, ALU.add))
                for h in range(2):
                    last = v.bn_stats(st[:, 6 * h:6 * h + 6], X[:, t, h * 512:(h + 1) * 512])
                link(last)
                link(v.bn_aggr(mv, st))
                v.tensor_scalar(stat[:, 32 + t:33 + t], mv[:, 1:2], LN_EPS, None, ALU.add).then_inc(var_ready, 1)
                link(v.scalar_tensor_tensor(x, x, mv[:, 0:1], gain[:, :], ALU.subtract, ALU.mult))
                rstd_wait(dve)
                v.scalar_tensor_tensor(x, x, stat[:, 32 + t:33 + t], shift[:, :], ALU.mult, ALU.add).then_inc(h_ready, 1)
                dve.wait_ge(h_ready, TT * ph.lnh + t + 1)
            dve.sem_inc(ln_used, 1)

        junk = work[:, 9200:9200 + D]

        def mod_of(i):
            return mod[:, i * D:(i + 1) * D]

        def square_scalar(act, x, col, to=junk, ready=var_ready):
            nc.scalar.activation(to, x, ACT.Square, scale=float(D) ** -0.5, accum_out=stat[:, col:col + 1]).then_inc(squared, 1)
            act.wait_ge(squared, squares.next())
            act.sem_inc(ready, 1)

        def squares_scalar(act, first, to=junk):
            for t in range(TT):
                act.wait_ge(x_ready, first + t + 1)
                square_scalar(act, X[:, t, :], 32 + t, to)

        def scale_vector(dve, ln, link, which):
            dve.wait_ge(ln_loaded, 32 * (ln + 1))
            link(nc.vector.scalar_tensor_tensor(shift[:, :], mod_of(which + 1), 1.0, gain[:, :], ALU.add, ALU.mult))
            dve.sem_inc(ln_used, 1)

        def modulate_vector(dve, link, which, t, h):
            v = nc.vector
            link(v.tensor_tensor(HM[:, t, :], X[:, t, :], shift[:, :], ALU.mult))
            rstd_wait(dve)
            v.scalar_tensor_tensor(HM[:, t, :], HM[:, t, :], stat[:, 32 + t:33 + t], mod_of(which), ALU.mult, ALU.add).then_inc(h_ready, 1)
            dve.wait_ge(h_ready, h)

        def gated_vector(dve, link, which, t, n):
            link(nc.vector.tensor_tensor(HM[:, t, :], acc[:, t, :], mod_of(which)[:, :], ALU.mult))
            nc.vector.tensor_tensor(X[:, t, :], X[:, t, :], HM[:, t, :], ALU.add).then_inc(x_ready, 1)
            dve.wait_ge(x_ready, n)

        def mixed_vector(dve, ph, link):
            nxt = plan[ph.i + 1]
            dve.wait_ge(row_copied, ph.rows0)
            scale_vector(dve, nxt.ln, link, 3)
            for t in range(TT):
                dve.wait_ge(mix_done, TT * ph.mix + t + 1)
                gated_vector(dve, link, 2, t, ph.x0 + t + 1)
                modulate_vector(dve, link, 3, t, TT * (nxt.h - 1) + t + 1)

        area = Area(work)
        m_xg = XT[:, :, 0:P]
        m_p = area.take(TT, P)
        m_pw = area.take(TT, P)
        m_pwt = area.take(TOK)
        m_silu = area.take(512)
        m_hh = area.take(512)
        m_ht = area.take(4, P)
        m_yg = XT[:, :, P:TOK]
        m_log = area.take(TT, 4 + NE)
        m_lt = work[0:NG + NE, 9200 + D:9200 + D + TOK]
        m_rank = area.take(TT, NE)
        m_w = area.take(TT, NE)
        m_a = area.take(TT, NE)
        m_t = [area.take(TT, NE) for _ in range(4)]
        m_g = [area.take(TT, NG) for _ in range(3)]
        m_s = area.take(16, TT)
        xring = area.take(XSLOTS, SLOT)

        R = [{n: sem(f"{n}{k}") for n in (
            "p_ready", "pw_ready", "rank_next", "gathered", "xg_copied", "pwt_ps", "pwt_copied", "silu_done", "hh_ready", "ht_ps", "ht_copied", "y_copied", "added")} for k in ("", "_x")]
        xfull = [sem(f"xslot{i}_full") for i in range(XSLOTS)]
        xfreed = sem("xslot_freed")
        logits_done, ranks_done = sem("logits_done"), sem("ranks_done")
        logits_biased, logits_t = sem("logits_biased"), sem("logits_by_token")
        assign_ready, extra_ready = sem("assign_ready"), sem("extra_ready")
        rexp_in, rexp_out = sem("router_exp_in"), sem("router_exp_out")
        wr_loaded = sem("router_loaded")

        def moe_names(ph):
            if ph.fn == FN1:
                return a["moe_w_gate"][ph.layer], a["moe_w_up"][ph.layer], a["moe_w_down"][ph.layer]
            return a["moe_w1_2"][ph.layer], a["moe_w3_2"][ph.layer], a["moe_w2_2"][ph.layer]

        def router_pool(pool, ph):
            s = "" if ph.fn == FN1 else "_2"
            if ph.moe:
                pool.wait_ge(assign_ready, ph.moe)
            for lo, hi, n in ((0, NG, "g"), (NG, NG + NE, "e")):
                pool.dma_start(wr[:, :, lo:hi], a[f"moe_w_r{n}{s}"][ph.layer].rearrange("(k p) n -> p k n", p=P)).then_inc(wr_loaded, 16)
                pool.dma_start(br[lo:hi, :], a[f"moe_b_r{n}{s}"][ph.layer].rearrange("(n o) -> n o", o=1)).then_inc(wr_loaded, 16)

        def next_router_pool(pool, ph):
            if ph.i + 1 < len(plan) and plan[ph.i + 1].kind == "moe":
                router_pool(pool, plan[ph.i + 1])

        def router_tensor(pe, ph):
            pe.wait_ge(xt_ready, 2 * (ph.xt + 1))
            pe.wait_ge(wr_loaded, 64 * (ph.moe + 1))
            for k in range(KC):
                last = nc.tensor.matmul(pa[0:NG + NE, 0, 0:TOK], wr[:, k, :], XT[:, k, :], start=(k == 0), stop=(k == KC - 1))
            last.then_inc(logits_done, 1)
            pe.wait_ge(logits_biased, ph.moe + 1)
            for t in range(TT):
                last = nc.tensor.transpose(pa[:, 1, t * (NG + NE):(t + 1) * (NG + NE)], m_lt[:, t * P:(t + 1) * P], ident[0:NG + NE, 0:NG + NE])
            last.then_inc(logits_t, 1)
            for t in range(TT):
                for h in range(2):
                    nc.tensor.matmul(acc[:, t, h * 512:(h + 1) * 512], zeros[:, :], source(ph)[:, t, h * 512:(h + 1) * 512],
                                     start=True, stop=True)
            pe.wait_ge(assign_ready, ph.moe + 1)
            nc.tensor.matmul(pb[:, 0, 0:NE], before[:, :], m_a[:, 0, :], start=True, stop=True)
            nc.tensor.matmul(pb[:, 0, NE:2 * NE], before[:, :], m_a[:, 1, :], start=True, stop=False)
            nc.tensor.matmul(pb[:, 0, NE:2 * NE], ones[:, :], m_a[:, 0, :], start=False, stop=True)
            nc.tensor.matmul(pb[:, 1, 0:NE], ones[:, :], m_a[:, 0, :], start=True, stop=False)
            nc.tensor.matmul(pb[:, 1, 0:NE], ones[:, :], m_a[:, 1, :], start=False, stop=True).then_inc(ranks_done, 1)

        def router_scalar(act, ph):
            act.wait_ge(logits_done, ph.moe + 1)
            nc.scalar.activation(m_lt, pa[0:NG + NE, 0, 0:TOK], ACT.Identity, bias=br[:, :]).then_inc(logits_biased, 1)
            n = 2 * ph.moe
            act.wait_ge(rexp_in, n + 1)
            nc.scalar.activation(m_g[1], m_g[1], ACT.Exp).then_inc(rexp_out, 1)
            act.wait_ge(rexp_in, n + 2)
            nc.scalar.activation(m_s[:, 4, :], m_s[:, 4, :], ACT.Exp).then_inc(rexp_out, 1)

        def router_vector(dve, ph, link):
            v = nc.vector

            def first_of(out_, x, m, iv, tmp, n):
                link(v.tensor_tensor(tmp, x, bc(m.unsqueeze(2), [P, TT, n]), ALU.is_equal))
                link(v.scalar_tensor_tensor(tmp, tmp, -64.0, bc(iv.unsqueeze(1), [P, TT, n]), ALU.mult, ALU.add))
                link(v.tensor_reduce(m_s[:, 15, :], tmp, AX.X, ALU.min))
                link(v.tensor_tensor(out_, tmp, bc(m_s[:, 15, :].unsqueeze(2), [P, TT, n]), ALU.is_equal))

            dve.wait_ge(logits_t, ph.moe + 1)
            link(v.tensor_copy(m_log, pa[:, 1, 0:TT * (NG + NE)].rearrange("p (t n) -> p t n", t=TT)))
            lg, le = m_log[:, :, 0:NG], m_log[:, :, NG:]
            gmax, l1, l2, gw, dif, w1, w2 = (m_s[:, i, :] for i in range(7))
            link(v.tensor_reduce(gmax, lg, AX.X, ALU.max))
            first_of(m_g[0], lg, gmax, iota[:, 0:NG], m_g[2], NG)
            v.tensor_tensor(m_g[1], lg, bc(gmax.unsqueeze(2), [P, TT, NG]), ALU.subtract).then_inc(rexp_in, 1)
            link(v.tensor_scalar(m_g[2], m_g[0], 1.0, -NEG, ALU.subtract, ALU.mult))
            lm, o1, o2, tmp = m_t
            link(v.tensor_tensor(lm.rearrange("p t (g e) -> p t g e", g=NG), le.rearrange("p t (g e) -> p t g e", g=NG),
                                 bc(m_g[2].unsqueeze(3), [P, TT, NG, EPG]), ALU.add))
            link(v.tensor_reduce(l1, lm, AX.X, ALU.max))
            first_of(o1, lm, l1, iota[:, 0:NE], tmp, NE)
            link(v.scalar_tensor_tensor(lm, o1, 3 * NEG, lm, ALU.mult, ALU.add))
            link(v.tensor_reduce(l2, lm, AX.X, ALU.max))
            first_of(o2, lm, l2, iota[:, 0:NE], tmp, NE)
            v.tensor_tensor(dif, l2, l1, ALU.subtract).then_inc(rexp_in, 1)
            v.tensor_tensor(m_a, o1, o2, ALU.add).then_inc(assign_ready, 1)
            dve.wait_ge(rexp_out, 2 * ph.moe + 2)
            link(v.tensor_reduce(gw, m_g[1], AX.X, ALU.add))
            link(v.tensor_scalar(w1, dif, 1.0, None, ALU.add))
            link(v.tensor_tensor(w1, w1, gw, ALU.mult))
            link(v.reciprocal(w1, w1))
            link(v.tensor_tensor(w2, w1, dif, ALU.mult))
            link(v.tensor_tensor(o1, o1, bc(w1.unsqueeze(2), [P, TT, NE]), ALU.mult))
            link(v.tensor_tensor(o2, o2, bc(w2.unsqueeze(2), [P, TT, NE]), ALU.mult))
            link(v.tensor_tensor(m_w, o1, o2, ALU.add))
            dve.wait_ge(ranks_done, ph.moe + 1)
            link(v.scalar_tensor_tensor(m_rank, pb[:, 0, 0:2 * NE].rearrange("p (t e) -> p t e", t=TT), 1.0, m_a,
                                        ALU.add, ALU.mult))
            link(v.tensor_scalar(m_rank, m_rank, 1.0, None, ALU.subtract))
            link(v.tensor_reduce(extra_f[:, 2:3], pb[:, 1, 0:NE], AX.X, ALU.max))
            link(v.tensor_scalar(m_s[:, 8:12, :].rearrange("p a b -> p (a b)")[:, 0:MAXPASS - 1], thresh[:, :], extra_f[:, 2:3], None, ALU.is_lt))
            link(v.tensor_reduce(extra_f[:, 0:1], m_s[:, 8:12, :].rearrange("p a b -> p (a b)")[:, 0:MAXPASS - 1], AX.X, ALU.add))
            link(v.tensor_copy(extra_i[0:1, ph.moe, :], extra_f[0:1, 0:2]))
            link(v.tensor_tensor(extra_f[:, 1:2], extra_f[:, 1:2], extra_f[:, 0:1], ALU.add))
            dve.sem_inc(extra_ready, 1)

        def round_sync(sp, ph, g, wait_free, fills, slot_of, inc):
            gate, up, down = moe_names(ph)
            ex = bass.ds(g * SIDE, SIDE)
            n = moe_slots(ph.fn)
            n_down = ph.fn // P
            rows = SLOT // (2 * SIDE * ph.fn)
            for i in range(n):
                dst = slot_of(i)
                wait_free(i)
                if i < n - n_down:
                    for m, w in enumerate((gate, up)):
                        src = w[ex].rearrange("j (c p r) f -> c p j (r f)", p=P, r=rows)[i]
                        sp.dma_start(dst[:, m * SLOT // 2:(m + 1) * SLOT // 2].rearrange("p (j f) -> p j f", j=SIDE), src).then_inc(fills(i), inc)
                else:
                    for m in range(2):
                        c = i - (n - n_down)
                        src = down[bass.ds(g * SIDE + m * 2, 2), c * P:(c + 1) * P, :].rearrange("j p f -> p j f")
                        sp.dma_start(dst[:, m * SLOT // 2:(m + 1) * SLOT // 2].rearrange("p (j f) -> p j f", j=2), src).then_inc(fills(i), inc)

        def round_tensor(pe, ph, r, t, wait_full, free, slot_of):
            fn = ph.fn
            src = source(ph)
            rows = SLOT // (2 * SIDE * fn)
            n_down = fn // P
            n_up = moe_slots(fn) - n_down
            xg_ps = pa[:, :, :].rearrange("p a (k c) -> p (a k) c", c=P)
            hbank = (pb[:, 0, 0:fn], pb[:, 1, 0:fn])
            pe.wait_ge(r["p_ready"], t + 1 + START)
            pe.wait_ge(r["y_copied"], 2 * t + START)
            for c in range(n_up):
                for q in range(rows):
                    for tt in range(TT):
                        lhs = src[:, tt, c * P * rows:(c + 1) * P * rows].rearrange("p (f r) -> p f r", r=rows)[:, :, q]
                        last = nc.tensor.matmul(xg_ps[:, c * rows + q, :], lhs, m_p[:, tt, :], start=(tt == 0), stop=(tt == TT - 1))
            last.then_inc(r["gathered"], 1)
            pe.wait_ge(r["pw_ready"], t + 1 + START)
            pe.wait_ge(r["hh_ready"], t + START)
            for tt in range(TT):
                last = nc.tensor.transpose(pb[:, 1, tt * P:(tt + 1) * P], m_pw[:, tt, :], ident[:, :])
            last.then_inc(r["pwt_ps"], 1)
            pe.wait_ge(r["pwt_copied"], t + 1 + START)
            pe.wait_ge(r["ht_copied"], t + START)
            pe.wait_ge(r["xg_copied"], 2 * (t + 1) + START)
            for c in range(n_up):
                wait_full(c)
                slot = slot_of(c).rearrange("p (m j r f) -> p m j r f", m=2, j=SIDE, r=rows)
                for q in range(rows):
                    k = c * rows + q
                    for m in range(2):
                        for j in range(SIDE):
                            last = nc.tensor.matmul(hbank[m][j * CAP:(j + 1) * CAP, :], m_xg[:, k, j * CAP:(j + 1) * CAP],
                                                    slot[:, m, j, q, :], start=(k == 0), stop=(k == KC - 1))
                last.then_inc(*free)
            pe.wait_ge(r["hh_ready"], t + 1 + START)
            for c in range(n_down):
                last = nc.tensor.transpose(pb[:, 0, c * P:(c + 1) * P], m_hh[:, c * P:(c + 1) * P], ident[:, :])
            last.then_inc(r["ht_ps"], 1)
            pe.wait_ge(r["ht_copied"], t + 1 + START)
            for c in range(n_down):
                wait_full(n_up + c)
                slot = slot_of(n_up + c).rearrange("p (j f) -> p j f", j=SIDE)
                for h in range(2):
                    for j in range(SIDE):
                        last = nc.tensor.matmul(pa[j * CAP:(j + 1) * CAP, h, :], m_ht[:, c, j * CAP:(j + 1) * CAP],
                                                slot[:, j, h * 512:(h + 1) * 512], start=(c == 0), stop=(c == n_down - 1))
                last.then_inc(*free)
            pe.wait_ge(r["y_copied"], 2 * (t + 1) + START)
            for tt in range(TT):
                for h in range(2):
                    last = nc.tensor.matmul(acc[:, tt, h * 512:(h + 1) * 512], m_pwt[:, tt * P:(tt + 1) * P],
                                            m_yg[:, 4 * h:4 * h + 4, :], start=False, stop=True, skip_group_check=True)
            last.then_inc(r["added"], 1)

        def round_scalar(act, ph, r, t, freed_up, freed_all):
            fn = ph.fn
            act.wait_ge(r["gathered"], t + 1 + START)
            nc.scalar.copy(m_xg[:, 0:4, :], pa[:, 0, :].rearrange("p (k c) -> p k c", c=P)).then_inc(r["xg_copied"], 1)
            freed_up(act)
            nc.scalar.activation(m_silu[:, 0:fn], pb[:, 0, 0:fn], ACT.Silu).then_inc(r["silu_done"], 1)
            freed_all(act)
            nc.scalar.copy(m_yg[:, 0:4, :], pa[:, 0, :].rearrange("p (k c) -> p k c", c=P)).then_inc(r["y_copied"], 1)

        def round_vector(dve, ph, r, t, g, freed_all):
            fn = ph.fn
            v = nc.vector
            ex = bass.ds(g * SIDE, SIDE)
            shape = [P, TT, SIDE, CAP]
            dve.wait_ge(r["rank_next"], t + START)
            dve.wait_ge(r["gathered"], t + START)
            one = m_p.rearrange("p t (j s) -> p t j s", j=SIDE)
            gated = m_pw.rearrange("p t (j s) -> p t j s", j=SIDE)
            v.tensor_tensor(one, bc(iota[:, :].unsqueeze(1).unsqueeze(1), shape),
                            bc(m_rank[:, :, ex].unsqueeze(3), shape), ALU.is_equal).then_inc(r["p_ready"], 1)
            dve.wait_ge(r["p_ready"], t + 1 + START)
            dve.wait_ge(r["pwt_ps"], t + START)
            v.tensor_tensor(gated, one, bc(m_w[:, :, ex].unsqueeze(3), shape), ALU.mult).then_inc(r["pw_ready"], 1)
            v.tensor_scalar(m_rank[:, :, ex], m_rank[:, :, ex], float(CAP), None, ALU.subtract).then_inc(r["rank_next"], 1)
            dve.wait_ge(r["gathered"], t + 1 + START)
            v.tensor_copy(m_xg[:, 4:8, :], pa[:, 1, :].rearrange("p (k c) -> p k c", c=P)).then_inc(r["xg_copied"], 1)
            dve.wait_ge(r["pwt_ps"], t + 1 + START)
            v.tensor_copy(m_pwt, pb[:, 1, 0:TOK]).then_inc(r["pwt_copied"], 1)
            dve.wait_ge(r["silu_done"], t + 1 + START)
            v.tensor_tensor(m_hh[:, 0:fn], m_silu[:, 0:fn], pb[:, 1, 0:fn], ALU.mult).then_inc(r["hh_ready"], 1)
            dve.wait_ge(r["ht_ps"], t + 1 + START)
            v.tensor_copy(m_ht[:, 0:fn // P, :], pb[:, 0, 0:fn].rearrange("p (c s) -> p c s", s=P)).then_inc(r["ht_copied"], 1)
            freed_all(dve)
            v.tensor_copy(m_yg[:, 4:8, :], pa[:, 1, :].rearrange("p (k c) -> p k c", c=P)).then_inc(r["y_copied"], 1)

        def moe_sync(sp, ph):
            n = moe_slots(ph.fn)
            with sp.Fori(0, ROUNDS) as g:
                def wait_free(i):
                    sp.wait_ge(freed, ph.slot0 + g * n + i - RING + 1)
                round_sync(sp, ph, g, wait_free, lambda i: full[(ph.slot0 + i) % RING],
                           lambda i: ring[:, (ph.slot0 + i) % RING, :], 16)
            sp.wait_ge(extra_ready, ph.moe + 1)
            more = sp.value_load(extra_i[0:1, ph.moe, 0:1], min_val=0, max_val=MAXPASS - 1)
            base = sp.value_load(extra_i[0:1, ph.moe, 1:2], min_val=0, max_val=4 * (MAXPASS - 1))
            unit = UNITS // n
            with sp.If(more > 0):
                with sp.Fori(0, more) as ps:
                    with sp.Fori(0, ROUNDS) as g:
                        t = (base + ps) * ROUNDS + g

                        def wait_free(i):
                            sp.wait_ge(xfreed, t * UNITS + (CREDIT + unit * (i + 1 - XSLOTS)))
                        round_sync(sp, ph, g, wait_free, lambda i: xfull[i % XSLOTS],
                                   lambda i: xring[:, i % XSLOTS, :], 16 * unit)

        def moe_tensor(pe, ph):
            n = moe_slots(ph.fn)
            router_tensor(pe, ph)
            with pe.Fori(0, ROUNDS) as g:
                def wait_full(i):
                    q = ph.slot0 + i
                    pe.wait_ge(full[q % RING], g * (FILL * (n // RING)) + FILL * (q // RING + 1))
                round_tensor(pe, ph, R[0], g + ROUNDS * ph.moe, wait_full, (freed, 1),
                             lambda i: ring[:, (ph.slot0 + i) % RING, :])
            pe.wait_ge(extra_ready, ph.moe + 1)
            more = pe.value_load(extra_i[0:1, ph.moe, 0:1], min_val=0, max_val=MAXPASS - 1)
            base = pe.value_load(extra_i[0:1, ph.moe, 1:2], min_val=0, max_val=4 * (MAXPASS - 1))
            unit = UNITS // n
            with pe.If(more > 0):
                pe.wait_ge(R[0]["y_copied"], 2 * ROUNDS * (ph.moe + 1) + START)
                with pe.Fori(0, more) as ps:
                    with pe.Fori(0, ROUNDS) as g:
                        t = (base + ps) * ROUNDS + g

                        def wait_full(i):
                            pe.wait_ge(xfull[i % XSLOTS], t * (FILL * UNITS // XSLOTS) + 32 * unit * (i // XSLOTS + 1))
                        round_tensor(pe, ph, R[1], t, wait_full, (xfreed, unit), lambda i: xring[:, i % XSLOTS, :])

        def moe_other(eng, ph, body, last=False):
            n = moe_slots(ph.fn)
            up = n - ph.fn // P
            with eng.Fori(0, ROUNDS) as g:
                body(R[0], g + ROUNDS * ph.moe, g,
                     lambda e: e.wait_ge(freed, ph.slot0 + g * n + up),
                     lambda e: e.wait_ge(freed, ph.slot0 + g * n + n))
            if last:
                eng.wait_ge(R[0]["added"], ROUNDS * (ph.moe + 1) + START)
            eng.wait_ge(extra_ready, ph.moe + 1)
            more = eng.value_load(extra_i[0:1, ph.moe, 0:1], min_val=0, max_val=MAXPASS - 1)
            base = eng.value_load(extra_i[0:1, ph.moe, 1:2], min_val=0, max_val=4 * (MAXPASS - 1))
            unit = UNITS // n
            with eng.If(more > 0):
                eng.wait_ge(R[0]["added"], ROUNDS * (ph.moe + 1) + START)
                eng.wait_ge(R[0]["rank_next"], ROUNDS * (ph.moe + 1) + START)
                with eng.Fori(0, more) as ps:
                    with eng.Fori(0, ROUNDS) as g:
                        t = (base + ps) * ROUNDS + g
                        body(R[1], t, g,
                             lambda e: e.wait_ge(xfreed, t * UNITS + (CREDIT + unit * up)),
                             lambda e: e.wait_ge(xfreed, t * UNITS + (CREDIT + UNITS)))
            if last:
                eng.wait_ge(R[1]["added"], (base + more) * ROUNDS + START)

        def tables_pool(pool, link):
            g = nc.gpsimd
            g.memset(ones[:, :], 1.0).then_inc(consts, 1)
            g.memset(zeros[:, :], 0.0).then_inc(consts, 1)
            g.memset(half[:, :], -0.5).then_inc(consts, 1)
            g.memset(mod_rows[:, :], 0.0).then_inc(consts, 1)
            link(g.memset(ident[:, :], 0.0))
            g.affine_select(out=ident[:, :], in_=ident[:, :], compare_op=ALU.not_equal, fill=1.0, base=0,
                            pattern=[[-1, P]], channel_multiplier=1).then_inc(consts, 1)
            link(g.memset(before[:, :], 1.0))
            g.affine_select(out=before[:, :], in_=before[:, :], compare_op=ALU.is_gt, fill=0.0, base=0,
                            pattern=[[1, P]], channel_multiplier=-1).then_inc(consts, 1)
            link(g.memset(causal[:, :], 0.0))
            g.affine_select(out=causal[:, :], in_=causal[:, :], compare_op=ALU.is_ge, fill=NEG, base=0,
                            pattern=[[-1, P]], channel_multiplier=1).then_inc(consts, 1)
            link(g.iota(iota_i[:, :], pattern=[[1, CAP]], base=0, channel_multiplier=0))
            g.tensor_copy(iota[:, :], iota_i[:, :]).then_inc(consts, 1)
            link(g.tensor_copy(thresh[:, :], iota_i[:, 0:MAXPASS - 1]))
            link(g.tensor_scalar(thresh[:, :], thresh[:, :], 1.0, float(CAP), ALU.add, ALU.mult))
            g.memset(extra_f[:, :], 0.0).then_inc(consts, 1)

        MODC = 6 * D // 512
        CTXC = 2 * D // 512
        area = Area(work)
        area.at = 8208
        d_cond = area.take(KC, CAP)
        d_sel = work[:, 6144:6144 + (MODC + CTXC) * P].rearrange("p (n c) -> p n c", c=P)
        c_mod = work[:, 9200:9200 + 2 * D]
        d_bank = acc[:, 0, 512:D]
        cond_ready, cond_silu = sem("cond_ready"), sem("cond_silu")
        part_copied, row_ps, row_copied, sel_ready = sem("part_copied"), sem("row_ps"), sem("row_copied"), sem("selectors_ready")
        work_free = sem("work_free")
        bias_loaded = sem("bias_loaded")
        rows_moved = [sem(f"rows_moved{i}") for i in range(2)]

        def rows_count(layer, n):
            done = 0
            for l in range(layer + 1):
                for m in range(n % 2, MODC if l < layer else n + 1, 2):
                    done += 32 if l == 0 and m < CTXC else 16
            return done

        def d_part(n, early):
            return work[:, 5120 + n % 2 * 512:5632 + n % 2 * 512] if n >= early else XT[:, 2 * (n % 2):2 * (n % 2) + 2, :].rearrange("p k c -> p (k c)")

        def w_mod_sync(sp, ph, layer):
            w = a["w_mod_2"][layer]
            for n in range(MODC):
                q = ph.slot_mod + n
                dst = ring[:, q % RING, :].rearrange("p (k c) -> p k c", k=KC)
                src = w[:, n * 512:(n + 1) * 512].rearrange("(k p) c -> p k c", p=P)
                slot_fill(sp, q, [(dst[:, 0:4, :], src[:, 0:4, :]), (dst[:, 4:8, :], src[:, 4:8, :])])

        def cond_vector(dve, layer):
            nc.vector.memset(d_cond, 0.0).then_inc(cond_ready, 1)

        def cond_scalar(act, ph, layer):
            act.wait_ge(cond_ready, layer + 1)
            nc.scalar.activation(d_cond[:, :, 0:2], raw[:, :].rearrange("p (c k) -> p k c", c=2), ACT.Silu).then_inc(cond_silu, 1)

        def between(block, ph, layer, early):
            def step(eng, i):
                n = early + i // 2
                if i % 2 and n < MODC:
                    block(eng, ph, layer, n, early)
            return step

        def block_tensor(pe, ph, layer, n, early):
            if n == 0:
                pe.wait_ge(cond_silu, layer + 1)
            else:
                pe.wait_ge(part_copied, MODC * layer + n)
            q = ph.slot_mod + n
            slot_wait(pe, q)
            w = ring[:, q % RING, :].rearrange("p (k c) -> p k c", k=KC)
            for r in range(2):
                for j in range(SIDE):
                    k = SIDE * r + j
                    last = nc.tensor.matmul(d_bank[j * CAP:(j + 1) * CAP, :], d_cond[:, k, :], w[:, k, :], start=(r == 0), stop=(r == 1))
            last.then_inc(freed, 1)

        def block_scalar(act, ph, layer, n, early):
            act.wait_ge(freed, ph.slot_mod + n + 1)
            if n >= 2:
                act.wait_ge(rows_moved[n % 2], rows_count(layer, n - 2))
            nc.scalar.copy(d_part(n, early), d_bank).then_inc(part_copied, 1)

        def rows_pool(pool, layer, early):
            if layer:
                pool.wait_ge(row_ps, MODC + CTXC)
            pool.dma_start(mod_rows[64:64 + MODC, :], a["b_mod_2"][layer].rearrange("(n c) -> n c", c=512)).then_inc(bias_loaded, 16)
            for n in range(MODC):
                pool.wait_ge(part_copied, MODC * layer + n + 1)
                part = d_part(n, early)
                pool.dma_start(mod_rows[4 * n:4 * n + 4, :], part[0:P:CAP, :]).then_inc(rows_moved[n % 2], 16)
                if layer == 0 and n < CTXC:
                    pool.dma_start(mod_rows[48 + 4 * n:52 + 4 * n, :], part[1:P:CAP, :]).then_inc(rows_moved[n % 2], 16)

        N_SHIFT_SCALE = 4

        def mod_blocks(ph):
            return [*range(N_SHIFT_SCALE), *(range(MODC, MODC + CTXC) if ph.layer == 0 else ()), *range(N_SHIFT_SCALE, MODC)]

        def mod_bank(i):
            return (pa, pb)[i // 2 % 2][:, i % 2, :]

        def mod_tensor(pe, ph):
            pe.wait_ge(bias_loaded, 16 * (ph.layer + 1))
            for n in (MODC - 2, MODC - 1):
                pe.wait_ge(rows_moved[n % 2], rows_count(ph.layer, n))
            blocks = mod_blocks(ph)
            for i, n in enumerate(blocks):
                if i == 0 or i == N_SHIFT_SCALE:
                    pe.wait_ge(sel_ready, 2 * ph.layer + 1 + (i > 0))
                if i >= 4:
                    pe.wait_ge(row_copied, ph.rows0 + i - 3)
                nc.tensor.matmul(mod_bank(i), d_sel[:, n, :], mod_rows[:, :], start=True, stop=True).then_inc(row_ps, 1)
            pe.wait_ge(row_copied, ph.rows0 + len(blocks))

        flat_xt = XT[:, 0:4, :].rearrange("p k c -> p (k c)")

        def mod_scalar(act, ph):
            act.wait_ge(work_free, ph.layer + 1)
            for lo, hi in ((0, N_SHIFT_SCALE), (N_SHIFT_SCALE, MODC + CTXC)):
                nc.scalar.copy(d_sel[:, lo:hi, :], bc(select[:, lo:hi].unsqueeze(2), [P, hi - lo, P])).then_inc(sel_ready, 1)
            if ph.layer == 0:
                act.wait_ge(cx_loaded, 16)
                for t in range(TT):
                    square_scalar(act, HM[:, t, :], 34 + t, flat_xt, cx_var)
                act.wait_ge(cx_rstd, 2)
                for t in range(TT):
                    nc.scalar.mul(g_cx[:, t, :], HM[:, t, :], stat[:, 34 + t:35 + t]).then_inc(cx_normed, 1)
            for i, n in enumerate(mod_blocks(ph)):
                if ph.layer == 1 and i == N_SHIFT_SCALE:
                    squares_scalar(act, ph.x0 - TT, flat_xt)
                act.wait_ge(row_ps, ph.rows0 + i + 1)
                dst = mod[:, n * 512:(n + 1) * 512] if n < MODC else c_mod[:, (n - MODC) * 512:(n - MODC + 1) * 512]
                nc.scalar.copy(dst, mod_bank(i)).then_inc(row_copied, 1)
            if ph.layer == 0:
                squares_scalar(act, ph.x0 - TT, flat_xt)

        def weights_of(w, cols, kk, i):
            return w[i * kk * P:(i + 1) * kk * P, cols].rearrange("(k p) c -> p k c", p=P)

        def stream_sync(sp, w, q0, n, kk, width):
            for i in range(n):
                dst = ring[:, (q0 + i) % RING, 0:kk * width].rearrange("p (k c) -> p k c", k=kk)
                src = weights_of(w, slice(0, width), kk, i)
                h = kk // 2
                slot_fill(sp, q0 + i, [(dst[:, 0:h, :], src[:, 0:h, :]), (dst[:, h:kk, :], src[:, h:kk, :])])

        area = Area(work)
        area.at = 6144
        t_e = area.take(2, 2 * 512)
        t_m = area.take(2, 4)
        t_s = area.take(2, 4)
        s_done, s_masked, s_max, s_exp = sem("scores_done"), sem("scores_masked"), sem("scores_max"), sem("scores_exp")
        s_sumr, s_norm, s_pt, s_ptc, s_pv = sem("sum_inverse"), sem("weights_ready"), sem("weights_ps"), sem("weights_copied"), sem("values_done")
        s_gated, s_out = sem("gated_inverse"), sem("heads_copied")

        def s_banks(i):
            return (pa, pb)[i % 2]

        CAUSAL = dict(e=t_e, rows=[(0, 0, P), (512, 2, TOK)], blocks=[(0, 0), (P, 512), (2 * P, P), (3 * P, 512 + TOK), (512, 512 + P), (512 + P, 512 + TOK + P)])
        WHOLE = dict(e=HM, rows=[(0, 0, 512)], blocks=[(b * P, b * P) for b in range(8)])

        def pair_rows(v, lo, w):
            return v[:, lo:lo + 2 * w].rearrange("p (u w) -> p u w", u=2)

        def att_tensor(pe, ph, sp):
            n0, n = ph.att0, ph.natt
            for i in range(n + 3):
                if i < n:
                    if i >= 2:
                        pe.wait_ge(s_exp, n0 + i - 1)
                    for dst, lhs, rhs in sp["scores"](i, s_banks(i)):
                        last = nc.tensor.matmul(dst, lhs, rhs, start=True, stop=True)
                    last.then_inc(s_done, 1)
                j = i - 2
                if 0 <= j < n:
                    pe.wait_ge(s_norm, n0 + j + 1)
                    if j >= 1:
                        pe.wait_ge(s_ptc, n0 + j)
                    for dst, src in sp["blocks"]:
                        last = nc.tensor.transpose(acc[:, 1, dst:dst + P], sp["e"][:, j % 2, src:src + P], ident[:, :])
                    last.then_inc(s_pt, 1)
                j = i - 3
                if j >= 0:
                    pe.wait_ge(s_ptc, n0 + j + 1)
                    done = j // sp["per_pair"]
                    if j % sp["per_pair"] == 0 and done:
                        pe.wait_ge(s_out, ph.out0 + ph.nout - n // sp["per_pair"] + done)
                    for dst, lhs, rhs, first, end in sp["values"](j, sp["pt"][:, j % 2, :]):
                        last = nc.tensor.matmul(dst, lhs, rhs, start=first, stop=end, skip_group_check=True)
                    last.then_inc(s_pv, 1)
                if sp["extra"]:
                    sp["extra"](pe, i)

        def att_scalar(act, ph, sp):
            n0, n = ph.att0, ph.natt
            w = len(sp["blocks"]) * P
            for i in range(n + 3):
                if i < n:
                    act.wait_ge(s_max, n0 + i + 1)
                    if i >= 2:
                        act.wait_ge(s_pt, n0 + i - 1)
                    flat = s_banks(i)[:, :, :].rearrange("p a c -> p (a c)")
                    for lo, k, width in sp["rows"]:
                        for u in range(2):
                            c = slice(lo + u * width, lo + (u + 1) * width)
                            last = nc.scalar.activation(sp["e"][:, i % 2, c], flat[:, c], ACT.Exp, bias=t_m[:, i % 2, k + u:k + u + 1],
                                                        accum_out=t_s[:, i % 2, k + u:k + u + 1])
                    last.then_inc(s_exp, 1)
                j = i - 2
                if 0 <= j < n:
                    act.wait_ge(s_pt, n0 + j + 1)
                    if j >= 2:
                        act.wait_ge(s_pv, n0 + j - 1)
                    nc.scalar.copy(sp["pt"][:, j % 2, 0:w], acc[:, 1, 0:w]).then_inc(s_ptc, 1)
                j = i - 3
                if j >= 0 and j % sp["per_pair"] == sp["per_pair"] - 1:
                    act.wait_ge(s_pv, n0 + j + 1)
                    nc.scalar.copy(sp["out"][:, j // sp["per_pair"], :], acc[:, 0, 0:TOK]).then_inc(s_out, 1)
                if sp["extra"]:
                    sp["extra"](act, i)

        def att_vector(dve, ph, sp):
            n0, n = ph.att0, ph.natt
            v = nc.vector
            for i in range(n + 1):
                if i < n:
                    dve.wait_ge(s_done, n0 + i + 1)
                    flat = s_banks(i)[:, :, :].rearrange("p a c -> p (a c)")
                    if sp["masked"]:
                        for lo, k, width in sp["rows"]:
                            x = pair_rows(flat, lo, width)[:, :, width - P:width]
                            last = v.tensor_tensor(x, x, bc(causal[:, :].unsqueeze(1), [P, 2, P]), ALU.add)
                        last.then_inc(s_masked, 1)
                        dve.wait_ge(s_masked, ph.masked0 + i + 1)
                    if i >= 2:
                        dve.wait_ge(s_exp, n0 + i - 1)
                    for lo, k, width in sp["rows"]:
                        last = v.tensor_reduce(t_m[:, i % 2, k:k + 2], pair_rows(flat, lo, width), AX.X, ALU.max, negate=True)
                    last.then_inc(s_max, 1)
                j = i - 1
                if j >= 0:
                    dve.wait_ge(s_exp, n0 + j + 1)
                    sums = t_s[:, j % 2, 0:2 * len(sp["rows"])]
                    v.reciprocal(sums, sums).then_inc(s_sumr, 1)
                    dve.wait_ge(s_sumr, n0 + j + 1)
                    if sp["gate"]:
                        sums = sums.rearrange("p (t u) -> p t u", u=2)
                        v.tensor_tensor(sums, sums, sp["gate"](j), ALU.mult).then_inc(s_gated, 1)
                        dve.wait_ge(s_gated, j + 1)
                    for lo, k, width in sp["rows"]:
                        x = pair_rows(sp["e"][:, j % 2, :], lo, width)
                        last = v.tensor_tensor(x, x, bc(t_s[:, j % 2, k:k + 2].unsqueeze(2), [P, 2, width]), ALU.mult)
                    last.then_inc(s_norm, 1)

        def out_tensor(pe, ph, q0):
            pe.wait_ge(s_out, ph.out0 + ph.nout)
            for t in range(TT):
                for c in range(KC):
                    if t == 0 and c % 4 == 0:
                        slot_wait(pe, q0 + c // 4)
                    w = ring[:, (q0 + c // 4) % RING, :].rearrange("p (k c) -> p k c", k=4)[:, c % 4, :]
                    for h in range(2):
                        last = nc.tensor.matmul(acc[:, t, h * 512:(h + 1) * 512], XT[:, c, t * P:(t + 1) * P], w[:, h * 512:(h + 1) * 512],
                                                start=(c == 0), stop=(c == KC - 1))
                    if c == 3 and t == 1:
                        last.then_inc(freed, 1)
                if t == 0:
                    last.then_inc(mix_done, 1)
            last.then_inc(freed, 1)
            pe.wait_ge(freed, q0 + 2)
            pe.sem_inc(mix_done, 1)

        NH, HD, NKV = 16, 64, 4
        NKEY = 2 * TOK
        area = Area(work)
        g_cx = area.take(TT, D)
        g_k = work[:, 0:2048].rearrange("p (t j u e) -> p t j u e", t=4, j=NKV, u=2)
        g_hct = area.take(KC, TOK)
        g_q = g_hct
        g_v = area.take(4, NKV * HD)
        g_tmp = area.take(D)
        area.at = 8480
        g_root = area.take(48)
        g_turn = area.take(TT, 2, 2, 2, HD // 2)
        g_rope = rope[:, :].rearrange("p (t s a e) -> p t s a e", t=TT, s=2, a=2)
        g_kte = work[:, 9200:11248].rearrange("p (j t) -> p j t", j=NKV)
        g_kto = work[:, 6144:8192].rearrange("p (j t) -> p j t", j=NKV)
        cx_loaded, cx_var, cx_rstd, cx_normed = sem("context_loaded"), sem("context_squares"), sem("context_rstd"), sem("context_normed")
        cx_ready, kt_cleared, q_copied = sem("context_ready"), sem("keys_cleared"), sem("q_copied")
        g_sq = [g_tmp, XT[:, 4:8, :].rearrange("p k c -> p (k c)")]
        q_squared = sem("queries_squared")
        qk_var, qk_root = sem("qk_squares"), sem("qk_roots")
        qk_ready, qkt_ps, qkt_copied = sem("qk_ready"), sem("qkt_ps"), sem("qkt_copied")

        G_EARLY = 3

        def gqa_spec(extra=None):
            def scores(i, banks):
                pair, t = i // TT, i % TT
                for u, keys in enumerate((g_kte, g_kto)):
                    yield banks[:, u, :], g_q[:, pair, t * P:(t + 1) * P], keys[:, 2 * pair // (NH // NKV), :]

            def values(i, weights):
                pair, t = i // TT, i % TT
                j = 2 * pair // (NH // NKV)
                for b in range(4):
                    for u in range(2):
                        yield (acc[u * HD:(u + 1) * HD, 0, t * P:(t + 1) * P], g_v[:, b, j * HD:(j + 1) * HD],
                               weights[:, (4 * u + b) * P:(4 * u + b + 1) * P], b == 0, b == 3)
            return dict(WHOLE, scores=scores, values=values, masked=False, gate=None, per_pair=TT, extra=extra, out=XT,
                        pt=work[:, 0:2048].rearrange("p (a c) -> p a c", a=2))

        def gqa_sync(sp, ph):
            stream_sync(sp, a["attn_w_qkv_2"][0], ph.slot0, 4, 2, D + 2 * NKV * HD)
            w_mod_sync(sp, ph, 1)
            stream_sync(sp, a["attn_w_o_2"][0], ph.slot_mod + MODC, 2, 4, D)

        def gqa_pool(pool, ph):
            tile_pows(pool, RMS_EPS)
            pool.wait_ge(cx_ready, 1)
            pool.wait_ge(row_ps, ph.rows0)
            nc.gpsimd.memset(g_kte[HD:P, :, :], 0.0).then_inc(kt_cleared, 1)
            pool.wait_ge(kt_cleared, 1)
            nc.gpsimd.memset(g_kto[0:HD, :, :], 0.0).then_inc(kt_cleared, 1)
            pool.wait_ge(kt_cleared, 2)
            rows_pool(pool, 1, G_EARLY)
            next_router_pool(pool, ph)

        def gqa_tensor(pe, ph):
            transpose_tensor(pe, HM, ph)
            pe.wait_ge(cx_ready, 1)
            pe.wait_ge(xt_ready, 2 * (ph.xt + 1))
            transpose_tensor(pe, g_cx)
            pe.wait_ge(xt_ready, 2 * (ph.xt + 2))
            for k in range(KC):
                q = ph.slot0 + k // 2
                if k % 2 == 0:
                    slot_wait(pe, q)
                w = ring[:, q % RING, 0:3072].rearrange("p (k c) -> p k c", k=2)[:, k % 2, :]
                for t in range(TT):
                    fl = dict(start=(k == 0), stop=(k == KC - 1))
                    lat = XT[:, k, t * P:(t + 1) * P]
                    for h in range(2):
                        nc.tensor.matmul(acc[:, t, h * 512:(h + 1) * 512], lat, w[:, h * 512:(h + 1) * 512], **fl)
                    nc.tensor.matmul(pa[:, t, :], lat, w[:, D:D + 512], **fl)
                    last = nc.tensor.matmul(pb[:, t, :], g_hct[:, k, t * P:(t + 1) * P], w[:, D:D + 512], **fl)
                if k % 2:
                    last.then_inc(freed, 1)
            pe.wait_ge(q_copied, TT)
            for n in range(G_EARLY):
                block_tensor(pe, ph, 1, n, G_EARLY)
            pe.wait_ge(part_copied, MODC + G_EARLY)
            for t in range(TT):
                pe.wait_ge(qk_ready, t + 1)
                for c in range(KC):
                    last = nc.tensor.transpose(acc[:, c // 4, (c % 4) * TOK + t * P:(c % 4) * TOK + (t + 1) * P],
                                               HM[:, t, c * P:(c + 1) * P], ident[:, :])
            pe.wait_ge(qk_ready, TT + 1)
            for j in range(NKV):
                for t in range(4):
                    last = nc.tensor.transpose((pa, pb)[j // 2][:, j % 2, t * P:(t + 1) * P],
                                               work[:, (t * NKV + j) * P:(t * NKV + j + 1) * P], ident[:, :])
            last.then_inc(qkt_ps, 1)
            pe.wait_ge(qkt_copied, 2)
            pe.wait_ge(kt_cleared, 2)
            att_tensor(pe, ph, gqa_spec(between(block_tensor, ph, 1, G_EARLY)))
            out_tensor(pe, ph, ph.slot_mod + MODC)

        def gqa_scalar(act, ph):
            transpose_scalar(act, ph.xt, XT)
            transpose_scalar(act, ph.xt + 1, g_hct)
            act.wait_ge(small, ph.small)
            cond_scalar(act, ph, 1)
            act.wait_ge(freed, ph.slot0 + 4)
            for t in range(TT):
                nc.scalar.activation(g_sq[t], acc[:, t, :], ACT.Square).then_inc(q_squared, 1)
                nc.scalar.copy(HM[:, t, :], acc[:, t, :]).then_inc(q_copied, 1)
            for n in range(G_EARLY):
                block_scalar(act, ph, 1, n, G_EARLY)
                if n == 0:
                    act.wait_ge(qk_var, 1)
                    nc.scalar.activation(g_root, stat[:, 0:48], ACT.Sqrt).then_inc(qk_root, 1)
            for n in (G_EARLY - 2, G_EARLY - 1):
                act.wait_ge(rows_moved[n % 2], rows_count(1, n))
            act.wait_ge(qkt_ps, 1)
            nc.scalar.mul(g_q[:, 0:4, :], acc[:, 0, :].rearrange("p (k c) -> p k c", c=TOK), HD ** -0.5)
            nc.scalar.copy(g_kte[0:HD, 0:2, :], pa[0:HD, :, :])
            nc.scalar.copy(g_kto[HD:P, 0:2, :], pa[HD:P, :, :]).then_inc(qkt_copied, 1)
            att_scalar(act, ph, gqa_spec(between(block_scalar, ph, 1, G_EARLY)))

        def gqa_vector(dve, ph, link):
            v = nc.vector
            cond_vector(dve, 1)
            dve.wait_ge(small, ph.small)
            dve.wait_ge(row_copied, ph.rows0 - MODC + N_SHIFT_SCALE)
            link(v.scalar_tensor_tensor(shift[:, :], mod_of(1), 1.0, early[:, :], ALU.add, ALU.mult))
            link(v.scalar_tensor_tensor(c_mod[:, D:], c_mod[:, D:], 1.0, early[:, :], ALU.add, ALU.mult))
            for t in range(TT):
                modulate_vector(dve, link, 0, t, TT * (ph.h - 1) + t + 1)
            dve.wait_ge(cx_normed, TT)
            for t in range(TT):
                link(v.tensor_tensor(g_cx[:, t, :], g_cx[:, t, :], c_mod[:, D:], ALU.mult))
                link(v.tensor_tensor(g_cx[:, t, :], g_cx[:, t, :], c_mod[:, 0:D], ALU.add))
            dve.sem_inc(cx_ready, 1)
            transpose_vector(dve, ph.xt, XT)
            transpose_vector(dve, ph.xt + 1, g_hct)
            for w in range(2):
                for c in range(2):
                    for u in range(2):
                        g = hgain[:, w, :].rearrange("p (a u e) -> p a u e", a=2, u=2)[:, :, u, :]
                        link(v.tensor_tensor(g_turn[:, :, w, c, u, :].rearrange("p t (a e) -> p t a e", a=2), g_rope[:, :, c, :, :],
                                             bc(g.unsqueeze(1), [P, TT, 2, 16]), ALU.mult))
            dve.wait_ge(freed, ph.slot0 + 4)
            for i, bank in enumerate((pa, pb)):
                link(v.tensor_copy(g_v[:, 2 * i:2 * i + 2, :], bank[:, :, 256:512]))
                link(v.tensor_copy(g_k[:, 2 * i:2 * i + 2, :, 0, :], bank[:, :, 0:256].rearrange("p t (j e) -> p t j e", j=NKV)))
            keys = work[:, 0:2048].rearrange("p (n u e) -> p n u e", u=2, e=HD)[:, :, 0, :]
            for t in range(TT):
                dve.wait_ge(q_squared, t + 1)
                link(v.tensor_reduce(stat[:, 16 * t:16 * t + 16], g_sq[t].rearrange("p (h e) -> p h e", e=HD), AX.X, ALU.add))
            sq = g_sq[0].rearrange("p (h e) -> p h e", e=HD)
            link(v.tensor_tensor(sq, keys, keys, ALU.mult))
            link(v.tensor_reduce(stat[:, 32:48], sq, AX.X, ALU.add))
            link(v.tensor_scalar(stat[:, 0:48], stat[:, 0:48], 1.0 / HD, RMS_EPS, ALU.mult, ALU.add))
            dve.sem_inc(qk_var, 1)
            dve.wait_ge(qk_root, 1)
            rs, x = g_root, stat[:, 0:48]
            link(v.reciprocal(rs, rs))
            link(v.tensor_tensor(x, x, rs, ALU.mult))
            link(v.tensor_tensor(x, x, rs, ALU.mult))
            link(v.tensor_scalar(x, x, -0.5, 1.5, ALU.mult, ALU.add))
            link(v.tensor_tensor(x, x, rs, ALU.mult))

            def rotate(x, t, w):
                n = x.shape[1]
                x5 = x.rearrange("p h (a u e) -> p h a u e", a=2, u=2)
                x1, x2 = x5[:, :, :, 0, :], x5[:, :, :, 1, :]
                turn = [[bc(g_turn[:, t, w, c, u, :].rearrange("p (a e) -> p a e", a=2).unsqueeze(1), [P, n, 2, 16]) for u in range(2)] for c in range(2)]
                u1, u2 = (g_tmp[:, o:o + 32 * n].rearrange("p (h a e) -> p h a e", h=n, a=2) for o in (0, 512))
                link(v.tensor_tensor(u1, x1, turn[1][0], ALU.mult))
                link(v.tensor_tensor(u2, x2, turn[1][1], ALU.mult))
                link(v.tensor_tensor(x1, x1, turn[0][0], ALU.mult))
                link(v.tensor_tensor(x2, x2, turn[0][1], ALU.mult))
                link(v.tensor_tensor(x1, x1, u2, ALU.subtract))
                link(v.tensor_tensor(x2, x2, u1, ALU.add))
            for t in range(TT):
                dve.wait_ge(q_copied, t + 1)
                x = HM[:, t, :].rearrange("p (h e) -> p h e", e=HD)
                link(v.tensor_tensor(x, x, bc(stat[:, 16 * t:16 * t + 16].unsqueeze(2), [P, 16, HD]), ALU.mult))
                rotate(x, t, 0)
                dve.sem_inc(qk_ready, 1)
            link(v.tensor_tensor(keys, keys, bc(stat[:, 32:48].unsqueeze(2), [P, 16, HD]), ALU.mult))
            for t in range(TT):
                rotate(keys[:, t * NKV:(t + 1) * NKV, :], t, 1)
            own = keys[:, TT * NKV:, :]
            link(v.tensor_tensor(own, own, bc(hgain[:, 1, :].unsqueeze(1), [P, TT * NKV, HD]), ALU.mult))
            link(v.tensor_copy(work[:, 0:2048].rearrange("p (n u e) -> p n u e", u=2, e=HD)[:, :, 1, :], keys))
            dve.sem_inc(qk_ready, 1)
            dve.wait_ge(qkt_ps, 1)
            v.tensor_scalar(g_q[:, 4:8, :], acc[:, 1, :].rearrange("p (k c) -> p k c", c=TOK), HD ** -0.5, None, ALU.mult)
            v.tensor_copy(g_kte[0:HD, 2:4, :], pb[0:HD, :, :])
            v.tensor_copy(g_kto[HD:P, 2:4, :], pb[HD:P, :, :]).then_inc(qkt_copied, 1)
            att_vector(dve, ph, gqa_spec())
            mixed_vector(dve, ph, link)

        GD = D // 4
        area = Area(work)
        f_tab = early[:, :].rearrange("p (t s n) -> p t s n", t=TT, s=2)
        f_a = area.take(KC, 2 * TOK)
        f_loaded = sem("dft_tables_loaded")
        f_ps, f_done = sem("dft_ps"), sem("dft_done")
        f_copied = [sem(f"dft_copied{i}") for i in range(2)]

        def fourier_sync(sp, ph):
            stream_sync(sp, a["fourier_w_o_2"][0], ph.slot0, 2, 4, D)

        def ahead_pool(pool, ph):
            if plan[ph.i + 1].layer == 0:
                pool.wait_ge(phase_done, ph.i)
                pool.dma_start(HM[:, :, :], a["ctx_2"][0].rearrange("(t p) d -> p t d", p=P)).then_inc(cx_loaded, 16)
            else:
                pool.wait_ge(cx_ready, 1)
                pool.dma_start(early[:, :].rearrange("p (t n) -> p t n", t=TT), a["dft"].rearrange("(t p) n -> p t n", p=P)).then_inc(f_loaded, 16)
                gain_pool(pool, plan[ph.i + 2].ln, a["norm_mix_2"][1])

        def context_pow(pool):
            pool.wait_ge(cx_var, TT)
            cx = stat[:, 34:34 + TT]
            nc.gpsimd.tensor_scalar(cx, cx, RMS_EPS, None, ALU.add).then_inc(cx_rstd, 1)
            pool.wait_ge(cx_rstd, 1)
            nc.gpsimd.tensor_tensor(cx, cx, half[:, 0:TT], ALU.pow).then_inc(cx_rstd, 1)

        def fourier_pool(pool, ph):
            next_router_pool(pool, ph)
            tile_pows(pool, RMS_EPS)

        def fourier_tensor(pe, ph):
            input_wait(pe, ph)
            pe.wait_ge(f_loaded, 16)
            for c in range(KC):
                if c >= 4:
                    pe.wait_ge(f_copied[c % 2], c // 2 - 1)
                for t in range(TT):
                    last = nc.tensor.matmul((pa, pb)[c // 2 % 2][:, c % 2, :], HM[:, t, c * P:(c + 1) * P], f_tab[:, t, :, :],
                                            start=(t == 0), stop=(t == 1))
                last.then_inc(f_ps, 1)
            for i in range(2):
                pe.wait_ge(f_copied[i], KC // 2)
            for c in range(KC):
                g = c // 2
                for i in range(2):
                    for s in range(2):
                        last = nc.tensor.matmul(acc[:, c // 4, (c % 4) * TOK:(c % 4 + 1) * TOK], f_tab[:, i, s, (c % 2) * P:(c % 2 + 1) * P],
                                                f_a[:, 2 * g + i, s * TOK:(s + 1) * TOK], start=(i + s == 0), stop=(i + s == 2))
            last.then_inc(f_done, 1)
            out_tensor(pe, ph, ph.slot0)

        def fourier_scalar(act, ph):
            for c in range(1, KC, 2):
                act.wait_ge(f_ps, c + 1)
                ps = (pa, pb)[c // 2 % 2][:, c % 2, :]
                nc.scalar.copy(f_a[:, c, 0:TOK], ps[:, 0:TOK])
                nc.scalar.mul(f_a[:, c, TOK:], ps[:, TOK:], -1.0).then_inc(f_copied[1], 1)
            act.wait_ge(f_done, 1)
            nc.scalar.copy(XT[:, 0:4, :], acc[:, 0, :].rearrange("p (k c) -> p k c", c=TOK)).then_inc(s_out, 1)

        def fourier_vector(dve, ph, link):
            v = nc.vector
            dve.wait_ge(row_copied, ph.rows0 - MODC + N_SHIFT_SCALE)
            scale_vector(dve, ph.ln, link, 0)
            for t in range(TT):
                modulate_vector(dve, link, 0, t, TT * (ph.h - 1) + t + 1)
            for c in range(0, KC, 2):
                dve.wait_ge(f_ps, c + 1)
                ps = (pa, pb)[c // 2 % 2][:, c % 2, :]
                v.tensor_copy(f_a[:, c, 0:TOK], ps[:, 0:TOK])
                v.tensor_scalar(f_a[:, c, TOK:], ps[:, TOK:], -1.0, None, ALU.mult).then_inc(f_copied[0], 1)
            dve.wait_ge(f_done, 1)
            v.tensor_copy(XT[:, 4:8, :], acc[:, 1, :].rearrange("p (k c) -> p k c", c=TOK)).then_inc(s_out, 1)
            mixed_vector(dve, ph, link)

        NM, NOPE, ROPE, MV = 8, 64, 32, 64
        HQ = NOPE + ROPE
        GW = D // 2
        NGM = GW // P
        QR, KVR = D // 4, D // 8
        LAT = QR + KVR + ROPE
        AB_IN = 2 * GW + LAT
        wide = Area(mod)
        b_q = wide.take(TT, NM, HQ)
        b_k = wide.take(TT, NM, HQ)
        b_u = wide.take(NGM, TOK)
        b_v = wide.take(TT, GW)
        b_latt = wide.take(3, TOK)
        area = Area(work)
        b_qt = area.take(NM, TOK)
        b_kt = area.take(NM, TOK)
        b_wuq = area.take(2, NM * HQ)
        b_bs = area.take(NGM, P)
        area.at = 8720
        b_wst = area.take(NGM, P)
        b_vals = area.take(TT, NM * MV)
        b_qg = area.take(QR)
        b_kvg = area.take(KVR)
        b_kr = area.take(TT, ROPE)
        b_cos = area.take(TT, ROPE // 2)
        b_sin = area.take(TT, ROPE // 2)
        b_ang = area.take(2, TT, ROPE // 2)
        b_turn = area.take(2, TT, ROPE // 2)
        b_freq = area.take(ROPE // 2)
        b_pos = area.take(TT)
        hm = Area(HM[:, :, :].rearrange("p t d -> p (t d)"))
        b_lat = hm.take(TT, LAT)
        b_wuk = hm.take(NM * NOPE)
        b_wuv = hm.take(NM * MV)
        b_posi = hm.take(TT).bitcast(I32)
        area = Area(work)
        area.at = 6144
        b_rot = area.take(2, 512)
        b_ws = area.take(NGM, P)
        b_mask = area.take(P)
        B_SMALL = 11
        b_small = sem("mla_small_loaded")
        pad_cleared = sem("padding_cleared")
        ws_ps, ws_ready = sem("mixing_t_ps"), sem("mixing_ready")
        ang_ready, trig_ready, gelu_ready = sem("angles_ready"), sem("trig_ready"), sem("gelu_ready")
        vn_ready, gm_ps, gm_read = sem("gmlp_normed"), sem("gmlp_ps"), sem("gmlp_read")
        lat_ready, latt_ps, latt_copied = sem("latents_ready"), sem("latents_t_ps"), sem("latents_t_copied")
        up_done, up_copied = sem("up_done"), sem("up_copied")
        b_qk, b_qkt, b_qktc = sem("mla_qk_ready"), sem("mla_qkt_ps"), sem("mla_qkt_copied")
        TWO_PI = (6.28125, 1.93500518798828125e-3, 3.0198368e-7)
        MAGIC = 1.5 * 2.0 ** 23

        def ab_spec():
            def scores(i, banks):
                for t in range(TT):
                    for u in range(2):
                        w = (t + 1) * P
                        yield banks[:, t, u * w:(u + 1) * w], b_qt[:, 2 * i + u, t * P:(t + 1) * P], b_kt[:, 2 * i + u, 0:w]

            def values(i, weights):
                for t in range(TT):
                    for u in range(2):
                        w = TOK - t * P
                        yield (acc[u * MV:(u + 1) * MV, 0, t * P:TOK], b_vals[:, t, (2 * i + u) * MV:(2 * i + u + 1) * MV],
                               weights[:, t * 512 + u * w:t * 512 + (u + 1) * w], t == 0, t == 1)
            return dict(CAUSAL, scores=scores, values=values, masked=True, gate=None, per_pair=1, extra=None, out=XT[:, NGM:KC, :],
                        pt=work[:, 4096:6144].rearrange("p (a c) -> p a c", a=2))

        def ab_sync(sp, ph):
            stream_sync(sp, a["ab_w_in"][0], ph.slot0, 4, 2, AB_IN)
            stream_sync(sp, a["ab_w_o"][0], ph.slot0 + 4, 2, 4, D)

        def ab_pool(pool, ph):
            pool.wait_ge(consts, CONSTS)
            nc.gpsimd.memset(b_qt[HQ:P, :, :], 0.0).then_inc(pad_cleared, 1)
            pool.wait_ge(pad_cleared, 1)
            nc.gpsimd.memset(b_kt[HQ:P, :, :], 0.0).then_inc(pad_cleared, 1)
            pool.wait_ge(pad_cleared, 2)
            pow_pool(pool, slice(2, 6))
            pow_pool(pool, slice(0, 2))
            pool.wait_ge(vn_ready, 1)
            gain_pool(pool, ph.ln, a["ln1_g"][0], a["ln1_b"][0])
            next_router_pool(pool, ph)
            tile_pows(pool, None)

        def ab_tensor(pe, ph):
            transpose_tensor(pe, X, ph)
            pe.wait_ge(xt_ready, 2 * (ph.xt + 1))
            for k in range(KC):
                q = ph.slot0 + k // 2
                if k % 2 == 0:
                    slot_wait(pe, q)
                w = ring[:, q % RING, 0:2 * AB_IN].rearrange("p (k c) -> p k c", k=2)[:, k % 2, :]
                fl = dict(start=(k == 0), stop=(k == KC - 1), skip_group_check=True)
                for m in range(NGM):
                    nc.tensor.matmul(pa[:, m // 2, (m % 2) * TOK:(m % 2 + 1) * TOK], w[:, m * P:(m + 1) * P], XT[:, k, :],
                                     start=(k == 0 and m % 2 == 0), stop=(k == KC - 1), skip_group_check=True)
                for t in range(TT):
                    lat = XT[:, k, t * P:(t + 1) * P]
                    nc.tensor.matmul(acc[:, t, 0:GW], lat, w[:, GW:2 * GW], **fl)
                    last = nc.tensor.matmul(acc[:, t, 512:512 + LAT], lat, w[:, 2 * GW:AB_IN], **fl)
                if k % 2:
                    last.then_inc(freed, 1)
                if k == KC - 2:
                    pe.wait_ge(b_small, 16 * B_SMALL)
                    for g in range(NGM):
                        last = nc.tensor.transpose(pb[:, 1, g * P:(g + 1) * P], b_ws[:, g, :], ident[:, :])
                    last.then_inc(ws_ps, 1)
            pe.wait_ge(ws_ready, 1)
            pe.wait_ge(lat_ready, 1)
            flat = pb[:, :, :].rearrange("p a c -> p (a c)")
            for c in range(3):
                for t in range(TT):
                    last = nc.tensor.transpose(flat[:, c * TOK + t * P:c * TOK + (t + 1) * P], b_lat[:, t, c * P:(c + 1) * P], ident[:, :])
            last.then_inc(latt_ps, 1)
            pe.wait_ge(latt_copied, 1)
            for t in range(TT):
                for h in range(2):
                    for c in range(2):
                        nc.tensor.matmul(acc[:, t, 512 * h:512 * h + NM * HQ // 2], b_latt[:, c, t * P:(t + 1) * P],
                                         b_wuq[:, c, h * NM * HQ // 2:(h + 1) * NM * HQ // 2], start=(c == 0), stop=(c == 1))
                nc.tensor.matmul(pb[:, t, :], b_latt[:, 2, t * P:(t + 1) * P], b_wuk, start=True, stop=True)
            pe.wait_ge(vn_ready, 1)
            for g in range(NGM):
                for n in range(TT):
                    last = nc.tensor.matmul(pa[:, g // 2, (g % 2) * TOK + n * P:(g % 2) * TOK + (n + 1) * P],
                                            b_v[:, n, g * P:(g + 1) * P], b_wst[:, g, :], start=True, stop=True)
            last.then_inc(gm_ps, 1)
            pe.wait_ge(gm_read, 1)
            for t in range(TT):
                last = nc.tensor.matmul(pa[:, t, :], b_latt[:, 2, t * P:(t + 1) * P], b_wuv, start=True, stop=True)
            last.then_inc(up_done, 1)
            pe.wait_ge(b_qk, 1)
            for h in range(NM):
                for t in range(TT):
                    at = (h % 4) * TOK + t * P
                    nc.tensor.transpose(acc[0:HQ, h // 4, at:at + P], b_q[:, t, h, :], ident[:, :])
                    at = (h % 2) * TOK + t * P
                    last = nc.tensor.transpose((pa, pb)[h // 4][0:HQ, h // 2 % 2, at:at + P], b_k[:, t, h, :], ident[:, :])
            last.then_inc(b_qkt, 1)
            pe.wait_ge(b_qktc, 2)
            pe.wait_ge(pad_cleared, 2)
            att_tensor(pe, ph, ab_spec())
            out_tensor(pe, ph, ph.slot0 + 4)

        def ab_scalar(act, ph):
            for dst, src in (
                    (b_posi, a["pos_cols"]), (b_freq, a["freqs"][0].partition_broadcast(P)),
                    (b_ws, a["ab_gm_ws"][0].rearrange("g t s -> t g s")),
                    (b_wuq, a["ab_mla_w_uq"][0].rearrange("(c p) n -> p c n", p=P)),
                    (b_wuk, a["ab_mla_w_uk"][0]), (b_wuv, a["ab_mla_w_uv"][0]),
                    (b_qg, a["ab_mla_q_norm"][0].partition_broadcast(P)), (b_kvg, a["ab_mla_kv_norm"][0].partition_broadcast(P)),
                    (b_bs, a["ab_gm_bs"][0].partition_broadcast(P))):
                act.dma_start(dst, src).then_inc(b_small, 16)
            act.dma_start(gain[:, 0:GW], a["ab_gm_ln_g"][0].partition_broadcast(P)).then_inc(b_small, 16)
            act.dma_start(gain[:, GW:D], a["ab_gm_ln_b"][0].partition_broadcast(P)).then_inc(b_small, 16)
            transpose_scalar(act, ph.xt, XT)
            act.wait_ge(ang_ready, 1)
            nc.scalar.activation(b_sin, b_ang[:, 0, :, :], ACT.Sin)
            nc.scalar.activation(b_cos, b_ang[:, 1, :, :], ACT.Sin).then_inc(trig_ready, 1)
            act.wait_ge(freed, ph.slot0 + 4)
            for t in range(TT):
                nc.scalar.activation(b_v[:, t, :], acc[:, t, 0:GW], ACT.Gelu_apprx_tanh)
            nc.scalar.activation(b_u, pa[:, :, :].rearrange("p a (m c) -> p (a m) c", m=2), ACT.Gelu_apprx_tanh).then_inc(gelu_ready, 1)
            act.wait_ge(latt_ps, 1)
            nc.scalar.copy(b_latt, pb[:, :, :].rearrange("p a (m c) -> p (a m) c", m=2)[:, 0:3, :]).then_inc(latt_copied, 1)
            act.wait_ge(up_done, 1)
            for t in range(TT):
                nc.scalar.copy(b_q[:, t, :, :].rearrange("p (a h) e -> p a (h e)", a=2),
                               acc[:, t, :].rearrange("p (a c) -> p a c", a=2)[:, :, 0:NM * HQ // 2])
            nc.scalar.copy(b_vals, pa[:, :, :]).then_inc(up_copied, 1)
            act.wait_ge(b_qkt, 1)
            for i in range(2):
                last = nc.scalar.mul(b_qt[0:HQ, 4 * i:4 * i + 4, :], acc[0:HQ, i, :].rearrange("p (h c) -> p h c", c=TOK), HQ ** -0.5)
            last.then_inc(b_qktc, 1)
            att_scalar(act, ph, ab_spec())

        def ab_vector(dve, ph, link):
            v = nc.vector
            transpose_vector(dve, ph.xt, XT)
            dve.wait_ge(b_small, 16 * B_SMALL)
            link(v.tensor_copy(b_pos, b_posi))
            for i in range(2):
                link(v.tensor_tensor(b_ang[:, i, :, :], bc(b_pos.unsqueeze(2), [P, TT, ROPE // 2]), bc(b_freq.unsqueeze(1), [P, TT, ROPE // 2]), ALU.mult))
            link(v.tensor_scalar(b_turn[:, 0, :, :], b_ang[:, 0, :, :], 1 / (2 * np.pi), MAGIC, ALU.mult, ALU.add))
            link(v.tensor_scalar(b_turn[:, 1, :, :], b_ang[:, 1, :, :], 1 / (2 * np.pi), 0.25, ALU.mult, ALU.add))
            link(v.tensor_scalar(b_turn[:, 1, :, :], b_turn[:, 1, :, :], MAGIC, None, ALU.add))
            link(v.tensor_scalar(b_turn, b_turn, MAGIC, None, ALU.subtract))
            for part in TWO_PI:
                link(v.scalar_tensor_tensor(b_ang.rearrange("p i t e -> p (i t e)"), b_turn.rearrange("p i t e -> p (i t e)"), -part,
                                            b_ang.rearrange("p i t e -> p (i t e)"), ALU.mult, ALU.add))
            link(v.tensor_scalar(b_ang[:, 1, :, :], b_ang[:, 1, :, :], float(np.pi / 2), None, ALU.add))
            link(v.tensor_scalar(b_ang, b_ang, 3.1415925, -3.1415925, ALU.min, ALU.max))
            dve.sem_inc(ang_ready, 1)
            link(v.tensor_tensor(b_mask, before[:, :], ident[:, :], ALU.add))
            dve.wait_ge(ws_ps, 1)
            link(v.tensor_tensor(b_wst, pb[:, 1, :].rearrange("p (g t) -> p g t", g=NGM), bc(b_mask.unsqueeze(1), [P, NGM, P]), ALU.mult))
            dve.sem_inc(ws_ready, 1)
            dve.wait_ge(freed, ph.slot0 + 4)
            for t in range(TT):
                last = v.tensor_copy(b_lat[:, t, :], acc[:, t, 512:512 + LAT])
            link(last)
            junk = b_rot
            for t in range(TT):
                for lo, n, col in ((0, QR, 2), (QR, KVR, 4)):
                    x = b_lat[:, t, lo:lo + n]
                    link(v.tensor_tensor_reduce(out=junk[:, t, 0:n], in0=x, in1=x, scale=1.0 / n, scalar=0.0,
                                                op0=ALU.mult, op1=ALU.add, accum_out=stat[:, col + t:col + t + 1]))
            v.tensor_scalar(stat[:, 2:6], stat[:, 2:6], LN_EPS, None, ALU.add).then_inc(var_ready, 1)
            rstd_wait(dve)
            for t in range(TT):
                for lo, n, col in ((0, QR, 2), (QR, KVR, 4)):
                    x = b_lat[:, t, lo:lo + n]
                    link(v.scalar_tensor_tensor(x, x, stat[:, col + t:col + t + 1], b_qg if lo == 0 else b_kvg, ALU.mult, ALU.mult))
            dve.sem_inc(lat_ready, 1)
            dve.wait_ge(gelu_ready, 1)
            for t in range(TT):
                last = v.bn_stats(stat[:, 8 + 6 * t:14 + 6 * t], b_v[:, t, :])
            link(last)
            for t in range(TT):
                last = v.bn_aggr(stat[:, 24 + 2 * t:26 + 2 * t], stat[:, 8 + 6 * t:14 + 6 * t])
            link(last)
            mv = stat[:, 24:28].rearrange("p (t s) -> p t s", s=2)
            v.tensor_scalar(stat[:, 0:2], mv[:, :, 1], LN_EPS, None, ALU.add).then_inc(var_ready, 1)
            rstd_wait(dve)
            for t in range(TT):
                last = v.tensor_scalar(b_v[:, t, :], b_v[:, t, :], mv[:, t, 0:1], stat[:, t:t + 1], ALU.subtract, ALU.mult)
            link(last)
            link(v.tensor_tensor(b_v, b_v, bc(gain[:, 0:GW].unsqueeze(1), [P, TT, GW]), ALU.mult))
            link(v.tensor_tensor(b_v, b_v, bc(gain[:, GW:D].unsqueeze(1), [P, TT, GW]), ALU.add))
            dve.sem_inc(vn_ready, 1)
            dve.wait_ge(trig_ready, 1)

            def rotate(dst1, dst2, x1, x2, cos, sin, u1, u2):
                link(v.tensor_tensor(u1, x1, sin, ALU.mult))
                link(v.tensor_tensor(u2, x2, sin, ALU.mult))
                link(v.tensor_tensor(dst1, x1, cos, ALU.mult))
                link(v.tensor_tensor(dst2, x2, cos, ALU.mult))
                link(v.tensor_tensor(dst1, dst1, u2, ALU.subtract))
                link(v.tensor_tensor(dst2, dst2, u1, ALU.add))
            R2 = ROPE // 2
            x = b_lat[:, :, QR + KVR:LAT]
            u = [b_rot[:, i, 0:TT * R2].rearrange("p (t e) -> p t e", t=TT) for i in range(2)]
            rotate(b_kr[:, :, 0:R2], b_kr[:, :, R2:], x[:, :, 0:R2], x[:, :, R2:], b_cos, b_sin, *u)
            dve.wait_ge(gm_ps, 1)
            y = XT[:, 0:NGM, :]
            link(v.tensor_tensor(y.rearrange("p g (n t) -> p g n t", n=TT), pa[:, :, :].rearrange("p a (m n t) -> p (a m) n t", m=2, n=TT),
                                 bc(b_bs.unsqueeze(2), [P, NGM, TT, P]), ALU.add))
            dve.sem_inc(gm_read, 1)
            link(v.tensor_tensor(y, y, b_u, ALU.mult))
            dve.sem_inc(s_out, 1)
            dve.wait_ge(up_done, 1)
            for t in range(TT):
                link(v.tensor_copy(b_k[:, t, :, 0:NOPE], pb[:, t, :].rearrange("p (h e) -> p h e", e=NOPE)))
            link(v.tensor_copy(b_k[:, :, :, NOPE:HQ], bc(b_kr.unsqueeze(2), [P, TT, NM, ROPE])))
            dve.wait_ge(up_copied, 1)
            x1, x2 = b_q[:, :, :, NOPE:NOPE + R2], b_q[:, :, :, NOPE + R2:HQ]
            u = [b_rot[:, i, 0:TT * NM * R2].rearrange("p (t h e) -> p t h e", t=TT, h=NM) for i in range(2)]
            cs = [bc(z.unsqueeze(2), [P, TT, NM, R2]) for z in (b_cos, b_sin)]
            rotate(x1, x2, x1, x2, *cs, *u)
            dve.sem_inc(b_qk, 1)
            dve.wait_ge(b_qkt, 1)
            for i, bank in enumerate((pa, pb)):
                last = v.tensor_copy(b_kt[0:HQ, 4 * i:4 * i + 4, :], bank[0:HQ, :, :].rearrange("p a (h c) -> p (a h) c", h=2))
            last.then_inc(b_qktc, 1)
            att_vector(dve, ph, ab_spec())
            ln_vector(dve, ph, link, mixed=True)

        SH, SG, SD = 16, 2, 64
        CL, CS = 32, 16
        NB = TOK // CS - CL // CS + 1
        HID = 256
        SQ = SH * SD
        C_IN = SQ + 6 * SG * SD + 3 * SH
        CC = CL * SD // P
        VW = 3 * P + 3 * SH
        wide = Area(mod)
        n_pct = wide.take(SH, TOK)
        n_qt = wide.take(KC, TOK)
        hm = Area(HM[:, :, :].rearrange("p t d -> p (t d)"))
        n_kt = hm.take(2, 2, SG, TOK)
        area = Area(work)
        n_v = area.take(TT, VW)
        n_ft = area.take(2, CC, SG * NB)
        n_hid = area.take(2, HID)
        n_hidt = area.take(2, 2, SG * NB)
        n_kc = area.take(SG * NB)
        n_vc = area.take(SG, SD)
        n_e = area.take(TT, SH, NB)
        n_open = area.take(TT, NB)
        n_shut = area.take(TT, NB)
        n_w2 = area.take(2, 2, SD)
        n_pos = area.take(2 * CC)
        n_gb = area.take(3 * SH)
        n_gate = area.take(TT, 3 * SH)
        n_max = area.take(TT, SH)
        n_sum = area.take(TT, SH)
        assert area.at <= 5120
        n_cleared = sem("nsa_cleared")
        n_first, n_second, n_ftr, n_hps, n_hcp, n_htps, n_htcp = (sem(n) for n in (
            "nsa_projected", "nsa_copied", "blocks_ready", "hidden_ps", "hidden_copied", "hidden_t_ps", "hidden_t_copied"))
        n_cps, n_ccp, n_sps, n_xin, n_xout, n_pr, n_tps, n_tcp, n_opened, n_gin, n_gout, n_vr = (sem(n) for n in (
            "compressed_ps", "compressed_copied", "block_scores_ps", "block_exp_in", "block_exp_out", "block_weights_ready",
            "block_weights_ps", "block_weights_copied", "masks_ready", "gates_in", "gates_out", "token_values_ready"))

        N_EARLY = 3

        def nsa_spec(extra=None):
            def scores(i, banks):
                pair, br = i // 2, i % 2
                for t in range(TT):
                    w = (t + 1) * P
                    yield banks[:, t, 0:2 * w], n_qt[:, pair, t * P:(t + 1) * P], n_kt[:, :, br, 2 * pair // (SH // SG), 0:w]

            def values(i, weights):
                pair, br = i // 2, i % 2
                g = 2 * pair // (SH // SG)
                dst = [acc[u * SD:(u + 1) * SD, 0, 0:TOK] for u in range(2)]
                if br == 0:
                    for u in range(2):
                        yield dst[u], n_vc[:, g, :], n_pct[:, 2 * pair + u, :], True, False
                for t in range(TT):
                    for u in range(2):
                        w = TOK - t * P
                        yield (dst[u][:, t * P:TOK], n_v[:, t, br * 2 * P + g * SD:br * 2 * P + (g + 1) * SD],
                               weights[:, t * 512 + u * w:t * 512 + (u + 1) * w], False, br == 1 and t == 1)
            return dict(CAUSAL, scores=scores, values=values, masked=True, per_pair=2, extra=extra, out=XT,
                        pt=work[:, 9200:11248].rearrange("p (a c) -> p a c", a=2),
                        gate=lambda i: n_gate[:, :, (i % 2 + 1) * SH + i // 2 * 2:(i % 2 + 1) * SH + i // 2 * 2 + 2])

        def nsa_sync(sp, ph):
            stream_sync(sp, a["c_w_in"][0], ph.slot0, 4, 2, C_IN)
            for i, w in enumerate((a["c_w_ck1"][0], a["c_w_cv1"][0])):
                stream_sync(sp, w, ph.slot0 + 4 + i, 1, CC, HID)
            w_mod_sync(sp, ph, 0)
            stream_sync(sp, a["c_w_o"][0], ph.slot_mod + MODC, 2, 4, D)

        def nsa_pool(pool, ph):
            pool.wait_ge(phase_done, ph.i)
            for dst, src in ((n_w2[:, 0, :, :], a["c_w_ck2"][0].rearrange("(c p) n -> p c n", p=P)),
                             (n_w2[:, 1, :, :], a["c_w_cv2"][0].rearrange("(c p) n -> p c n", p=P)),
                             (n_pos, a["cmp_pos_cols"]), (n_gb, a["c_gate_b"][0].partition_broadcast(P))):
                pool.dma_start(dst, src).then_inc(small, 16)
            for dst, src in ((raw[:, :], a["cond"]), (early[:, :], a["norm_mix_2"][0].partition_broadcast(P)),
                             (rope[:, :].rearrange("p (t e) -> p t e", t=TT), a["rope_axes"].rearrange("(t p) e -> p t e", p=P)),
                             (hgain[:, 0, :], a["attn_q_norm_2"][0].partition_broadcast(P)),
                             (hgain[:, 1, :], a["attn_k_norm_2"][0].partition_broadcast(P))):
                pool.dma_start(dst, src).then_inc(small, 16)
            nc.gpsimd.memset(n_open, 1.0).then_inc(n_opened, 1)
            nc.gpsimd.memset(n_shut, 0.0).then_inc(n_opened, 1)
            pool.wait_ge(n_opened, 2)
            for m, fill in ((n_open, 0.0), (n_shut, NEG)):
                nc.gpsimd.affine_select(out=m, in_=m, compare_op=ALU.is_ge, fill=fill, base=-(CL - 1),
                                        pattern=[[P, TT], [-CS, NB]], channel_multiplier=1).then_inc(n_opened, 1)
            for i, z in enumerate((n_vc, n_kt[SD:P, 0, :, :, :], n_kt[0:SD, 1, :, :, :], n_pct)):
                nc.gpsimd.memset(z, 0.0).then_inc(n_cleared, 1)
                pool.wait_ge(n_cleared, i + 1)
            gain_pool(pool, ph.ln, a["ln1_g"][ph.layer], a["ln1_b"][ph.layer])
            rows_pool(pool, 0, N_EARLY)
            next_router_pool(pool, ph)
            tile_pows(pool, None)

        def nsa_tensor(pe, ph):
            transpose_tensor(pe, X, ph)
            pe.wait_ge(xt_ready, 2 * (ph.xt + 1))

            def w_of(k):
                return ring[:, (ph.slot0 + k // 2) % RING, 0:2 * C_IN].rearrange("p (k c) -> p k c", k=2)[:, k % 2, :]
            for k in range(KC):
                if k % 2 == 0:
                    slot_wait(pe, ph.slot0 + k // 2)
                w = w_of(k)
                end = dict(stop=(k == KC - 1), skip_group_check=True)
                for m in range(KC):
                    nc.tensor.matmul(acc[:, m // 4, (m % 4) * TOK:(m % 4 + 1) * TOK], w[:, m * P:(m + 1) * P], XT[:, k, :],
                                     start=(k == 0 and m % 2 == 0), **end)
                for i in range(2):
                    for g in range(SG):
                        c0 = SQ + (2 + 2 * i) * P + g * SD
                        for u in range(2):
                            nc.tensor.matmul(pa[u * SD:(u + 1) * SD, i, g * TOK:(g + 1) * TOK], w[:, c0:c0 + SD], XT[:, k, :],
                                             start=(k == 0 and g == 0), **end)
                for i in range(2):
                    for g in range(SG):
                        c0 = SQ + i * P + g * SD
                        for u in range(2):
                            last = nc.tensor.matmul(pb[u * SD:(u + 1) * SD, i, g * TOK:(g + 1) * TOK - u], w[:, c0:c0 + SD], XT[:, k, u:TOK],
                                                    start=(k == 0 and g == 0), **end)
            last.then_inc(n_first, 1)
            pe.wait_ge(n_second, 1)
            for k in range(KC):
                w = w_of(k)
                for t in range(TT):
                    last = nc.tensor.matmul(pa[:, t, 0:VW], XT[:, k, t * P:(t + 1) * P], w[:, C_IN - VW:C_IN], start=(k == 0), stop=(k == KC - 1))
                if k % 2:
                    last.then_inc(freed, 1)
            pe.wait_ge(n_ftr, 1)
            for i in range(2):
                slot_wait(pe, ph.slot0 + 4 + i)
                w = ring[:, (ph.slot0 + 4 + i) % RING, :].rearrange("p (c n) -> p c n", c=CC)
                for c in range(CC):
                    last = nc.tensor.matmul(pb[0:SG * NB, i, 0:HID], n_ft[:, i, c, :], w[:, c, :], start=(c == 0), stop=(c == CC - 1))
                last.then_inc(freed, 1)
            pe.wait_ge(n_hcp, 1)
            for i in range(2):
                for c in range(2):
                    last = nc.tensor.transpose(pb[:, 0, (2 * i + c) * 32:(2 * i + c) * 32 + SG * NB], n_hid[0:SG * NB, i, c * P:(c + 1) * P],
                                               ident[0:SG * NB, 0:SG * NB])
            last.then_inc(n_htps, 1)
            pe.wait_ge(n_htcp, 1)
            pe.wait_ge(small, ph.small)
            for u in range(2):
                for c in range(2):
                    nc.tensor.matmul(pb[u * SD:(u + 1) * SD, 1, 0:SG * NB], n_w2[:, 0, c, :], n_hidt[:, 0, c, :], start=(c == 0), stop=(c == 1))
            for g in range(SG):
                for c in range(2):
                    last = nc.tensor.matmul(pb[0:NB, 1, (g + 1) * SD:(g + 2) * SD], n_hidt[:, 1, c, g * NB:(g + 1) * NB], n_w2[:, 1, c, :],
                                            start=(c == 0), stop=(c == 1))
            last.then_inc(n_cps, 1)
            pe.wait_ge(n_ccp, 2)
            pe.wait_ge(n_vr, 1)
            for t in range(TT):
                for h in range(SH):
                    r = slice(64 * (h % 2), 64 * (h % 2) + 64)
                    g = h // (SH // SG)
                    last = nc.tensor.matmul(pa[:, h % 2, (t * SH + h) // 2 * NB:((t * SH + h) // 2 + 1) * NB], n_qt[r, h // 2, t * P:(t + 1) * P],
                                            n_kc[r, g * NB:(g + 1) * NB], start=True, stop=True)
            last.then_inc(n_sps, 1)
            for n in range(N_EARLY):
                block_tensor(pe, ph, 0, n, N_EARLY)
            pe.wait_ge(part_copied, N_EARLY)
            pe.wait_ge(n_pr, 1)
            for t in range(TT):
                if t:
                    pe.wait_ge(n_tcp, 2)
                for h in range(SH):
                    last = nc.tensor.transpose(acc[0:NB, h // 8, (h % 8) * P:(h % 8 + 1) * P], n_e[:, t, h, :], ident[:, :])
                last.then_inc(n_tps, 1)
            pe.wait_ge(n_tcp, 4)
            pe.wait_ge(n_cleared, 4)
            att_tensor(pe, ph, nsa_spec(between(block_tensor, ph, 0, N_EARLY)))
            out_tensor(pe, ph, ph.slot_mod + MODC)

        def nsa_scalar(act, ph):
            transpose_scalar(act, ph.xt, XT)
            act.wait_ge(n_first, 1)
            for i in range(TT):
                last = nc.scalar.mul(n_qt[:, 4 * i:4 * i + 4, :], acc[:, i, :].rearrange("p (k c) -> p k c", c=TOK), SD ** -0.5)
            last.then_inc(n_ccp, 1)
            act.wait_ge(small, ph.small)
            cond_scalar(act, ph, 0)
            act.wait_ge(n_gin, 1)
            nc.scalar.activation(n_gate, n_gate, ACT.Sigmoid).then_inc(n_gout, 1)
            act.wait_ge(freed, ph.slot0 + 6)
            nc.scalar.activation(n_hid[0:SG * NB, :, :], pb[0:SG * NB, :, 0:HID], ACT.Gelu_apprx_tanh).then_inc(n_hcp, 1)
            act.wait_ge(n_xin, 1)
            nc.scalar.activation(n_e, n_e, ACT.Exp).then_inc(n_xout, 1)
            for n in range(N_EARLY):
                block_scalar(act, ph, 0, n, N_EARLY)
            for n in (N_EARLY - 2, N_EARLY - 1):
                act.wait_ge(rows_moved[n % 2], rows_count(0, n))
            act.wait_ge(n_cleared, 4)
            for t in range(TT):
                act.wait_ge(n_tps, t + 1)
                nc.scalar.copy(n_pct[0:NB, 0:8, t * P:(t + 1) * P], acc[0:NB, 0, :].rearrange("p (h c) -> p h c", c=P)).then_inc(n_tcp, 1)
            att_scalar(act, ph, nsa_spec(between(block_scalar, ph, 0, N_EARLY)))

        def nsa_vector(dve, ph, link):
            v = nc.vector
            transpose_vector(dve, ph.xt, XT)
            cond_vector(dve, 0)
            dve.wait_ge(n_first, 1)
            for u in range(2):
                r = slice(u * SD, (u + 1) * SD)
                last = v.tensor_copy(n_kt[r, u, :, :, :], pa[r, :, :].rearrange("p i (g c) -> p i g c", g=SG))
            last.then_inc(n_second, 1)
            dve.wait_ge(small, ph.small)
            for i in range(2):
                for g in range(SG):
                    seen = pb[:, i, g * TOK:(g + 1) * TOK]
                    src = bass.AP(seen.tensor, seen.offset, [list(seen.ap[0]), [2, CC], [CS, NB]])
                    last = v.tensor_tensor(n_ft[:, i, :, g * NB:(g + 1) * NB], src, bc(n_pos[:, i * CC:(i + 1) * CC].unsqueeze(2), [P, CC, NB]), ALU.add)
            last.then_inc(n_ftr, 1)
            dve.wait_ge(freed, ph.slot0 + 4)
            for t in range(TT):
                last = v.tensor_copy(n_v[:, t, :], pa[:, t, 0:VW])
            last.then_inc(n_vr, 1)
            dve.wait_ge(n_vr, 1)
            v.tensor_tensor(n_gate, n_v[:, :, 3 * P:VW], bc(n_gb.unsqueeze(1), [P, TT, 3 * SH]), ALU.add).then_inc(n_gin, 1)
            dve.wait_ge(n_htps, 1)
            v.tensor_copy(n_hidt, pb[:, 0, 0:128].rearrange("p (i c n) -> p i c n", i=2, c=2)[:, :, :, 0:SG * NB]).then_inc(n_htcp, 1)
            dve.wait_ge(n_cps, 1)
            dve.wait_ge(n_cleared, 4)
            v.tensor_copy(n_vc[0:NB, :, :], pb[0:NB, 1, SD:3 * SD].rearrange("p (g e) -> p g e", g=SG))
            v.tensor_copy(n_kc, pb[:, 1, 0:SG * NB]).then_inc(n_ccp, 1)
            dve.wait_ge(n_sps, 1)
            dve.wait_ge(n_opened, 4)
            for t in range(TT):
                for u in range(2):
                    half_n = SH // 2 * NB
                    last = v.scalar_tensor_tensor(n_e[:, t, u::2, :], pa[:, u, t * half_n:(t + 1) * half_n].rearrange("p (h n) -> p h n", n=NB),
                                                  1.0, bc(n_shut[:, t, :].unsqueeze(1), [P, SH // 2, NB]), ALU.mult, ALU.add)
            link(last)
            link(v.tensor_reduce(n_max, n_e, AX.X, ALU.max))
            v.tensor_tensor(n_e, n_e, bc(n_max.unsqueeze(3), [P, TT, SH, NB]), ALU.subtract).then_inc(n_xin, 1)
            dve.wait_ge(n_xout, 1)
            link(v.tensor_reduce(n_sum, n_e, AX.X, ALU.add))
            dve.wait_ge(n_gout, 1)
            link(v.reciprocal(n_sum, n_sum))
            link(v.tensor_tensor(n_sum, n_gate[:, :, 0:SH], n_sum, ALU.mult))
            link(v.tensor_tensor(n_e, n_e, bc(n_sum.unsqueeze(3), [P, TT, SH, NB]), ALU.mult))
            link(v.tensor_tensor(n_e, n_e, bc(n_open.unsqueeze(2), [P, TT, SH, NB]), ALU.mult))
            dve.sem_inc(n_pr, 1)
            for t in range(TT):
                dve.wait_ge(n_tps, t + 1)
                v.tensor_copy(n_pct[0:NB, 8:SH, t * P:(t + 1) * P], acc[0:NB, 1, :].rearrange("p (h c) -> p h c", c=P)).then_inc(n_tcp, 1)
            att_vector(dve, ph, nsa_spec())
            ln_vector(dve, ph, link, mixed=True)

        block = ctx.enter_context(nc.Block())
        last_ph = plan[-1]
        final = last_ph.kind not in ("ab", "nsa") and last_ph.fn != FN1

        @block.sync
        def _(sp):
            if plan[0].kind == "moe":
                for s in full:
                    sp.sem_inc(s, FILL)
            sp.dma_start(X[:, :, :], a["x"].rearrange("(t p) d -> p t d", p=P)).then_inc(x_loaded, 16)
            sp.dma_start(select[:, :], a["mod_select"]).then_inc(select_loaded, 16)
            for ph in plan:
                if ph.kind != "mod":
                    dict(ab=ab_sync, nsa=nsa_sync, gqa=gqa_sync, fourier=fourier_sync, moe=moe_sync)[ph.kind](sp, ph)
            for t in range(TT):
                if final:
                    sp.wait_ge(result_ready, t + 1)
                else:
                    sp.wait_ge(phase_done, len(plan))
                sp.dma_start(out[t * P:(t + 1) * P, :], X[:, t, :]).then_inc(out_done, 16)
            sp.wait_ge(out_done, 16 * TT)

        @block.gpsimd
        def _(pool):
            tables_pool(pool, Link(pool, poo))
            for ph in plan:
                if ph.kind == "moe":
                    if ph.i == 0:
                        router_pool(pool, ph)
                    if ph.fn == FN1:
                        gain_pool(pool, ph.ln, a["ln2_g"][ph.layer], a["ln2_b"][ph.layer])
                    else:
                        gain_pool(pool, ph.ln, a["norm_ffn_2"][ph.layer])
                    if ph.i + 1 < len(plan) and plan[ph.i + 1].kind == "mod":
                        ahead_pool(pool, ph)
                    before_gqa = ph.fn == FN1 and ph.i + 1 < len(plan) and plan[ph.i + 1].kind == "mod"
                    tile_pows(pool, None if ph.fn == FN1 else RMS_EPS, context_pow if before_gqa else None)
                elif ph.kind != "mod":
                    dict(ab=ab_pool, nsa=nsa_pool, gqa=gqa_pool, fourier=fourier_pool)[ph.kind](pool, ph)
            if final:
                gain_pool(pool, last_ph.ln + 1, a["final_norm_2"])
                tile_pows(pool, RMS_EPS)

        @block.tensor
        def _(pe):
            if plan[0].kind == "moe":
                pe.sem_inc(freed, RING)
            pe.sem_inc(xfreed, CREDIT)
            for r in R:
                for s in r.values():
                    pe.sem_inc(s, START)
            for ph in plan:
                if ph.kind == "moe":
                    transpose_tensor(pe, source(ph), ph)
                    moe_tensor(pe, ph)
                else:
                    dict(ab=ab_tensor, nsa=nsa_tensor, mod=mod_tensor, gqa=gqa_tensor, fourier=fourier_tensor)[ph.kind](pe, ph)

        @block.scalar
        def _(act):
            for ph in plan:
                if ph.kind == "moe":
                    if ph.fn == FN2:
                        squares_scalar(act, ph.x0 - TT)
                    transpose_scalar(act, ph.xt, XT)
                    router_scalar(act, ph)
                    moe_other(act, ph, lambda r, t, g, up, every: round_scalar(act, ph, r, t, up, every))
                else:
                    dict(ab=ab_scalar, nsa=nsa_scalar, mod=mod_scalar, gqa=gqa_scalar, fourier=fourier_scalar)[ph.kind](act, ph)
            if final:
                squares_scalar(act, last_ph.x0)

        @block.vector
        def _(dve):
            link = Link(dve, vec)
            dve.wait_ge(x_loaded, 16)
            dve.wait_ge(consts, CONSTS)
            dve.wait_ge(select_loaded, 16)
            for ph in plan:
                if ph.kind == "moe":
                    transpose_vector(dve, ph.xt, XT)
                    router_vector(dve, ph, link)
                    moe_other(dve, ph, lambda r, t, g, up, every: round_vector(dve, ph, r, t, g, every), last=True)
                    if ph.i + 1 < len(plan) and plan[ph.i + 1].kind == "mod":
                        dve.sem_inc(work_free, 1)
                    if ph.fn == FN1:
                        ln_vector(dve, ph, link)
                    else:
                        for t in range(TT):
                            gated_vector(dve, link, 5, t, ph.x0 + t + 1)
                elif ph.kind != "mod":
                    dict(ab=ab_vector, nsa=nsa_vector, gqa=gqa_vector, fourier=fourier_vector)[ph.kind](dve, ph, link)
                dve.sem_inc(phase_done, 1)
                if ph.i + 1 < len(plan) and ph.fn == FN1 and plan[ph.i + 1].kind == "mod":
                    dve.sem_inc(x_ready, TT)
            if final:
                dve.wait_ge(ln_loaded, 32 * (last_ph.ln + 2))
                for t in range(TT):
                    rstd_wait(dve)
                    nc.vector.scalar_tensor_tensor(X[:, t, :], X[:, t, :], stat[:, 32 + t:33 + t], gain[:, :], ALU.mult, ALU.mult).then_inc(result_ready, 1)


def make_plan(kinds):
    plan = []
    slot = RING if kinds[0][0] == "moe" else 0
    moe = xt = h = ln = small = att = out_ = masked = rows = mix = x = 0
    for i, (kind, layer, fn) in enumerate(kinds):
        ph = Phase(kind, layer, fn)
        ph.i = i
        block1 = kind in ("ab", "nsa") or fn == FN1
        if not block1 and kind != "mod":
            h += 1
        ph.slot0, ph.moe, ph.xt, ph.h, ph.ln, ph.att0, ph.out0, ph.masked0 = slot, moe, xt, h, ln, att, out_, masked
        ph.natt = {"ab": 4, "nsa": 16, "gqa": 16}.get(kind, 0)
        ph.slot_mod = slot + {"nsa": 6, "gqa": 4}.get(kind, 0)
        ph.rows0 = rows
        rows += {0: 16, 1: 12}[layer] if kind == "mod" else 0
        ph.nout = {"ab": 5, "nsa": 8, "gqa": 8, "fourier": 2}.get(kind, 0)
        small += 16 * {"ab": 0, "nsa": 9, "moe": 0, "gqa": 0, "fourier": 0, "mod": 0}[kind]
        ph.small = small
        slot += ph.slots()
        moe += kind == "moe"
        xt += {"mod": 0, "fourier": 0, "gqa": 2}.get(kind, 1)
        att += ph.natt
        out_ += ph.nout
        masked += ph.natt if kind in ("ab", "nsa") else 0
        ln += kind not in ("mod", "gqa")
        ph.lnh = h
        h += block1
        ph.mix = mix
        mix += kind in ("ab", "nsa", "gqa", "fourier")
        if block1:
            x = TT
        ph.x0 = x
        x += 0 if block1 or kind == "mod" else TT
        plan.append(ph)
    return plan


def axis_tables():
    n = 16
    inv = np.float32(10000.0) ** (-np.arange(n, dtype=np.float32) / np.float32(n))
    tok = np.arange(TOK)
    ang = np.stack([(tok // 64).astype(np.float32)[:, None] * inv, (tok % 64).astype(np.float32)[:, None] * inv], 1)
    return np.stack([np.cos(ang), np.sin(ang)], 1).reshape(TOK, 4 * n).astype(np.float32)


def dft_tables():
    i = np.arange(TOK)
    ang = 2 * np.pi * (np.outer(i, i) % TOK) / TOK
    return np.concatenate([np.cos(ang) / 16, np.sin(ang) / 16], 1).astype(np.float32)


def mod_selectors():
    p = np.arange(P)[:, None]
    n = np.arange(16)[None]
    return (((p // 4 == n) & (p < 64)) | (p == 64 + n % 12) ).astype(np.float32)


def by_feature(c, c_ctx):
    return np.ascontiguousarray(np.stack([c.reshape(KC, P), c_ctx.reshape(KC, P)]).transpose(2, 0, 1).reshape(P, 2 * KC))


def latent_freqs():
    return np.exp(np.float32(-np.log(10000.0)) * np.arange(16, dtype=np.float32) / np.float32(16)).astype(np.float32)[None]


def position_columns(cmp_pos):
    return np.ascontiguousarray(cmp_pos.reshape(2, 16, P).transpose(2, 0, 1).reshape(P, 32))


KINDS = [("ab", 0, 0), ("moe", 0, FN1), ("nsa", 1, 0), ("moe", 1, FN1),
         ("mod", 0, 0), ("gqa", 0, 0), ("moe", 0, FN2), ("mod", 1, 0), ("fourier", 1, 0), ("moe", 1, FN2)]
AS_THEY_ARE = """ab_w_in ab_gm_ln_g ab_gm_ln_b ab_gm_ws ab_gm_bs ab_mla_q_norm ab_mla_kv_norm ab_mla_w_uq ab_mla_w_uk
ab_mla_w_uv ab_w_o c_w_in c_w_ck1 c_w_ck2 c_w_cv1 c_w_cv2 c_gate_b c_w_o moe_w_rg moe_b_rg moe_w_re moe_b_re
moe_w_gate moe_w_up moe_w_down ln1_g ln1_b ln2_g ln2_b ctx_2 w_mod_2 b_mod_2 norm_mix_2 norm_ffn_2 attn_w_qkv_2
attn_q_norm_2 attn_k_norm_2 attn_w_o_2 fourier_w_o_2 moe_w_rg_2 moe_b_rg_2 moe_w_re_2 moe_b_re_2 moe_w1_2 moe_w3_2
moe_w2_2 final_norm_2""".split()


def kernel(**inputs):
    import concourse.bacc as bacc
    from concourse.bass_utils import run_bass_kernel_spmd

    nc = bacc.Bacc("TRN2", target_bir_lowering=False, num_devices=1)
    given = {n: np.ascontiguousarray(inputs[n]) for n in AS_THEY_ARE}
    given["x"] = np.ascontiguousarray(inputs["x"]).reshape(TOK, D)
    given["pos_cols"] = np.ascontiguousarray(np.asarray(inputs["positions"]).reshape(TT, P).T)
    given["cond"] = by_feature(np.asarray(inputs["c_2"]), np.asarray(inputs["c_ctx_2"]))
    given["cmp_pos_cols"] = position_columns(np.asarray(inputs["c_cmp_pos"]))
    given["mod_select"] = mod_selectors()
    given["freqs"] = latent_freqs()
    given["rope_axes"] = axis_tables()
    given["dft"] = dft_tables()
    a = {n: nc.dram_tensor(f"in_{n}", v.shape, mybir.dt.from_np(v.dtype), kind="ExternalInput").ap() for n, v in given.items()}
    out = nc.dram_tensor("out", (TOK, D), F32, kind="ExternalOutput").ap()
    build_model(nc, a, out, make_plan(KINDS))
    r = run_bass_kernel_spmd(nc, [{f"in_{n}": v for n, v in given.items()}], core_ids=[0])
    return r.results[0]["out"].reshape(1, TOK, D)
```
